# Optimizing a Trainium2 kernel written in Bass

```python
import math
import jax, jax.numpy as jnp
from jax import lax
import numpy as np

D_MODEL = 1024
BATCH = 1
SEQ = 512
DEPTH = 2
DEC_BATCH = 1
DEC_SEQ = 64
PAST_LEN = 128

CHUNK = 64
N_PAR_LAYERS = (DEPTH + 1) // 2
N_GM_LAYERS = DEPTH // 2

POOL_WINDOWS = (2, 4, 8, 16)
POOL_GROUPS = 4
POOL_GROUP_DIM = D_MODEL // 8
POOL_WIDTH = POOL_GROUPS * POOL_GROUP_DIM
POOL_STATE = max(POOL_WINDOWS) - 1

N_HEADS = 8
HEAD_DIM = D_MODEL // 16
N_KV_HEADS = 4
Q_PER_KV = N_HEADS // N_KV_HEADS
ATT_WIDTH = N_HEADS * HEAD_DIM
N_IDX_HEADS = 8
IDX_DIM = 64
TOPK_MAX = 256
Q_BLOCK = 128
ROPE_THETA = 500000.0
MIX_WIDTH = POOL_WIDTH + ATT_WIDTH

GM_CHUNK = 128
GM_HALF = D_MODEL
GM_GROUPS = 8
GM_GROUP_DIM = GM_HALF // GM_GROUPS

N_EXPERT_GROUPS = 4
EXPERTS_PER_GROUP = 8
N_EXPERTS = N_EXPERT_GROUPS * EXPERTS_PER_GROUP
TOPK_IN_GROUP = 2
D_EXPERT = D_MODEL // 4
MOE_BLOCK = 128

RMS_EPS = 1e-6
LN_EPS = 1e-5

kernel_name = "hybrid_pool_dsa_gmlp_hmoe_stream_step"

def rmsnorm(x, g):
    xf = x.astype(jnp.float32)
    y = xf * lax.rsqrt(jnp.mean(xf * xf, axis=-1, keepdims=True) + RMS_EPS)
    return (y * g.astype(jnp.float32)).astype(x.dtype)

def layernorm(x, g, b):
    xf = x.astype(jnp.float32)
    mu = jnp.mean(xf, axis=-1, keepdims=True)
    var = jnp.mean(jnp.square(xf - mu), axis=-1, keepdims=True)
    y = (xf - mu) * lax.rsqrt(var + LN_EPS)
    return (y * g.astype(jnp.float32) + b.astype(jnp.float32)).astype(x.dtype)

def partial_rope(x, pos):
    rd = x.shape[-1] // 4
    half = rd // 2
    inv = 1.0 / (ROPE_THETA ** (jnp.arange(half, dtype=jnp.float32) / half))
    ang = pos.astype(jnp.float32)[:, None] * inv[None, :]
    cos = jnp.cos(ang)[None, :, None, :]
    sin = jnp.sin(ang)[None, :, None, :]
    xr = x[..., :rd].astype(jnp.float32)
    x1, x2 = xr[..., :half], xr[..., half:]
    rot = jnp.concatenate([x1 * cos - x2 * sin, x2 * cos + x1 * sin], axis=-1).astype(x.dtype)
    return jnp.concatenate([rot, x[..., rd:]], axis=-1)

def pool_mixer(xp, hist, pos, w_grp, scale):
    B, T, _ = xp.shape
    full = jnp.concatenate([hist, xp], axis=1)
    cs = jnp.cumsum(full.astype(jnp.float32), axis=1)
    cs = jnp.concatenate([jnp.zeros((B, 1, POOL_WIDTH), jnp.float32), cs], axis=1)
    means = []
    for gi, w in enumerate(POOL_WINDOWS):
        sl = slice(gi * POOL_GROUP_DIM, (gi + 1) * POOL_GROUP_DIM)
        s = cs[:, POOL_STATE + 1:POOL_STATE + 1 + T, sl] - cs[:, POOL_STATE + 1 - w:POOL_STATE + 1 - w + T, sl]
        cnt = jnp.minimum(pos + 1, w).astype(jnp.float32)[None, :, None]
        means.append(s / cnt)
    mean = jnp.concatenate(means, axis=-1)
    d = (mean - xp.astype(jnp.float32)).astype(xp.dtype).reshape(B, T, POOL_GROUPS, POOL_GROUP_DIM)
    y = jnp.einsum('btgc,gcd->btgd', d, w_grp).reshape(B, T, POOL_WIDTH) * scale
    return y, full[:, -POOL_STATE:]

def dsa_block(q, qi, wi, q_pos, k_all, v_all, ki_all):
    B, Tq = q.shape[:2]
    L = k_all.shape[1]
    n_sel = min(TOPK_MAX, L // 4)
    limit = (q_pos // CHUNK + 1) * CHUNK
    admissible = jnp.arange(L)[None, :] < limit[:, None]
    sc = jnp.einsum('bthd,bsd->bths', qi, ki_all, preferred_element_type=jnp.float32)
    index = jnp.einsum('bths,bth->bts', jax.nn.relu(sc), wi.astype(jnp.float32))
    index = jnp.where(admissible[None], index, -jnp.inf)
    _, top_idx = lax.top_k(index, n_sel)
    sel_ok = top_idx < limit[None, :, None]
    k_sel = jax.vmap(lambda kb, ib: kb[ib])(k_all, top_idx)
    v_sel = jax.vmap(lambda vb, ib: vb[ib])(v_all, top_idx)
    qg = q.reshape(B, Tq, N_KV_HEADS, Q_PER_KV, HEAD_DIM)
    s = jnp.einsum('btkgd,btjkd->btkgj', qg, k_sel, preferred_element_type=jnp.float32) * (HEAD_DIM ** -0.5)
    s = jnp.where(sel_ok[:, :, None, None, :], s, -1e30)
    p = jax.nn.softmax(s, axis=-1)
    o = jnp.einsum('btkgj,btjkd->btkgd', p, v_sel.astype(jnp.float32))
    return o.reshape(B, Tq, ATT_WIDTH).astype(q.dtype)

def dsa_mixer(q, qi, wi, pos, k_all, v_all, ki_all):
    B, T = q.shape[:2]
    if T % Q_BLOCK != 0:
        return dsa_block(q, qi, wi, pos, k_all, v_all, ki_all)
    nb = T // Q_BLOCK

    def to_blocks(a):
        return jnp.swapaxes(a.reshape((B, nb, Q_BLOCK) + a.shape[2:]), 0, 1)

    def one_block(args):
        qb, qib, wib, pb = args
        return dsa_block(qb, qib, wib, pb, k_all, v_all, ki_all)

    o = lax.map(one_block, (to_blocks(q), to_blocks(qi), to_blocks(wi), pos.reshape(nb, Q_BLOCK)))
    return jnp.swapaxes(o, 0, 1).reshape(B, T, ATT_WIDTH)

def parallel_mixer(h, pos, pool_hist, past_k, past_v, past_ki, w_in, pool_w, pool_scale, w_out):
    B, T, _ = h.shape
    proj = jnp.einsum('btd,de->bte', h, w_in)
    sizes = (POOL_WIDTH, N_HEADS * HEAD_DIM, N_KV_HEADS * HEAD_DIM, N_KV_HEADS * HEAD_DIM,
             N_IDX_HEADS * IDX_DIM, IDX_DIM, N_IDX_HEADS)
    cuts = [sum(sizes[:i + 1]) for i in range(len(sizes) - 1)]
    xp, q, k, v, qi, ki, wi = jnp.split(proj, cuts, axis=-1)
    q = partial_rope(q.reshape(B, T, N_HEADS, HEAD_DIM), pos)
    k = partial_rope(k.reshape(B, T, N_KV_HEADS, HEAD_DIM), pos)
    v = v.reshape(B, T, N_KV_HEADS, HEAD_DIM)
    qi = partial_rope(qi.reshape(B, T, N_IDX_HEADS, IDX_DIM), pos)
    ki = partial_rope(ki[:, :, None, :], pos)[:, :, 0, :]
    y_pool, new_hist = pool_mixer(xp, pool_hist, pos, pool_w, pool_scale)
    if past_k is None:
        k_all, v_all, ki_all = k, v, ki
    else:
        k_all = jnp.concatenate([past_k, k], axis=1)
        v_all = jnp.concatenate([past_v, v], axis=1)
        ki_all = jnp.concatenate([past_ki, ki], axis=1)
    y_att = dsa_mixer(q, qi, wi, pos, k_all, v_all, ki_all)
    y = jnp.einsum('btc,cd->btd', jnp.concatenate([y_pool, y_att], axis=-1), w_out)
    return y, k, v, ki, new_hist

def gmlp_mixer(h, w_in, ln_g, ln_b, ws, bs, w_out):
    B, T, _ = h.shape
    z = jax.nn.gelu(jnp.einsum('btd,de->bte', h, w_in))
    u, v = z[..., :GM_HALF], z[..., GM_HALF:]
    v = layernorm(v, ln_g, ln_b)
    if T % GM_CHUNK == 0:
        n, c = T // GM_CHUNK, GM_CHUNK
    else:
        n, c = 1, T
    mask = jnp.tril(jnp.ones((c, c), dtype=bool))
    wsm = jnp.where(mask[None], ws[:, :c, :c], jnp.zeros((), ws.dtype))
    vg = v.reshape(B, n, c, GM_GROUPS, GM_GROUP_DIM)
    mixed = jnp.einsum('gts,bnsgd->bntgd', wsm, vg) + jnp.transpose(bs[:, :c])[None, None, :, :, None]
    gated = u * mixed.reshape(B, T, GM_HALF)
    return jnp.einsum('btc,cd->btd', gated, w_out), v

def routed_experts(xt, expert_id, gates, w_gate, w_up, w_down):
    N, D = xt.shape
    A = N * TOPK_IN_GROUP
    flat_e = expert_id.reshape(-1).astype(jnp.int32)
    flat_tok = jnp.arange(A, dtype=jnp.int32) // TOPK_IN_GROUP
    order = jnp.argsort(flat_e)
    e_sorted = flat_e[order]
    tok_sorted = flat_tok[order]
    gate_sorted = gates.reshape(-1)[order]
    counts = jnp.bincount(flat_e, length=N_EXPERTS)
    padded = (counts + MOE_BLOCK - 1) // MOE_BLOCK * MOE_BLOCK
    pad_end = jnp.cumsum(padded)
    pad_start = pad_end - padded
    start = jnp.cumsum(counts) - counts
    dest = pad_start[e_sorted] + jnp.arange(A, dtype=jnp.int32) - start[e_sorted]
    n_blocks = -(-A // MOE_BLOCK) + N_EXPERTS
    n_rows = n_blocks * MOE_BLOCK
    row_tok = jnp.full((n_rows,), N, dtype=jnp.int32).at[dest].set(tok_sorted)
    x_rows = jnp.concatenate([xt, jnp.zeros((1, D), xt.dtype)], axis=0)[row_tok]
    block_start = jnp.arange(n_blocks, dtype=jnp.int32) * MOE_BLOCK
    block_e = jnp.minimum(jnp.searchsorted(pad_end, block_start, side='right'), N_EXPERTS - 1)

    def expert_block(args):
        xb, e = args
        return (jax.nn.silu(xb @ w_gate[e]) * (xb @ w_up[e])) @ w_down[e]

    y_rows = lax.map(expert_block, (x_rows.reshape(n_blocks, MOE_BLOCK, D), block_e)).reshape(n_rows, D)
    y_assign = y_rows[dest] * gate_sorted[:, None].astype(y_rows.dtype)
    return jnp.zeros_like(xt).at[tok_sorted].add(y_assign)

def hier_moe(h, w_rg, w_re, w_gate, w_up, w_down):
    B, T, D = h.shape
    xt = h.reshape(B * T, D)
    N = xt.shape[0]
    lg = jnp.einsum('nd,dg->ng', xt, w_rg, preferred_element_type=jnp.float32)
    g_sel = jnp.argmax(lg, axis=-1)
    p_grp = jnp.take_along_axis(jax.nn.softmax(lg, axis=-1), g_sel[:, None], axis=-1)[:, 0]
    le = jnp.einsum('nd,de->ne', xt, w_re, preferred_element_type=jnp.float32)
    le = le.reshape(N, N_EXPERT_GROUPS, EXPERTS_PER_GROUP)
    le_g = jnp.take_along_axis(le, g_sel[:, None, None], axis=1)[:, 0]
    top_v, top_j = lax.top_k(le_g, TOPK_IN_GROUP)
    gates = p_grp[:, None] * jax.nn.softmax(top_v, axis=-1)
    expert_id = g_sel[:, None].astype(jnp.int32) * EXPERTS_PER_GROUP + top_j.astype(jnp.int32)
    return routed_experts(xt, expert_id, gates, w_gate, w_up, w_down).reshape(B, T, D)

def setup_inputs(seed: int = 0) -> dict:
    key = jax.random.key(seed)
    ks = jax.random.split(key, 24)
    f32 = jnp.float32
    in_width = (POOL_WIDTH + N_HEADS * HEAD_DIM + 2 * N_KV_HEADS * HEAD_DIM
                + N_IDX_HEADS * IDX_DIM + IDX_DIM + N_IDX_HEADS)

    def nrm(k, shape, scale):
        return jax.random.normal(k, shape, f32) * scale

    return {
        "x_prompt": nrm(ks[0], (BATCH, SEQ, D_MODEL), 1.0),
        "x_sample": nrm(ks[1], (DEC_BATCH, DEC_SEQ, D_MODEL), 1.0),
        "cache_k": nrm(ks[2], (N_PAR_LAYERS, DEC_BATCH, PAST_LEN, N_KV_HEADS, HEAD_DIM), 1.0),
        "cache_v": nrm(ks[3], (N_PAR_LAYERS, DEC_BATCH, PAST_LEN, N_KV_HEADS, HEAD_DIM), 1.0),
        "cache_idx_k": nrm(ks[4], (N_PAR_LAYERS, DEC_BATCH, PAST_LEN, IDX_DIM), 1.0),
        "state_pool": nrm(ks[5], (N_PAR_LAYERS, DEC_BATCH, POOL_STATE, POOL_WIDTH), 1.0),
        "norm_mix": 1.0 + nrm(ks[6], (DEPTH, D_MODEL), 0.05),
        "norm_ffn": 1.0 + nrm(ks[7], (DEPTH, D_MODEL), 0.05),
        "norm_final": 1.0 + nrm(ks[8], (D_MODEL,), 0.05),
        "par_w_in": nrm(ks[9], (N_PAR_LAYERS, D_MODEL, in_width), D_MODEL ** -0.5),
        "par_pool_w": nrm(ks[10], (N_PAR_LAYERS, POOL_GROUPS, POOL_GROUP_DIM, POOL_GROUP_DIM), POOL_GROUP_DIM ** -0.5),
        "par_pool_scale": 1.0 + nrm(ks[11], (N_PAR_LAYERS, POOL_WIDTH), 0.1),
        "par_w_out": nrm(ks[12], (N_PAR_LAYERS, MIX_WIDTH, D_MODEL), MIX_WIDTH ** -0.5),
        "gm_w_in": nrm(ks[13], (N_GM_LAYERS, D_MODEL, 2 * GM_HALF), D_MODEL ** -0.5),
        "gm_ln_g": 1.0 + nrm(ks[14], (N_GM_LAYERS, GM_HALF), 0.05),
        "gm_ln_b": nrm(ks[15], (N_GM_LAYERS, GM_HALF), 0.02),
        "gm_ws": nrm(ks[16], (N_GM_LAYERS, GM_GROUPS, GM_CHUNK, GM_CHUNK), GM_CHUNK ** -0.5),
        "gm_bs": 1.0 + nrm(ks[17], (N_GM_LAYERS, GM_GROUPS, GM_CHUNK), 0.1),
        "gm_w_out": nrm(ks[18], (N_GM_LAYERS, GM_HALF, D_MODEL), GM_HALF ** -0.5),
        "moe_router_group": nrm(ks[19], (DEPTH, D_MODEL, N_EXPERT_GROUPS), D_MODEL ** -0.5),
        "moe_router_expert": nrm(ks[20], (DEPTH, D_MODEL, N_EXPERTS), D_MODEL ** -0.5),
        "moe_w_gate": nrm(ks[21], (DEPTH, N_EXPERTS, D_MODEL, D_EXPERT), D_MODEL ** -0.5),
        "moe_w_up": nrm(ks[22], (DEPTH, N_EXPERTS, D_MODEL, D_EXPERT), D_MODEL ** -0.5),
        "moe_w_down": nrm(ks[23], (DEPTH, N_EXPERTS, D_EXPERT, D_MODEL), D_EXPERT ** -0.5),
    }

def reference(x_prompt, x_sample, cache_k, cache_v, cache_idx_k, state_pool,
              norm_mix, norm_ffn, norm_final,
              par_w_in, par_pool_w, par_pool_scale, par_w_out,
              gm_w_in, gm_ln_g, gm_ln_b, gm_ws, gm_bs, gm_w_out,
              moe_router_group, moe_router_expert, moe_w_gate, moe_w_up, moe_w_down):
    Bp, Tp, _ = x_prompt.shape
    Bs, Ts, _ = x_sample.shape
    past_len = cache_k.shape[2]
    pos_p = jnp.arange(Tp, dtype=jnp.int32)
    pos_s = past_len + jnp.arange(Ts, dtype=jnp.int32)
    xp, xs = x_prompt, x_sample
    kp_l, vp_l, kip_l, poolp_l = [], [], [], []
    ks_l, vs_l, kis_l, pools_l, gmv_l = [], [], [], [], []
    for layer in range(DEPTH):
        j = layer // 2
        hp = rmsnorm(xp, norm_mix[layer])
        hs = rmsnorm(xs, norm_mix[layer])
        if layer % 2 == 0:
            zero_hist = jnp.zeros((Bp, POOL_STATE, POOL_WIDTH), hp.dtype)
            yp, kp, vp, kip, poolp = parallel_mixer(hp, pos_p, zero_hist, None, None, None,
                                                    par_w_in[j], par_pool_w[j], par_pool_scale[j], par_w_out[j])
            ys, ks_, vs_, kis, pools = parallel_mixer(hs, pos_s, state_pool[j], cache_k[j], cache_v[j], cache_idx_k[j],
                                                      par_w_in[j], par_pool_w[j], par_pool_scale[j], par_w_out[j])
            kp_l.append(kp); vp_l.append(vp); kip_l.append(kip); poolp_l.append(poolp)
            ks_l.append(ks_); vs_l.append(vs_); kis_l.append(kis); pools_l.append(pools)
        else:
            yp, _ = gmlp_mixer(hp, gm_w_in[j], gm_ln_g[j], gm_ln_b[j], gm_ws[j], gm_bs[j], gm_w_out[j])
            ys, gv = gmlp_mixer(hs, gm_w_in[j], gm_ln_g[j], gm_ln_b[j], gm_ws[j], gm_bs[j], gm_w_out[j])
            gmv_l.append(gv)
        xp = xp + yp
        xs = xs + ys
        xp = xp + hier_moe(rmsnorm(xp, norm_ffn[layer]), moe_router_group[layer], moe_router_expert[layer],
                           moe_w_gate[layer], moe_w_up[layer], moe_w_down[layer])
        xs = xs + hier_moe(rmsnorm(xs, norm_ffn[layer]), moe_router_group[layer], moe_router_expert[layer],
                           moe_w_gate[layer], moe_w_up[layer], moe_w_down[layer])
    y_prompt = rmsnorm(xp, norm_final)
    y_sample = rmsnorm(xs, norm_final)
    return (y_prompt, y_sample,
            jnp.stack(kp_l), jnp.stack(vp_l), jnp.stack(kip_l), jnp.stack(poolp_l),
            jnp.stack(ks_l), jnp.stack(vs_l), jnp.stack(kis_l), jnp.stack(pools_l),
            jnp.stack(gmv_l))


_drawn_inputs = setup_inputs


def setup_inputs(seed=0):
    import zlib

    import numpy as np

    out = dict(_drawn_inputs(seed))
    spreads = {}
    factors = {'gm_ln_b': 2.868}
    for name, (base, spread) in spreads.items():
        noise = np.random.default_rng([zlib.crc32(name.encode()), seed]).standard_normal(out[name].shape)
        drawn = base * np.exp(spread * noise) if base else spread * noise
        out[name] = __import__('jax').numpy.asarray(drawn.astype(out[name].dtype))
    for name, factor in factors.items():
        out[name] = (out[name] * factor).astype(out[name].dtype)
    return out
```

```python
from contextlib import ExitStack

import numpy as np
import concourse.bass as bass
from concourse import mybir

F32 = mybir.dt.float32
BF16 = mybir.dt.bfloat16
I32 = mybir.dt.int32
U32 = mybir.dt.uint32
ALU = mybir.AluOpType
ACT = mybir.ActivationFunctionType
AX = mybir.AxisListType

P = 128
D = 1024
C = D // P
TP, TS = 512, 64
T = TP + TS
PAST = 128
ROWS = [P] * (TP // P) + [TS]
T0 = [P * j for j in range(len(ROWS))]
NT = len(ROWS)
PW_ = 512
NG = 4
HIST = 15
NH, NKV, HD = 8, 4, 64
NIH = 8
QKV = 1608
QC = QKV // 4
OQ, OK_, OV, OQI, OKI, OWI = 0, 512, 768, 1024, 1536, 1600
NE, EG, NGRP = 32, 8, 4
FE = 256
BLK = 64
PAIRS = NE * BLK // P
MAIN = NE * BLK
NOV = 18
SLOTS = MAIN + NOV * BLK + P
OOB = 1 << 20
TK_P, TK_S = 128, 48
NEG_ADM = -3.0e38
NEG_SEL = -3.4e38
NEG = -1.0e30
LINE = HIST + TP + HIST + TS
XP0, XS0 = HIST, HIST + TP + HIST
HALF = T // 2
SCALE = HD ** -0.5

CON = {}
_at = 0
for _name, _w in [("ident", P), ("cos", NT * 8), ("sin", NT * 8), ("tri", P), ("upper", P), ("ones", P),
                  ("iota", NE), ("egrp", NE), ("base", NE), ("rcnt", NG * 16), ("nov", NOV * NE)]:
    CON[_name] = (_at, _at + _w)
    _at += _w
NCON = _at


def constants():
    con = np.zeros((P, NCON), np.float32)

    def put(name, a):
        lo, hi = CON[name]
        con[:, lo:hi] = a

    put("ident", np.eye(P))
    half = 8
    inv = (np.float32(1.0) / (np.float32(500000.0) ** (np.arange(half, dtype=np.float32) / np.float32(half)))).astype(np.float32)
    pos = np.stack([np.arange(P) + P * j for j in range(4)] + [PAST + np.arange(P)], 1).astype(np.float32)
    ang = (pos[:, :, None] * inv[None, None, :]).astype(np.float32)
    put("cos", np.cos(ang).reshape(P, -1))
    put("sin", np.sin(ang).reshape(P, -1))
    r = np.arange(P)
    put("tri", (r[:, None] <= r[None, :]))
    put("upper", (r[:, None] < r[None, :]))
    put("ones", 1.0)
    e = np.arange(NE)
    put("iota", e)
    put("egrp", e // EG)
    put("base", e * BLK)
    put("rcnt", np.concatenate([1.0 / np.minimum(np.arange(16) + 1, 2 << g) for g in range(NG)]))
    put("nov", np.repeat(np.arange(NOV), NE))
    token = np.full((P, NT, 2, 2), OOB, np.int32)
    for j in range(NT):
        for k in range(2):
            token[:, j, k, 0] = T0[j] + r
            token[:, j, k, 1] = 2 * (T0[j] + r) + k
    return con, np.concatenate([token.reshape(P, -1), np.full((P, 2 * SLOTS // P), OOB, np.int32)], 1)


NTOK = NT * 4


def build(nc, a, out):
    es = ExitStack()
    with es:
        sb = lambda name, shape, dt=F32: es.enter_context(nc.sbuf_tensor(name, shape, dt))
        sem = lambda name: es.enter_context(nc.semaphore(name))
        ps = [es.enter_context(nc.psum_tensor(f"bank{i}", [P, 512], F32)) for i in range(8)]
        dram = lambda name, shape, dt=F32: nc.dram_tensor(name, shape, dt, kind="Internal").ap()

        h_rows = [dram(f"h_rows{l}", [T, D]) for l in range(2)]
        y_rows = [dram(f"y_rows{l}", [2 * T, D]) for l in range(2)]
        slot_tab = [dram(f"slot_tab{l}", [SLOTS, 2], I32) for l in range(2)]

        x = sb("x", [P, NT, D])
        hT = sb("hT", [P, C, T])
        ring = sb("ring", [P, 24576])
        mid = sb("mid", [P, 7168])
        dw = sb("dw", [P, 2, C, 512])
        gain = sb("gain", [P, D])
        con = sb("con", [P, NCON])
        icon = sb("icon", [P, NTOK + 2 * SLOTS // P], I32)
        wr = sb("wr", [P, C, 4 + NE])
        cbf = sb("cbf", [P, 2, P], BF16)
        pscale = sb("pscale", [P, NG])
        gbias = sb("gbias", [P, 8])
        st = sb("st", [P, 64])
        eps = sb("eps", [P, 2])
        cell = sb("cell", [1, 6])
        m8 = sb("m8", [P, 8])
        gates = sb("gates", [P, NT, 2])
        slot_i = sb("slot_i", [P, NT, 2], I32)
        gix = sb("gix", [P, 2, 2], I32)
        six = sb("six", [P, 2, 2], I32)
        ovf = sb("ovf", [P, NOV + 2], I32)

        def c_(name, n=None):
            lo, hi = CON[name]
            v = con[:, lo:hi]
            return v.rearrange("p (a b) -> p a b", a=n) if n else v

        ident, cos, sin = c_("ident"), c_("cos", NT), c_("sin", NT)

        at = [0]

        def cut(mem, n):
            v = mem[:, at[0]:at[0] + n]
            at[0] += n
            return v
        qiT = cut(ring, 4 * T).rearrange("p (a t) -> p a t", a=4)
        kiT = cut(ring, TP)
        kiTs = cut(ring, PAST + TS)
        rl = cut(ring, 1024).rearrange("p (a n) -> p a n", a=2)
        pool_out = rl.rearrange("p a n -> p (a n)").rearrange("p (a n) -> p a n", a=2)
        sm = cut(ring, 1024).rearrange("p (a n) -> p a n", a=2)
        pr = cut(ring, 1024).rearrange("p (a n) -> p a n", a=2)
        pT = cut(ring, 1024).rearrange("p (a n) -> p a n", a=2)
        kdc = pT.rearrange("p a n -> p (a n)")[:, 0:640].rearrange("p (a n) -> p a n", a=5)
        kd = cut(ring, 1024).rearrange("p (b a n) -> p b a n", b=2, a=4)
        at[0] = 8192
        R = cut(ring, NT * QKV).rearrange("p (j n) -> p j n", j=NT)
        qT = cut(ring, 4 * T).rearrange("p (a t) -> p a t", a=4)
        kT = cut(ring, NKV * TP).rearrange("p (a t) -> p a t", a=NKV)
        kTs = cut(ring, NKV * (PAST + TS)).rearrange("p (a t) -> p a t", a=NKV)
        index = cut(ring, NT * TP).rearrange("p (j n) -> p j n", j=NT)
        vc = cut(ring, 256)
        kic = cut(ring, 64)
        kdi = cut(ring, 256).rearrange("p (b n) -> p b n", b=2)
        assert at[0] <= 24576
        wgu = [ring[:, 12288 * b:12288 * b + 8192].rearrange("p (e c n) -> p e c n", e=2, c=C) for b in range(2)]
        wdn = [ring[:, 12288 * b + 8192:12288 * b + 12288].rearrange("p (e c n) -> p e c n", e=2, c=2) for b in range(2)]
        ut = ring[:, 20480:21504].rearrange("p (b n) -> p b n", b=2)
        wsr = ring[:, 20480:21504].rearrange("p (g n) -> p g n", g=8)
        lng, lnb = ring[:, 21504:22528], ring[:, 22528:23552]
        wsm = ring[:, 23552:24576].rearrange("p (g n) -> p g n", g=8)

        hr = mid[:, 0:2048].rearrange("p (b n) -> p b n", b=2)
        junk = mid[:, 6144:7168]
        ckr = mid[:, 2048:2304]
        dT = mid[:, 0:4 * T].rearrange("p (g t) -> p g t", g=NG)
        line = mid[:, 2304:2304 + NG * LINE].rearrange("p (g t) -> p g t", g=NG)
        ta, tb = mid[:, 4728:4728 + LINE], mid[:, 4728 + LINE:4728 + 2 * LINE]
        rt = mid[:, 6144:6528].rearrange("p (a n) -> p a n", a=4)
        pw = mid[:, 6528:7040].rearrange("p (g n) -> p g n", g=NG)
        sp15 = sb("sp15", [HIST, 512])
        xg = hr
        xT = mid[:, 2048:4096].rearrange("p (b c n) -> p b c n", b=2, c=C)
        yb = mid[:, 4096:6144].rearrange("p (b n) -> p b n", b=2)
        sg, hh = mid[:, 6144:6400], mid[:, 6400:6656]
        hhT = mid[:, 6656:7168].rearrange("p (b c n) -> p b c n", b=2, c=2)
        cb = mid[:, 0:4096].rearrange("p (b k n) -> p b k n", b=2, k=2)
        v = mid[:, 2048:7168].rearrange("p (j n) -> p j n", j=NT)
        rq = hT[:, :, :].rearrange("p c t -> p (c t)")
        rat = [0]

        def rcut(n, k=None):
            w = rq[:, rat[0]:rat[0] + n]
            rat[0] += n
            return w.rearrange("p (j n) -> p j n", j=k) if k else w
        ls = rcut(NT * 36, NT)
        lgp = rcut(NT * 8, NT)
        mg = rcut(NT * 8, NT)
        ig = rcut(NT * 8, NT)
        igf = rcut(NT, NT)
        lem = rcut(NT * NE, NT)
        me = rcut(NT * 8, NT)
        ie = rcut(NT * 8, NT)
        ief = rcut(NT * 2, NT)
        oh = [rcut(NT * NE, NT) for _ in range(2)]
        mbf = rcut(NT * NE // 2).bitcast(BF16).rearrange("p (j n) -> p j n", j=NT)
        cnt = rcut(NE)
        cnti = rcut(NE).bitcast(I32)
        nov = rcut(NE)
        inc = rcut(NE)
        dlt = rcut(NE)
        slt = rcut(NT * NE, NT)
        slo = rcut(NT * NE, NT)
        slf = rcut(NT * 2, NT)
        gex = rcut(NT * 4, NT)
        gsm = rcut(NT * 2, NT)
        gdf = rcut(NT * 2, NT)
        ov1 = rcut(NOV * NE, NOV)
        ov2 = rcut(NOV + 2)
        assert rat[0] <= 4096

        s_con, s_small, s_xl = sem("con_loaded"), sem("small_loaded"), [sem(f"x_loaded{j}") for j in range(NT)]
        s_cache, s_gain, s_wr = sem("cache_loaded"), sem("gain_loaded"), sem("router_loaded")
        s_dw, s_dwf = [sem(f"dense_loaded{b}") for b in range(2)], sem("dense_used")
        s_pwl, s_gml = sem("pool_w_loaded"), sem("gmlp_small_loaded")
        s_ssq, s_h, s_tp, s_ht = sem("squares"), sem("rows_normed"), sem("rows_turned"), sem("hT_written")
        s_eps = sem("eps_set")
        s_rs, s_va, s_vr, s_vc = sem("rstd"), sem("v_stats"), sem("v_rstd"), sem("v_centred")
        s_hst = [sem(f"rows_stored{b}") for b in range(2)]
        s_res = sem("residual_added")
        s_pps, s_pev = sem("proj_done"), sem("proj_copied")
        s_dup, s_rope, s_tt, s_te = sem("keys_doubled"), sem("roped"), sem("heads_turned"), sem("heads_copied")
        s_is, s_ie, s_ia, s_mb = sem("index_scores"), sem("index_relu"), sem("index_added"), sem("mask_made")
        s_m0, s_pz = sem("mask0_made"), sem("line_zeroed")
        s_s, s_sm, s_nm, s_ex = sem("scores"), sem("scores_masked"), sem("neg_max"), sem("exp_done")
        s_pr, s_ptp, s_pte = sem("probs"), sem("probs_turned"), sem("probsT_copied")
        s_pv, s_oe = sem("pv_done"), sem("heads_out")
        s_pc, s_dt, s_yp, s_ype = sem("pool_chain"), sem("pool_diff"), sem("pool_y"), sem("pool_y_copied")
        s_pot, s_poe = sem("pool_state_turned"), sem("pool_state_copied")
        s_ops = sem("dense_out_done")
        s_lz, s_lg, s_m, s_cnt, s_slot = sem("logits_zeroed"), sem("logits"), sem("choices"), sem("counts"), sem("slots")
        s_dc, s_bf = sem("vector_chain"), sem("bf16_consts")
        s_ovf, s_nrm4 = sem("overflow_table"), sem("gate_exp_in")
        s_ge = sem("gate_exp")
        s_tabz = sem("slot_tab_cleared")
        s_tab = sem("slot_tab_written")
        s_kvo, s_poo, s_gvo, s_out = sem("kv_out"), sem("pool_state_out"), sem("gm_v_out"), sem("y_out")
        s_wst, s_wsm, s_gps, s_gev = sem("ws_turned"), sem("ws_masked"), sem("gm_in_done"), sem("gelu_done")
        s_ln, s_mx, s_mxe, s_gu, s_gt, s_gte = (sem("v_normed"), sem("mixed"), sem("mixed_copied"), sem("gated"),
                                               sem("gated_turned"), sem("gated_copied"))
        L2 = range(2)
        s_wgu = [[sem(f"gate_up_loaded{l}{b}") for b in range(2)] for l in L2]
        s_wd = [[sem(f"down_loaded{l}{b}") for b in range(2)] for l in L2]
        s_gx = [[sem(f"gather_index{l}{b}") for b in range(2)] for l in L2]
        s_sx = [[sem(f"scatter_index{l}{b}") for b in range(2)] for l in L2]
        s_xg = [[sem(f"gathered{l}{b}") for b in range(2)] for l in L2]
        s_sc = [[sem(f"scattered{l}{b}") for b in range(2)] for l in L2]
        s_xt, s_xte, s_gud = sem("x_turned"), sem("xT_copied"), sem("gate_up_done")
        s_sg, s_hh, s_ht2 = sem("silu_done"), sem("hidden"), sem("hidden_turned")
        s_hte, s_dd, s_yea, s_yed = sem("hiddenT"), sem("down_done"), sem("y_by_act"), sem("y_by_dve")
        s_moe = [sem(f"moe_done{l}") for l in L2]
        s_cl = [[sem(f"y_loaded{l}{b}") for b in range(2)] for l in L2]
        s_cry, o_cry = ([sem(f"{n}{l}") for l in L2] for n in ("carried", "ov_carried"))
        o_ix, o_w, o_xg, o_t, o_te, o_gu = ([sem(f"ov_{n}{l}") for l in L2] for n in
                                            ("index", "weights", "gathered", "turned", "xT", "gate_up"))
        o_sg, o_h, o_ht, o_hte, o_d, o_y, o_sc = ([sem(f"ov_{n}{l}") for l in L2] for n in
                                                  ("silu", "hidden", "hid_turned", "hiddenT", "down", "y", "scattered"))

        IDX_TILES = [1, 2, 3, 4]
        tasks = [("turn", 0)]
        tasks += [("proj", q, j) for q in (0, 1) for j in range(NT)]
        tasks += [("proj", 2, 0)] + [("turn", 1 + j) for j in range(NT)]
        idx = lambda b: [("index", (b - 1) * NIH + h) for h in range(NIH)]
        tasks += idx(1) + [("proj", 2, 1), ("proj", 2, 2)] + idx(2) + [("proj", 2, 3), ("proj", 2, 4), ("proj", 3, 0)]
        tasks += idx(3) + [("proj", 3, j) for j in range(1, NT)] + [("pool", m) for m in range(4)]
        tasks += [("turn", 6 + j) for j in range(NT)] + idx(4) + [("pool", m) for m in range(4, 8)]
        NPROJ = 28
        nkeys = lambda b: PAST + TS if b == 4 else P * (b + 1)
        NU = NT * NH

        def order(q):
            return (3 - q) * QC

        block = es.enter_context(nc.Block())

        @block.sync
        def _(sp):
            def dense(q):
                if q >= 2:
                    sp.wait_ge(s_dwf, q - 1)
                if q < 4:
                    lo = PW_ + order(q)
                    src = a["par_w_in"][0, :, lo:lo + QC].rearrange("(p c) n -> p c n", c=C)
                elif q == 4:
                    src = a["par_w_in"][0, :, 0:PW_].rearrange("(p c) n -> p c n", c=C)
                elif q < 7:
                    src = a["par_w_out"][0, :, (q - 5) * 512:(q - 4) * 512].rearrange("(c p) n -> p c n", c=C)
                elif q < 11:
                    lo = [1024, 1536, 0, 512][q - 7]
                    src = a["gm_w_in"][0, :, lo:lo + 512].rearrange("(p c) n -> p c n", c=C)
                else:
                    src = a["gm_w_out"][0, :, (q - 11) * 512:(q - 10) * 512].rearrange("(p c) n -> p c n", c=C)
                sp.dma_start(dw[:, q % 2, :, 0:src.shape[2]], src).then_inc(s_dw[q % 2], 16)

            def load_gain(n):
                src = [a["norm_mix"][0], a["norm_ffn"][0], a["norm_mix"][1], a["norm_ffn"][1], a["norm_final"]][n]
                if n:
                    sp.wait_ge(s_h, NT * n)
                sp.dma_start(gain[:, :], src.partition_broadcast(P)).then_inc(s_gain, 16)

            def load_router(l):
                if l:
                    sp.wait_ge(s_lg, 1)
                sp.dma_start(wr[:, :, 0:4], a["moe_router_group"][l].rearrange("(p c) n -> p c n", c=C)).then_inc(s_wr, 16)
                sp.dma_start(wr[:, :, 4:36], a["moe_router_expert"][l].rearrange("(p c) n -> p c n", c=C)).then_inc(s_wr, 16)

            def gate_up(l, e, dst, signal):
                sp.dma_start(dst[:, :, 0:FE], a["moe_w_gate"][l, e].rearrange("(p c) n -> p c n", c=C)).then_inc(signal, 16)
                sp.dma_start(dst[:, :, FE:2 * FE], a["moe_w_up"][l, e].rearrange("(p c) n -> p c n", c=C)).then_inc(signal, 16)

            def down(l, e, dst, signal):
                sp.dma_start(dst, a["moe_w_down"][l, e].rearrange("(p c) n -> p c n", c=2)).then_inc(signal, 16)

            def pair_gu(l, i, b):
                for k in range(2):
                    gate_up(l, 2 * i + k, wgu[b][:, k], s_wgu[l][b])

            def pair_dn(l, i, b):
                for k in range(2):
                    down(l, 2 * i + k, wdn[b][:, k], s_wd[l][b])

            def store_rows(n, l):
                for j in range(NT):
                    sp.wait_ge(s_h, NT * n + j + 1)
                    sp.dma_start(h_rows[l][T0[j]:T0[j] + ROWS[j], :], hr[0:ROWS[j], j % 2, :]).then_inc(s_hst[j % 2], 16)

            def indices(l, i, b):
                sp.dma_start(gix[:, b, :], slot_tab[l][bass.ds(i * P, P), :]).then_inc(s_gx[l][b], 16)

            def indices_out(l, i, b):
                sp.dma_start(six[:, b, :], slot_tab[l][bass.ds(i * P, P), :]).then_inc(s_sx[l][b], 16)

            def experts(l):
                sp.wait_ge(s_tab, 16 * 2 * NT * (l + 1))
                for i in range(2):
                    indices(l, i, i)
                    indices_out(l, i, i)

                def pair(i, b, g):
                    sp.wait_ge(s_xg[l][b], 16 * g)
                    indices(l, i, b)
                    sp.wait_ge(s_gud, i - 1 + PAIRS * l)
                    for k in range(2):
                        e = 2 * i + k
                        sp.dma_start(wgu[b][:, k, :, 0:FE], a["moe_w_gate"][l, bass.ds(e, 1)].rearrange("e (p c) n -> p (e c) n", c=C)).then_inc(s_wgu[l][b], 16)
                        sp.dma_start(wgu[b][:, k, :, FE:2 * FE], a["moe_w_up"][l, bass.ds(e, 1)].rearrange("e (p c) n -> p (e c) n", c=C)).then_inc(s_wgu[l][b], 16)
                    sp.wait_ge(s_dd, i - 1 + PAIRS * l)
                    for k in range(2):
                        sp.dma_start(wdn[b][:, k], a["moe_w_down"][l, bass.ds(2 * i + k, 1)].rearrange("e (p c) n -> p (e c) n", c=2)).then_inc(s_wd[l][b], 16)
                    sp.wait_ge(s_sc[l][b], 16 * g)
                    indices_out(l, i, b)

                with sp.Fori(1, PAIRS // 2) as r:
                    pair(2 * r, 0, r)
                    pair(2 * r + 1, 1, r)
                sp.wait_ge(s_ovf, l + 1)
                sp.wait_ge(s_dd, PAIRS + PAIRS * l)
                sp.wait_ge(s_sc[l][0], 16 * PAIRS // 2)
                sp.wait_ge(s_xg[l][0], 16 * PAIRS // 2)
                npairs = sp.value_load(ovf[0:1, NOV + 1:NOV + 2], min_val=0, max_val=NOV // 2)
                with sp.If(npairs > 0):
                    sp.dma_start(gix[:, 0, :], slot_tab[l][MAIN:MAIN + P, :]).then_inc(o_ix[l], 16)
                    sp.dma_start(six[:, 0, :], slot_tab[l][MAIN:MAIN + P, :]).then_inc(o_ix[l], 16)
                    with sp.Fori(0, npairs) as m:
                        for k in range(2):
                            e = sp.value_load(ovf[0:1, bass.ds(2 * m + k, 1)], min_val=0, max_val=NE - 1)
                            sp.dma_start(wgu[0][:, k, :, 0:FE], a["moe_w_gate"][l, bass.ds(e, 1)].rearrange("e (p c) n -> p (e c) n", c=C)).then_inc(o_w[l], 16)
                            sp.dma_start(wgu[0][:, k, :, FE:2 * FE], a["moe_w_up"][l, bass.ds(e, 1)].rearrange("e (p c) n -> p (e c) n", c=C)).then_inc(o_w[l], 16)
                            sp.dma_start(wdn[0][:, k], a["moe_w_down"][l, bass.ds(e, 1)].rearrange("e (p c) n -> p (e c) n", c=2)).then_inc(o_w[l], 16)
                        sp.wait_ge(o_sc[l], 16 * m + 16)
                        sp.dma_start(gix[:, 0, :], slot_tab[l][bass.ds(m * P + MAIN + P, P), :]).then_inc(o_ix[l], 16)
                        sp.dma_start(six[:, 0, :], slot_tab[l][bass.ds(m * P + MAIN + P, P), :]).then_inc(o_ix[l], 16)
                with sp.Else():
                    pass

            def combine(l):
                sp.wait_ge(s_moe[l], 1)
                for j in range(NT):
                    if j >= 2:
                        sp.wait_ge(s_res, 15 * l + 10 + j - 1)
                    sp.dma_start(cb[0:ROWS[j], j % 2], y_rows[l][2 * T0[j]:2 * (T0[j] + ROWS[j]), :]
                                 .rearrange("(p k) n -> p k n", k=2)).then_inc(s_cl[l][j % 2], 16)

            sp.dma_start(x[:, 0, :], a["x_prompt"][0, 0:P, :]).then_inc(s_xl[0], 16)
            sp.dma_start(con[:, :], a["con"]).then_inc(s_con, 16)
            sp.dma_start(icon[:, :], a["icon"]).then_inc(s_con, 16)
            load_gain(0)
            for j in range(1, 4):
                sp.dma_start(x[:, j, :], a["x_prompt"][0, P * j:P * j + P, :]).then_inc(s_xl[j], 16)
            sp.dma_start(x[0:TS, 4, :], a["x_sample"][0]).then_inc(s_xl[4], 16)
            sp.dma_start(kic, a["cache_idx_k"][0, 0]).then_inc(s_cache, 16)
            sp.dma_start(ckr, a["cache_k"][0, 0].rearrange("s h d -> s (h d)")).then_inc(s_cache, 16)
            sp.dma_start(vc, a["cache_v"][0, 0].rearrange("s h d -> s (h d)")).then_inc(s_cache, 16)
            sp.dma_start(sp15[:, :], a["state_pool"][0, 0]).then_inc(s_cache, 16)
            dense(0)
            dense(1)
            sp.dma_start(pscale[:, :], a["par_pool_scale"][0].rearrange("(g p) -> p g", p=P), allow_slow_non_contiguous=True).then_inc(s_small, 16)
            sp.dma_start(gbias[:, :], a["gm_bs"][0].rearrange("g t -> t g"), allow_slow_non_contiguous=True).then_inc(s_small, 16)
            load_router(0)
            sp.wait_ge(s_con, 32)
            for l in range(2):
                sp.dma_start(slot_tab[l].rearrange("(p n) k -> p (n k)", p=P), icon[:, NTOK:]).then_inc(s_tabz, 16)
            sp.wait_ge(s_ssq, NT)
            sp.dma_start(pw[:, :, :], a["par_pool_w"][0].rearrange("g c d -> c g d")).then_inc(s_pwl, 16)
            load_gain(1)
            for q in range(2, 7):
                dense(q)
            sp.wait_ge(s_rope, 2 * NT)
            for o, lo, w in ((2, OK_, 256), (3, OV, 256), (4, OKI, 64)):
                dst = out[o][0, 0] if o == 4 else out[o][0, 0].rearrange("t h d -> t (h d)")
                sp.dma_start(dst.rearrange("(j p) n -> p j n", p=P), R[:, 0:4, lo:lo + w]).then_inc(s_kvo, 16)
                dst = out[o + 4][0, 0] if o == 4 else out[o + 4][0, 0].rearrange("t h d -> t (h d)")
                sp.dma_start(dst, R[0:TS, 4, lo:lo + w]).then_inc(s_kvo, 16)
            sp.wait_ge(s_poe, 1)
            for k in range(2):
                sp.dma_start(out[5 + 4 * k][0, 0], pool_out[0:HIST, k, :]).then_inc(s_poo, 16)
            sp.wait_ge(s_kvo, 16 * 6)
            sp.wait_ge(s_poo, 16 * 2)
            sp.wait_ge(s_pv, NU)
            for i in range(2):
                pair_gu(0, i, i)
                pair_dn(0, i, i)
            dense(7)
            dense(8)
            store_rows(1, 0)
            load_gain(2)
            experts(0)
            combine(0)
            for b in range(2):
                sp.dma_start(*((lng, a["gm_ln_g"][0].partition_broadcast(P)) if b else
                               (lnb, a["gm_ln_b"][0].partition_broadcast(P)))).then_inc(s_gml, 16)
            sp.dma_start(wsr, a["gm_ws"][0].rearrange("g t s -> t g s")).then_inc(s_gml, 16)
            load_router(1)
            pair_gu(1, 0, 0)
            pair_dn(1, 0, 0)
            pair_gu(1, 1, 1)
            load_gain(3)
            dense(9)
            dense(10)
            sp.wait_ge(s_ln, NT)
            sp.dma_start(out[10][0, 0], v[0:TS, 4, :]).then_inc(s_gvo, 16)
            dense(11)
            dense(12)
            sp.wait_ge(s_gt, NT)
            sp.wait_ge(s_gu, 2 * NT)
            pair_dn(1, 1, 1)
            store_rows(3, 1)
            load_gain(4)
            experts(1)
            combine(1)
            for j in range(NT):
                sp.wait_ge(s_h, 4 * NT + j + 1)
                dst = out[0][0, T0[j]:T0[j] + P, :] if j < 4 else out[1][0]
                sp.dma_start(dst, hr[0:ROWS[j], j % 2, :]).then_inc(s_hst[j % 2], 16)
            sp.wait_ge(s_hst[0], 16 * 9)
            sp.wait_ge(s_hst[1], 16 * 6)
            sp.wait_ge(s_gvo, 16)

        @block.gpsimd
        def _(pool):
            done = [0]

            def link(ins):
                done[0] += 1
                ins.then_inc(s_pc, 1)
                pool.wait_ge(s_pc, done[0])

            pool.memset(eps[:, 0:1], 1e-6).then_inc(s_eps, 1)
            pool.memset(eps[:, 1:2], 1e-5).then_inc(s_eps, 1)
            link(pool.memset(cell[:, :], 0.0))
            pool.memset(line[:, :, 0:HIST], 0.0).then_inc(s_pz, 1)
            link(pool.memset(index[:, 0, 0:P], 0.0))
            pool.memset(index[0:64, 0, 64:P], NEG).then_inc(s_m0, 1)
            pool.wait_ge(s_pev, NPROJ)
            pool.wait_ge(s_pz, 1)
            pool.wait_ge(s_te, 1)
            for g in range(NG):
                src, w = line[:, g, :], 1
                for i in range(g + 1):
                    dst = (ta, tb)[i % 2]
                    w *= 2
                    link(pool.tensor_tensor(dst[:, w - 1:LINE], src[:, w - 1:LINE], src[:, w - 1 - w // 2:LINE - w // 2], ALU.add))
                    src = dst
                dst = (ta, tb)[(g + 1) % 2]
                pool.tensor_tensor(dst[:, XP0:XP0 + 16], src[:, XP0:XP0 + 16], c_("rcnt", NG)[:, g, :], ALU.mult)
                link(pool.tensor_scalar(dst[:, XP0 + 16:LINE], src[:, XP0 + 16:LINE], 1.0 / w, None, ALU.mult))
                pool.tensor_tensor(dT[:, g, 0:TP], dst[:, XP0:XP0 + TP], line[:, g, XP0:XP0 + TP], ALU.subtract)
                link(pool.tensor_tensor(dT[:, g, TP:T], dst[:, XS0:LINE], line[:, g, XS0:LINE], ALU.subtract))
                pool.nop().then_inc(s_dt, 1)

            def carry(signal, to, before=None):
                if before is not None:
                    pool.wait_ge(signal, before)
                pool.tensor_tensor(cell[:, to:to + 1], cell[:, 4:5], cell[:, 5:6], ALU.add).then_inc(signal, 1)

            def gather(l, i, b, g, turned=None, before=None):
                if turned is not None:
                    pool.wait_ge(s_xt, turned + PAIRS * l)
                pool.wait_ge(s_gx[l][b], 16 * g)
                carry(s_cry[l], 2 * l, before)
                pool.indirect_dma_start(xg[:, b, :], None, h_rows[l], bass.IndirectOffsetOnAxis(ap=gix[:, b, 0:1], axis=0),
                                        bounds_check=T - 1, oob_is_err=False).then_inc(s_xg[l][b], 16)

            def scatter(l, i, b, g, before):
                pool.wait_ge(s_sx[l][b], 16 * g)
                pool.wait_ge(s_yea, i + 1 + PAIRS * l)
                pool.wait_ge(s_yed, i + 1 + PAIRS * l)
                carry(s_cry[l], 2 * l, before)
                pool.indirect_dma_start(y_rows[l], bass.IndirectOffsetOnAxis(ap=six[:, b, 1:2], axis=0), yb[:, b, :], None,
                                        bounds_check=2 * T - 1, oob_is_err=False).then_inc(s_sc[l][b], 16)

            for l in range(2):
                pool.wait_ge(s_tabz, 32)
                pool.wait_ge(s_slot, l + 1)
                for j in range(NT):
                    for k in range(2):
                        n = ROWS[j]
                        pool.indirect_dma_start(slot_tab[l], bass.IndirectOffsetOnAxis(ap=slot_i[0:n, j, k:k + 1], axis=0),
                                                icon[0:n, 4 * j + 2 * k:4 * j + 2 * k + 2], None,
                                                bounds_check=SLOTS - 1, oob_is_err=False).then_inc(s_tab, 16)
                for b in range(2):
                    pool.wait_ge(s_hst[b], 16 * ((3 - b) * (l + 1)))
                pool.wait_ge(s_tp, NT * (2 * l + 2))
                gather(l, 0, 0, 1)
                gather(l, 1, 1, 1, before=1)

                def step(i, b, g):
                    gather(l, i + 2, b, g + 2, i + 1, 2 * i + 2)
                    scatter(l, i, b, g + 1, 2 * i + 3)

                with pool.Fori(0, PAIRS // 2 - 1) as r:
                    step(2 * r, 0, r)
                    step(2 * r + 1, 1, r)
                scatter(l, PAIRS - 2, 0, PAIRS // 2, 2 * PAIRS - 2)
                scatter(l, PAIRS - 1, 1, PAIRS // 2, 2 * PAIRS - 1)
                for b in range(2):
                    pool.wait_ge(s_sc[l][b], 16 * PAIRS // 2)
                pool.wait_ge(s_ovf, l + 1)
                npairs = pool.value_load(ovf[0:1, NOV + 1:NOV + 2], min_val=0, max_val=NOV // 2)
                with pool.If(npairs > 0):
                    carry(o_cry[l], 2 * l + 1)
                    with pool.Fori(0, npairs) as m:
                        pool.wait_ge(o_ix[l], 32 * m + 32)
                        carry(o_cry[l], 2 * l + 1, 3 * m + 1)
                        pool.indirect_dma_start(xg[:, 0, :], None, h_rows[l], bass.IndirectOffsetOnAxis(ap=gix[:, 0, 0:1], axis=0),
                                                bounds_check=T - 1, oob_is_err=False).then_inc(o_xg[l], 16)
                        pool.wait_ge(o_y[l], 2 * m + 2)
                        carry(o_cry[l], 2 * l + 1, 3 * m + 2)
                        pool.indirect_dma_start(y_rows[l], bass.IndirectOffsetOnAxis(ap=six[:, 0, 1:2], axis=0), yb[:, 0, :], None,
                                                bounds_check=2 * T - 1, oob_is_err=False).then_inc(o_sc[l], 16)
                        pool.wait_ge(o_sc[l], 16 * m + 16)
                        carry(o_cry[l], 2 * l + 1, 3 * m + 3)
                    pool.wait_ge(o_ix[l], 32 * npairs + 32)
                    carry(o_cry[l], 2 * l + 1, 3 * npairs + 1)
                with pool.Else():
                    pass
                pool.nop().then_inc(s_moe[l], 1)

        @block.scalar
        def _(act):
            def copy(dst, src):
                return act.activation(dst, src, ACT.Copy)

            def norm(n):
                def square(j):
                    if n == 0:
                        act.wait_ge(s_xl[j], 16)
                    else:
                        act.wait_ge(s_res, [0, 10, 15, 25, 30][n] - NT + j + 1)
                    act.activation(junk[0:ROWS[j], :], x[0:ROWS[j], j, :], ACT.Square, scale=D ** -0.5,
                                   accum_out=st[0:ROWS[j], j:j + 1]).then_inc(s_ssq, 1)
                    act.wait_ge(s_ssq, NT * n + j + 1)
                    act.activation(st[0:ROWS[j], 5 + j:6 + j], st[0:ROWS[j], j:j + 1], ACT.Sqrt, bias=eps[0:ROWS[j], 0:1]).then_inc(s_rs, 1)

                def hT_copy(j):
                    act.wait_ge(s_tp, NT * n + j + 1)
                    for k in range(2):
                        ins = copy(hT[:, 4 * k:4 * k + 4, T0[j]:T0[j] + ROWS[j]],
                                   ps[2 * (j % 2) + k][:, :].rearrange("p (c t) -> p c t", c=4)[:, :, 0:ROWS[j]])
                    ins.then_inc(s_ht, 1)
                square(0)
                for j in range(NT):
                    if j + 1 < NT:
                        square(j + 1)
                    if n < 4:
                        hT_copy(j)

            act.wait_ge(s_eps, 2)
            norm(0)
            for task in tasks:
                if task[0] == "proj":
                    _, q, j = task
                    n = NT * q + j
                    act.wait_ge(s_pps, n + 1)
                    copy(R[0:ROWS[j], j, order(q):order(q) + QC], ps[4 + n % 4][0:ROWS[j], 0:QC]).then_inc(s_pev, 1)
                elif task[0] == "pool":
                    m = task[1]
                    g, n = m // 2, 20 + m
                    act.wait_ge(s_pps, n + 1)
                    acc = ps[4 + n % 4]
                    if m % 2 == 0:
                        copy(line[:, g, XP0:XP0 + HALF], acc[:, 0:HALF]).then_inc(s_pev, 1)
                    else:
                        copy(line[:, g, XP0 + HALF:XP0 + TP], acc[:, 0:TP - HALF])
                        copy(line[:, g, XS0:LINE], acc[:, TP - HALF:HALF]).then_inc(s_pev, 1)
                elif task[0] == "turn":
                    i = task[1]
                    act.wait_ge(s_tt, i + 1)
                    b0 = ps[0][:, :].rearrange("p (a n) -> p a n", a=4)
                    b1 = ps[1][:, :].rearrange("p (a n) -> p a n", a=4)
                    if i == 0:
                        copy(kiTs[:, 0:PAST], b0[:, 0, :])
                        copy(line[:, :, XS0 - HIST:XS0], ps[0][:, 128:192].rearrange("p (g n) -> p g n", g=4)[:, :, 0:HIST])
                        copy(kTs[:, :, 0:PAST], b1).then_inc(s_te, 1)
                    elif i < 6:
                        j = i - 1
                        copy(qiT[:, :, T0[j]:T0[j] + ROWS[j]], b0[:, :, 0:ROWS[j]])
                        dst = kiT[:, T0[j]:T0[j] + P] if j < 4 else kiTs[:, PAST:PAST + TS]
                        copy(dst, b1[:, 0, 0:ROWS[j]]).then_inc(s_te, 1)
                    else:
                        j = i - 6
                        copy(qT[:, :, T0[j]:T0[j] + ROWS[j]], b0[:, :, 0:ROWS[j]])
                        dst = kT[:, :, T0[j]:T0[j] + P] if j < 4 else kTs[:, :, PAST:PAST + TS]
                        copy(dst, b1[:, :, 0:ROWS[j]]).then_inc(s_te, 1)
                else:
                    u = task[1]
                    b = IDX_TILES[u // NIH]
                    act.wait_ge(s_is, u + 1)
                    if u >= 2:
                        act.wait_ge(s_ia, u - 1)
                    act.activation(rl[0:ROWS[b], u % 2, 0:nkeys(b)], ps[2 + u % 2][0:ROWS[b], 0:nkeys(b)],
                                   ACT.Relu).then_inc(s_ie, 1)

            def exp(u):
                b = u // NH
                n, r = nkeys(b), ROWS[b]
                act.wait_ge(s_nm, u + 1)
                if u >= 2:
                    act.wait_ge(s_ptp, u - 1)
                act.activation(pr[0:r, u % 2, 0:n], sm[0:r, u % 2, 0:n], ACT.Exp, bias=st[0:r, 10 + u % 2:11 + u % 2],
                               scale=SCALE, accum_out=st[0:r, 12 + u % 2:13 + u % 2]).then_inc(s_ex, 1)

            def probsT(u):
                b = u // NH
                act.wait_ge(s_ptp, u + 1)
                if u >= 2:
                    act.wait_ge(s_pv, u - 1)
                src, dst = (z.rearrange("p (c n) -> p c n", c=4) for z in (ps[u % 2][:, :], pT[:, u % 2, :]))
                if b < 4:
                    copy(dst[:, 0:b + 1, :], src[:, 0:b + 1, :]).then_inc(s_pte, 1)
                else:
                    copy(dst[:, 0, 0:TS], src[:, 0, 0:TS])
                    copy(dst[0:TS, 1, 0:TS], src[0:TS, 1, 0:TS]).then_inc(s_pte, 1)

            def heads(k):
                b, g = k // NKV, k % NKV
                act.wait_ge(s_pv, 2 * k + 2)
                copy(hT[:, 4 + g, T0[b]:T0[b] + ROWS[b]], ps[4 + k % 2][:, 0:ROWS[b]]).then_inc(s_oe, 1)

            exp(0)
            for u in range(NU):
                if u + 1 < NU:
                    exp(u + 1)
                probsT(u)
                if u % 2 == 0 and u:
                    heads(u // 2 - 1)
            heads(NU // 2 - 1)
            act.wait_ge(s_pot, 1)
            for k in range(2):
                ins = copy(pool_out[0:HIST, k, :], ps[6 + k][0:HIST, :])
            ins.then_inc(s_poe, 1)
            act.wait_ge(s_small, 32)
            for m in range(8):
                act.wait_ge(s_yp, m + 1)
                g = m // 2
                act.activation(hT[:, g, (m % 2) * HALF:(m % 2 + 1) * HALF], ps[6 + m % 2][:, 0:HALF], ACT.Copy,
                               scale=pscale[:, g:g + 1]).then_inc(s_ype, 1)

            def experts(l):
                act.wait_ge(s_nrm4, l + 1)
                act.activation(gex[:, :, :], ls[:, :, 0:4], ACT.Exp)
                act.activation(gsm[:, :, 1:2], gdf[:, :, 0:1], ACT.Exp).then_inc(s_ge, 1)

                def turned(i, b, first=False):
                    act.wait_ge(s_xt, i + 1 + PAIRS * l)
                    if not first:
                        act.wait_ge(s_gud, i - 1 + PAIRS * l)
                    for k in range(2):
                        ins = copy(xT[:, b, 4 * k:4 * k + 4, :], ps[k][:, :].rearrange("p (c t) -> p c t", c=4))
                    ins.then_inc(s_xte, 1)

                def rest(i, b, g, first=False, last=False):
                    act.wait_ge(s_gud, i + 1 + PAIRS * l)
                    if not (first and b == 0):
                        act.wait_ge(s_hh, i + PAIRS * l)
                    act.activation(sg, ps[2 + b][:, 0:FE], ACT.Silu).then_inc(s_sg, 1)
                    if not (last and b == 1):
                        turned(i + 1, 1 - b, first and b == 0)
                    act.wait_ge(s_dd, i + 1 + PAIRS * l)
                    if not first:
                        act.wait_ge(s_sc[l][b], 16 * g)
                    copy(yb[:, b, 512:1024], ps[7][:, :]).then_inc(s_yea, 1)

                turned(0, 0, True)
                rest(0, 0, 0, True)
                rest(1, 1, 0, True)
                with act.Fori(1, PAIRS // 2 - 1) as r:
                    rest(2 * r, 0, r)
                    rest(2 * r + 1, 1, r)
                rest(PAIRS - 2, 0, PAIRS // 2 - 1)
                rest(PAIRS - 1, 1, PAIRS // 2 - 1, last=True)
                act.wait_ge(s_ovf, l + 1)
                npairs = act.value_load(ovf[0:1, NOV + 1:NOV + 2], min_val=0, max_val=NOV // 2)
                with act.If(npairs > 0):
                    with act.Fori(0, npairs) as m:
                        act.wait_ge(o_t[l], m + 1)
                        for k in range(2):
                            ins = copy(xT[:, 0, 4 * k:4 * k + 4, :], ps[k][:, :].rearrange("p (c t) -> p c t", c=4))
                        ins.then_inc(o_te[l], 1)
                        act.wait_ge(o_gu[l], m + 1)
                        act.activation(sg, ps[2][:, 0:FE], ACT.Silu).then_inc(o_sg[l], 1)
                        act.wait_ge(o_d[l], m + 1)
                        copy(yb[:, 0, 512:1024], ps[7][:, :]).then_inc(o_y[l], 1)
                with act.Else():
                    pass

            norm(1)
            experts(0)
            norm(2)
            for n in range(2 * NT):
                j = n % NT
                act.wait_ge(s_gps, n + 1)
                act.activation(v[0:ROWS[j], j, (n // NT) * 512:(n // NT + 1) * 512], ps[4 + n % 4][0:ROWS[j], :],
                               ACT.Gelu_apprx_tanh).then_inc(s_gev, 1)

            def v_root(j):
                act.wait_ge(s_va, j + 1)
                act.activation(st[0:ROWS[j], 46 + j:47 + j], st[0:ROWS[j], 37 + 2 * j:38 + 2 * j], ACT.Sqrt,
                               bias=eps[0:ROWS[j], 1:2]).then_inc(s_vr, 1)

            def u_gelu(n):
                j = n % NT
                act.wait_ge(s_gps, n + 1)
                if n - 2 * NT >= 2:
                    act.wait_ge(s_gu, n - 2 * NT - 1)
                else:
                    act.wait_ge(s_wsm, 1)
                act.activation(ut[0:ROWS[j], n % 2, :], ps[4 + n % 4][0:ROWS[j], :], ACT.Gelu_apprx_tanh).then_inc(s_gev, 1)

            def gated(j):
                act.wait_ge(s_gt, j + 1)
                for k in range(2):
                    ins = copy(hT[:, 4 * k:4 * k + 4, T0[j]:T0[j] + ROWS[j]],
                               ps[2 * (j % 2) + k][:, :].rearrange("p (c t) -> p c t", c=4)[:, :, 0:ROWS[j]])
                ins.then_inc(s_gte, 1)
            for j in range(NT):
                v_root(j)
            for n in range(2 * NT, 3 * NT + 1):
                u_gelu(n)
            for j in range(NT):
                if j + 1 < NT:
                    u_gelu(3 * NT + j + 1)
                gated(j)
            norm(3)
            experts(1)
            norm(4)

        @block.vector
        def _(dve):
            done = [0]

            def link(ins):
                done[0] += 1
                ins.then_inc(s_dc, 1)
                dve.wait_ge(s_dc, done[0])

            def inverse_root(r, square, root, e, dst):
                link(dve.reciprocal(dst, root))
                link(dve.scalar_tensor_tensor(st[0:r, 60:61], square, e, dst, ALU.add, ALU.mult))
                link(dve.tensor_tensor(st[0:r, 60:61], st[0:r, 60:61], dst, ALU.mult))
                link(dve.tensor_scalar(st[0:r, 60:61], st[0:r, 60:61], -0.5, 1.5, ALU.mult, ALU.add))
                link(dve.tensor_tensor(dst, dst, st[0:r, 60:61], ALU.mult))

            def norm(n):
                dve.wait_ge(s_gain, 16 * (n + 1))
                for j in range(NT):
                    r = ROWS[j]
                    dve.wait_ge(s_rs, NT * n + j + 1)
                    inverse_root(r, st[0:r, j:j + 1], st[0:r, 5 + j:6 + j], 1e-6, st[0:r, 14 + j:15 + j])
                    if j >= 2:
                        if n < 4:
                            dve.wait_ge(s_tp, NT * n + j - 1)
                        if n in (1, 3, 4):
                            before = {1: 0, 3: 1, 4: 2}[n] * (3 - j % 2) + j // 2
                            dve.wait_ge(s_hst[j % 2], 16 * before)
                    dve.scalar_tensor_tensor(hr[0:r, j % 2, :], x[0:r, j, :], st[0:r, 14 + j:15 + j], gain[0:r, :],
                                             ALU.mult, ALU.mult).then_inc(s_h, 1)

            def rope(j, lo, nh, dup, dst_n):
                r = ROWS[j]
                hv = R[0:r, j, lo:lo + nh * HD].rearrange("p (h d) -> p h d", h=nh)
                x1, x2 = hv[:, :, 0:8], hv[:, :, 8:16]
                co = cos[0:r, j, :].unsqueeze(1).to_broadcast([r, nh, 8])
                si = sin[0:r, j, :].unsqueeze(1).to_broadcast([r, nh, 8])
                t = [rt[0:r, k, 0:nh * 8].rearrange("p (h d) -> p h d", h=nh) for k in range(4)]
                dve.tensor_tensor(t[0], x1, co, ALU.mult)
                dve.tensor_tensor(t[1], x2, si, ALU.mult)
                dve.tensor_tensor(t[2], x2, co, ALU.mult)
                link(dve.tensor_tensor(t[3], x1, si, ALU.mult))
                dve.tensor_tensor(x1, t[0], t[1], ALU.subtract)
                link(dve.tensor_tensor(x2, t[2], t[3], ALU.add))
                if j >= 2:
                    dve.wait_ge(s_tt, dst_n - 1)
                dve.tensor_copy(dup[0], dup[1]).then_inc(s_rope, 1)

            dve.wait_ge(s_con, 32)
            dve.tensor_copy(cbf[:, 0, :], c_("upper"))
            dve.tensor_copy(cbf[:, 1, :], c_("ones")).then_inc(s_bf, 1)
            dve.wait_ge(s_cache, 64)
            dve.tensor_copy(kdc[:, 0, :].rearrange("p (b n) -> p b n", b=2), kic.unsqueeze(1).to_broadcast([P, 2, HD]))
            for g in range(NKV):
                ins = dve.tensor_copy(kdc[:, 1 + g, :].rearrange("p (b n) -> p b n", b=2),
                                      ckr[:, g * HD:(g + 1) * HD].unsqueeze(1).to_broadcast([P, 2, HD]))
            ins.then_inc(s_dup, 1)
            norm(0)
            for j in range(NT):
                dve.wait_ge(s_pev, NT + j + 1)
                rope(j, OQI, NIH + 1, (kdi[0:ROWS[j], j % 2, :].rearrange("p (b n) -> p b n", b=2),
                                       R[0:ROWS[j], j, OKI:OKI + HD].unsqueeze(1).to_broadcast([ROWS[j], 2, HD])), j + 1)

            def index_add(b):
                r, n = ROWS[b], nkeys(b)
                acc = index[0:r, b, 0:n]
                for h in range(NIH):
                    u = IDX_TILES.index(b) * NIH + h
                    dve.wait_ge(s_ie, u + 1)
                    wi = R[0:r, b, OWI + h:OWI + h + 1]
                    if h == 0:
                        dve.tensor_scalar(acc, rl[0:r, u % 2, 0:n], wi, None, ALU.mult).then_inc(s_ia, 1)
                    else:
                        dve.scalar_tensor_tensor(acc, rl[0:r, u % 2, 0:n], wi, acc, ALU.mult, ALU.add).then_inc(s_ia, 1)
                    dve.wait_ge(s_ia, u + 1)

            def top_k(b):
                r, n = ROWS[b], nkeys(b)
                acc = index[0:r, b, 0:n]
                if b < 4:
                    link(dve.memset(index[0:64, b, n - 64:n], NEG_ADM))
                for _ in range((TK_P if b < 4 else TK_S) // 8):
                    link(dve.max(m8[0:r, :], acc))
                    link(dve.match_replace(acc, m8[0:r, :], acc, NEG_SEL))
                dve.tensor_scalar(acc, acc, 0.5 * (NEG_SEL + NEG_ADM), NEG, ALU.is_gt, ALU.mult).then_inc(s_mb, 1)

            for b in (1, 2, 3):
                index_add(b)
                top_k(b)
            for j in range(NT):
                dve.wait_ge(s_pev, 3 * NT + j + 1)
                r = ROWS[j]
                rope(j, OQ, NH + NKV, (kd[0:r, j % 2].rearrange("p a (b n) -> p a b n", b=2),
                                       R[0:r, j, OK_:OK_ + 256].rearrange("p (a n) -> p a n", a=NKV).unsqueeze(2)
                                       .to_broadcast([r, NKV, 2, HD])), j + 6)
            index_add(4)
            top_k(4)

            def masked(u):
                b = u // NH
                r, n = ROWS[b], nkeys(b)
                dve.wait_ge(s_s, u + 1)
                if b == 0:
                    dve.wait_ge(s_m0, 1)
                else:
                    dve.wait_ge(s_mb, b)
                if u >= 2:
                    dve.wait_ge(s_ex, u - 1)
                dve.tensor_tensor_reduce(sm[0:r, u % 2, 0:n], ps[2 + u % 2][0:r, 0:n], index[0:r, b, 0:n], 1.0, -3.0e38,
                                         ALU.add, ALU.max, st[0:r, 20 + u % 2:21 + u % 2]).then_inc(s_sm, 1)
                dve.wait_ge(s_sm, u + 1)
                dve.tensor_scalar(st[0:r, 10 + u % 2:11 + u % 2], st[0:r, 20 + u % 2:21 + u % 2], -SCALE, None,
                                  ALU.mult).then_inc(s_nm, 1)

            def normed(u):
                b = u // NH
                r, n = ROWS[b], nkeys(b)
                dve.wait_ge(s_ex, u + 1)
                link(dve.reciprocal(st[0:r, 22 + u % 2:23 + u % 2], st[0:r, 12 + u % 2:13 + u % 2]))
                dve.tensor_scalar(pr[0:r, u % 2, 0:n], pr[0:r, u % 2, 0:n], st[0:r, 22 + u % 2:23 + u % 2], None,
                                  ALU.mult).then_inc(s_pr, 1)

            masked(0)
            for u in range(NU):
                if u + 1 < NU:
                    masked(u + 1)
                normed(u)

            def dense_out(k):
                for n in range(2 * NT):
                    hf, j = n // NT, n % NT
                    r = ROWS[j]
                    dve.wait_ge(s_ops, 10 * k + n + 1)
                    xs = x[0:r, j, hf * 512:hf * 512 + 512]
                    dve.tensor_tensor(xs, xs, ps[4 + n % 4][0:r, :], ALU.add).then_inc(s_res, 1)

            def route(l):
                bc = lambda name: c_(name).unsqueeze(1).to_broadcast([P, NT, NE])
                dve.wait_ge(s_lg, l + 1)
                link(dve.memset(lgp, NEG))
                link(dve.tensor_copy(ls, ps[4][:, 0:180].rearrange("p (j n) -> p j n", j=NT)))
                link(dve.tensor_copy(lgp[:, :, 0:4], ls[:, :, 0:4]))
                for j in range(NT):
                    link(dve.max(mg[:, j, :], lgp[:, j, :]))
                    link(dve.max_index(ig[:, j, :].bitcast(U32), mg[:, j, :], lgp[:, j, :]))
                link(dve.tensor_copy(igf, ig[:, :, 0:1].bitcast(U32)))
                link(dve.tensor_tensor(lem, bc("egrp"), igf.to_broadcast([P, NT, NE]), ALU.not_equal))
                link(dve.scalar_tensor_tensor(lem, lem, NEG, ls[:, :, 4:36], ALU.mult, ALU.add))
                for j in range(NT):
                    link(dve.max(me[:, j, :], lem[:, j, :]))
                    link(dve.max_index(ie[:, j, :].bitcast(U32), me[:, j, :], lem[:, j, :]))
                link(dve.tensor_tensor(ls[:, :, 0:4], ls[:, :, 0:4], mg[:, :, 0:1].to_broadcast([P, NT, 4]), ALU.subtract))
                dve.tensor_tensor(gdf[:, :, 0:1], me[:, :, 1:2], me[:, :, 0:1], ALU.subtract).then_inc(s_nrm4, 1)
                link(dve.tensor_copy(ief, ie[:, :, 0:2].bitcast(U32)))
                for k in range(2):
                    link(dve.tensor_tensor(oh[k], bc("iota"), ief[:, :, k:k + 1].to_broadcast([P, NT, NE]), ALU.is_equal))
                dve.tensor_tensor(mbf, oh[0], oh[1], ALU.add).then_inc(s_m, 1)
                dve.wait_ge(s_cnt, l + 1)
                link(dve.tensor_scalar(cnti, ps[5][:, 160:192], float(BLK - 1), None, ALU.add))
                link(dve.tensor_scalar(cnti, cnti, 6, None, ALU.logical_shift_right))
                link(dve.tensor_scalar(nov, cnti, -1.0, 0.0, ALU.add, ALU.max))
                link(dve.tensor_tensor_scan(inc, c_("ones")[:, 0:NE], nov, 0.0, ALU.mult, ALU.add))
                link(dve.tensor_tensor(dlt, inc, nov, ALU.subtract))
                link(dve.tensor_scalar(dlt, dlt, float(BLK), float(MAIN - BLK), ALU.mult, ALU.add))
                link(dve.tensor_tensor(dlt, dlt, c_("base"), ALU.subtract))
                pp = ps[5][:, 0:160].rearrange("p (j n) -> p j n", j=NT)
                link(dve.scalar_tensor_tensor(slt, pp, float(BLK), dlt.unsqueeze(1).to_broadcast([P, NT, NE]), ALU.is_ge, ALU.mult))
                link(dve.tensor_tensor(slt, slt, pp, ALU.add))
                link(dve.tensor_tensor(slt, slt, bc("base"), ALU.add))
                for k in range(2):
                    link(dve.tensor_tensor(slo, slt, oh[k], ALU.mult))
                    link(dve.tensor_reduce(slf[:, :, k:k + 1], slo, AX.X, ALU.add))
                dve.tensor_copy(slot_i[:, :, :], slf).then_inc(s_slot, 1)
                link(dve.tensor_tensor(ov1, c_("nov", NOV), inc.unsqueeze(1).to_broadcast([P, NOV, NE]), ALU.is_ge))
                link(dve.tensor_reduce(ov2[:, 0:NOV].unsqueeze(2), ov1, AX.X, ALU.add))
                link(dve.tensor_scalar(ov2[:, 0:NOV], ov2[:, 0:NOV], float(NE - 1), None, ALU.min))
                link(dve.tensor_copy(ov2[:, NOV:NOV + 1], inc[:, NE - 1:NE]))
                link(dve.tensor_scalar(ov2[:, NOV + 1:NOV + 2], inc[:, NE - 1:NE], 1.0, None, ALU.add))
                link(dve.tensor_copy(ovf[:, :], ov2))
                dve.tensor_scalar(ovf[:, NOV + 1:NOV + 2], ovf[:, NOV + 1:NOV + 2], 1, None, ALU.logical_shift_right).then_inc(s_ovf, 1)
                dve.wait_ge(s_ge, l + 1)
                link(dve.tensor_reduce(gdf[:, :, 0:1], gex, AX.X, ALU.add))
                link(dve.tensor_scalar(gdf[:, :, 1:2], gsm[:, :, 1:2], 1.0, None, ALU.add))
                link(dve.tensor_tensor(gdf[:, :, 0:1], gdf[:, :, 0:1], gdf[:, :, 1:2], ALU.mult))
                link(dve.reciprocal(gates[:, :, 0:1], gdf[:, :, 0:1]))
                link(dve.tensor_tensor(gates[:, :, 1:2], gates[:, :, 0:1], gsm[:, :, 1:2], ALU.mult))

            def experts(l):
                def pair(i, b, g, first=False):
                    dve.wait_ge(s_sg, i + 1 + PAIRS * l)
                    if not (first and b == 0):
                        dve.wait_ge(s_ht2, i + PAIRS * l)
                    dve.tensor_tensor(hh, sg, ps[2 + b][:, FE:2 * FE], ALU.mult).then_inc(s_hh, 1)
                    dve.wait_ge(s_ht2, i + 1 + PAIRS * l)
                    if not first:
                        dve.wait_ge(s_dd, i - 1 + PAIRS * l)
                    dve.tensor_copy(hhT[:, b], ps[4][:, 0:256].rearrange("p (c n) -> p c n", c=2)).then_inc(s_hte, 1)
                    dve.wait_ge(s_dd, i + 1 + PAIRS * l)
                    if not first:
                        dve.wait_ge(s_sc[l][b], 16 * g)
                    dve.tensor_copy(yb[:, b, 0:512], ps[6][:, :]).then_inc(s_yed, 1)
                pair(0, 0, 0, True)
                pair(1, 1, 0, True)
                with dve.Fori(1, PAIRS // 2) as r:
                    pair(2 * r, 0, r)
                    pair(2 * r + 1, 1, r)
                dve.wait_ge(s_ovf, l + 1)
                npairs = dve.value_load(ovf[0:1, NOV + 1:NOV + 2], min_val=0, max_val=NOV // 2)
                with dve.If(npairs > 0):
                    with dve.Fori(0, npairs) as m:
                        dve.wait_ge(o_sg[l], m + 1)
                        dve.tensor_tensor(hh, sg, ps[2][:, FE:2 * FE], ALU.mult).then_inc(o_h[l], 1)
                        dve.wait_ge(o_ht[l], m + 1)
                        dve.tensor_copy(hhT[:, 0], ps[4][:, 0:256].rearrange("p (c n) -> p c n", c=2)).then_inc(o_hte[l], 1)
                        dve.wait_ge(o_d[l], m + 1)
                        dve.tensor_copy(yb[:, 0, 0:512], ps[6][:, :]).then_inc(o_y[l], 1)
                with dve.Else():
                    pass
                for j in range(NT):
                    r = ROWS[j]
                    dve.wait_ge(s_cl[l][j % 2], 16 * (j // 2 + 1))
                    link(dve.scalar_tensor_tensor(x[0:r, j, :], cb[0:r, j % 2, 0, :], gates[0:r, j, 0:1], x[0:r, j, :],
                                                  ALU.mult, ALU.add))
                    dve.scalar_tensor_tensor(x[0:r, j, :], cb[0:r, j % 2, 1, :], gates[0:r, j, 1:2], x[0:r, j, :],
                                             ALU.mult, ALU.add).then_inc(s_res, 1)

            def zero_logits(l):
                dve.wait_ge(s_res, 15 * l + 10)
                dve.memset(ps[4][64:P, 144:180], 0.0).then_inc(s_lz, 1)

            dense_out(0)
            zero_logits(0)
            norm(1)
            route(0)
            experts(0)
            norm(2)
            dve.wait_ge(s_wst, 1)
            for k in range(2):
                ins = dve.tensor_tensor(wsm[:, 4 * k:4 * k + 4, :], ps[k][:, :].rearrange("p (g n) -> p g n", g=4),
                                        c_("tri").unsqueeze(1).to_broadcast([P, 4, P]), ALU.mult)
            ins.then_inc(s_wsm, 1)
            dve.wait_ge(s_gml, 48)
            for j in range(NT):
                r = ROWS[j]
                dve.wait_ge(s_gev, NT + j + 1)
                for k in range(2):
                    ins = dve.bn_stats(st[0:r, 24 + 6 * k:30 + 6 * k], v[0:r, j, k * 512:k * 512 + 512])
                link(ins)
                dve.bn_aggr(st[0:r, 36 + 2 * j:38 + 2 * j], st[0:r, 24:36]).then_inc(s_va, 1)
                dve.wait_ge(s_va, j + 1)
                dve.scalar_tensor_tensor(v[0:r, j, :], v[0:r, j, :], st[0:r, 36 + 2 * j:37 + 2 * j], lng[0:r, :], ALU.subtract, ALU.mult).then_inc(s_vc, 1)
                dve.wait_ge(s_vc, j + 1)
                dve.wait_ge(s_vr, j + 1)
                inverse_root(r, st[0:r, 37 + 2 * j:38 + 2 * j], st[0:r, 46 + j:47 + j], 1e-5, st[0:r, 51 + j:52 + j])
                dve.scalar_tensor_tensor(v[0:r, j, :], v[0:r, j, :], st[0:r, 51 + j:52 + j], lnb[0:r, :], ALU.mult, ALU.add).then_inc(s_ln, 1)

            def mix_out(j):
                r = ROWS[j]
                dve.wait_ge(s_mx, j + 1)
                if j == 0:
                    dve.wait_ge(s_small, 32)
                if j == 4:
                    dve.wait_ge(s_gvo, 16)
                for k in range(2):
                    ins = dve.tensor_tensor(v[0:r, j, k * 512:k * 512 + 512].rearrange("p (g n) -> p g n", g=4),
                                            ps[2 * (j % 2) + k][0:r, :].rearrange("p (g n) -> p g n", g=4),
                                            gbias[0:r, 4 * k:4 * k + 4].unsqueeze(2).to_broadcast([r, 4, P]), ALU.add)
                ins.then_inc(s_mxe, 1)
                dve.wait_ge(s_mxe, j + 1)

            def gate(n):
                hf, j = n // NT - 2, n % NT
                r = ROWS[j]
                dve.wait_ge(s_gev, n + 1)
                vs = v[0:r, j, hf * 512:hf * 512 + 512]
                dve.tensor_tensor(vs, vs, ut[0:r, n % 2, :], ALU.mult).then_inc(s_gu, 1)
            for j in range(NT):
                mix_out(j)
                gate(2 * NT + j)
            for j in range(NT):
                gate(3 * NT + j)
            dense_out(1)
            zero_logits(1)
            norm(3)
            route(1)
            experts(1)
            norm(4)

        @block.tensor
        def _(pe):
            def turn(dst, src, k):
                return pe.transpose(dst, src, ident[0:k, 0:k])

            def norm_turn(n, j):
                r = ROWS[j]
                pe.wait_ge(s_h, NT * n + j + 1)
                if j >= 2:
                    pe.wait_ge(s_ht, NT * n + j - 1)
                for c in range(C):
                    ins = turn(ps[2 * (j % 2) + c // 4][:, (c % 4) * P:(c % 4) * P + r], hr[0:r, j % 2, c:D:C], r)
                ins.then_inc(s_tp, 1)

            pe.wait_ge(s_con, 32)
            for j in range(NT):
                norm_turn(0, j)

            def dense_ready(q):
                pe.wait_ge(s_dw[q % 2], 16 * (q // 2 + 1))

            for task in tasks:
                if task[0] == "proj":
                    _, q, j = task
                    n, r = NT * q + j, ROWS[j]
                    if j == 0:
                        dense_ready(q)
                    pe.wait_ge(s_ht, j + 1)
                    if n >= 4:
                        pe.wait_ge(s_pev, n - 3)
                    for c in range(C):
                        ins = pe.matmul(ps[4 + n % 4][0:r, 0:QC], hT[:, c, T0[j]:T0[j] + r], dw[:, q % 2, c, 0:QC],
                                        start=(c == 0), stop=(c == C - 1))
                    ins.then_inc(s_pps, 1)
                    if j == NT - 1:
                        pe.wait_ge(s_pps, n + 1)
                        pe.nop().then_inc(s_dwf, 1)
                elif task[0] == "pool":
                    m = task[1]
                    n, g = 20 + m, m // 2
                    if m == 0:
                        dense_ready(4)
                    pe.wait_ge(s_pev, n - 3)
                    for c in range(C):
                        ins = pe.matmul(ps[4 + n % 4][:, 0:HALF], dw[:, 0, c, g * P:(g + 1) * P],
                                        hT[:, c, (m % 2) * HALF:(m % 2 + 1) * HALF], start=(c == 0), stop=(c == C - 1))
                    ins.then_inc(s_pps, 1)
                    if m == 7:
                        pe.wait_ge(s_pps, n + 1)
                        pe.nop().then_inc(s_dwf, 1)
                elif task[0] == "turn":
                    i = task[1]
                    if i:
                        pe.wait_ge(s_te, i)
                    if i == 0:
                        pe.wait_ge(s_ht, NT)
                        pe.wait_ge(s_dup, 1)
                        turn(ps[0][:, 0:P], kdc[:, 0, :], P)
                        for g in range(NG):
                            turn(ps[0][:, P + 16 * g:P + 16 * g + HIST], sp15[:, g * P:(g + 1) * P], HIST)
                            ins = turn(ps[1][:, g * P:(g + 1) * P], kdc[:, 1 + g, :], P)
                    elif i < 6:
                        j = i - 1
                        r = ROWS[j]
                        pe.wait_ge(s_rope, j + 1)
                        for k in range(4):
                            turn(ps[0][:, k * P:k * P + r], R[0:r, j, OQI + k * P:OQI + (k + 1) * P], r)
                        ins = turn(ps[1][:, 0:r], kdi[0:r, j % 2, :], r)
                    else:
                        j = i - 6
                        r = ROWS[j]
                        pe.wait_ge(s_rope, NT + j + 1)
                        for k in range(4):
                            turn(ps[0][:, k * P:k * P + r], R[0:r, j, OQ + k * P:OQ + (k + 1) * P], r)
                            ins = turn(ps[1][:, k * P:k * P + r], kd[0:r, j % 2, k, :], r)
                    ins.then_inc(s_tt, 1)
                else:
                    u = task[1]
                    b, h = IDX_TILES[u // NIH], u % NIH
                    if u == 0:
                        pe.wait_ge(s_te, 6)
                    if u >= 2:
                        pe.wait_ge(s_ie, u - 1)
                    lo = 64 * (h % 2)
                    keys = kiTs if b == 4 else kiT
                    pe.matmul(ps[2 + u % 2][0:ROWS[b], 0:nkeys(b)], qiT[lo:lo + 64, h // 2, T0[b]:T0[b] + ROWS[b]],
                              keys[lo:lo + 64, 0:nkeys(b)], start=True, stop=True).then_inc(s_is, 1)

            def scores(u):
                b, h = u // NH, u % NH
                if u >= 2:
                    pe.wait_ge(s_sm, u - 1)
                else:
                    pe.wait_ge(s_ie, 4 * NIH)
                    pe.wait_ge(s_te, 11)
                lo, g = 64 * (h % 2), h // 2
                keys = kTs if b == 4 else kT
                pe.matmul(ps[2 + u % 2][0:ROWS[b], 0:nkeys(b)], qT[lo:lo + 64, g, T0[b]:T0[b] + ROWS[b]],
                          keys[lo:lo + 64, g, 0:nkeys(b)], start=True, stop=True).then_inc(s_s, 1)

            def chunks(b):
                if b == 4:
                    return [(P, vc[:, :]), (TS, R[0:TS, 4, OV:OV + 256])]
                return [(P, R[:, c, OV:OV + 256]) for c in range(b + 1)]

            def probs_turn(u):
                b = u // NH
                r = ROWS[b]
                pe.wait_ge(s_pr, u + 1)
                if u >= 2:
                    pe.wait_ge(s_pte, u - 1)
                for c, (k, _) in enumerate(chunks(b)):
                    ins = turn(ps[u % 2][0:k, c * P:c * P + r], pr[0:r, u % 2, c * P:c * P + k], r)
                ins.then_inc(s_ptp, 1)

            def values(u):
                b, h = u // NH, u % NH
                r, k2, lo = ROWS[b], u // 2, 64 * (h % 2)
                pe.wait_ge(s_pte, u + 1)
                if k2 >= 2:
                    pe.wait_ge(s_oe, k2 - 1)
                else:
                    pe.wait_ge(s_pev, NPROJ)
                ch = chunks(b)
                g = h // 2
                for c, (k, vals) in enumerate(ch):
                    ins = pe.matmul(ps[4 + k2 % 2][lo:lo + 64, 0:r], vals[:, g * HD:(g + 1) * HD],
                                    pT[0:k, u % 2, c * P:c * P + r], start=(c == 0), stop=(c == len(ch) - 1))
                ins.then_inc(s_pv, 1)

            scores(0)
            scores(1)
            for u in range(NU):
                probs_turn(u)
                if u + 2 < NU:
                    scores(u + 2)
                values(u)
            for g in range(NG):
                turn(ps[6][0:HIST, g * P:(g + 1) * P], line[:, g, XP0 + TP - HIST:XP0 + TP], P)
                ins = turn(ps[7][0:HIST, g * P:(g + 1) * P], line[:, g, LINE - HIST:LINE], P)
            ins.then_inc(s_pot, 1)
            pe.wait_ge(s_pwl, 16)
            for m in range(8):
                pe.wait_ge(s_dt, m // 2 + 1)
                if m < 2:
                    pe.wait_ge(s_poe, 1)
                else:
                    pe.wait_ge(s_ype, m - 1)
                pe.matmul(ps[6 + m % 2][:, 0:HALF], pw[:, m // 2, :], dT[:, m // 2, (m % 2) * HALF:(m % 2 + 1) * HALF],
                          start=True, stop=True).then_inc(s_yp, 1)

            def dense_out(k, ready):
                for n in range(2 * NT):
                    hf, j = n // NT, n % NT
                    q, r = 5 + 6 * k + hf, ROWS[j]
                    if j == 0:
                        dense_ready(q)
                    ready(n, j)
                    if n >= 4:
                        pe.wait_ge(s_res, 15 * k + n - 3)
                    for c in range(C):
                        ins = pe.matmul(ps[4 + n % 4][0:r, :], hT[:, c, T0[j]:T0[j] + r], dw[:, q % 2, c, :],
                                        start=(c == 0), stop=(c == C - 1))
                    ins.then_inc(s_ops, 1)
                    if j == NT - 1:
                        pe.wait_ge(s_ops, 10 * k + n + 1)
                        pe.nop().then_inc(s_dwf, 1)

            def route(l):
                n = 2 * l + 1
                pe.wait_ge(s_wr, 32 * (l + 1))
                for j in range(NT + 1):
                    if j < NT:
                        norm_turn(n, j)
                    if j:
                        i, r = j - 1, ROWS[j - 1]
                        pe.wait_ge(s_ht, NT * n + i + 1)
                        if i == 0:
                            pe.wait_ge(s_lz, l + 1)
                        for c in range(C):
                            ins = pe.matmul(ps[4][0:r, 36 * i:36 * i + 36], hT[:, c, T0[i]:T0[i] + r], wr[:, c, :],
                                            start=(c == 0), stop=(c == C - 1))
                ins.then_inc(s_lg, 1)
                pe.wait_ge(s_m, l + 1)
                pe.wait_ge(s_bf, 1)
                for j in range(NT):
                    for i in range(j + 1):
                        k, r = ROWS[i], ROWS[j]
                        w = cbf[0:k, 0, 0:r] if i == j else cbf[0:k, 1, 0:r]
                        pe.matmul(ps[5][0:r, NE * j:NE * j + NE], w, mbf[0:k, i, :], start=(i == 0), stop=(i == j))
                for i in range(NT):
                    ins = pe.matmul(ps[5][:, 160:192], cbf[0:ROWS[i], 1, :], mbf[0:ROWS[i], i, :],
                                    start=(i == 0), stop=(i == NT - 1))
                ins.then_inc(s_cnt, 1)

            def experts(l):
                def turn_rows(b):
                    for c in range(C):
                        ins = turn(ps[c // 4][:, (c % 4) * P:(c % 4 + 1) * P], xg[:, b, c:D:C], P)
                    return ins

                def up(b):
                    for c in range(C):
                        for k in range(2):
                            ins = pe.matmul(ps[2 + b][64 * k:64 * k + 64, :], xT[:, b, c, 64 * k:64 * k + 64],
                                            wgu[b][:, k, c, :], start=(c == 0), stop=(c == C - 1))
                    return ins

                def turn_hidden():
                    for c in range(2):
                        ins = turn(ps[4][:, c * P:(c + 1) * P], hh[:, c:FE:2], P)
                    return ins

                def down(b):
                    for c in range(2):
                        for hf in range(2):
                            for k in range(2):
                                ins = pe.matmul(ps[6 + hf][64 * k:64 * k + 64, :], hhT[:, b, c, 64 * k:64 * k + 64],
                                                wdn[b][:, k, c, hf * 512:hf * 512 + 512], start=(c == 0), stop=(c == 1))
                    return ins

                def turned(i, b, g, first=False):
                    pe.wait_ge(s_xg[l][b], 16 * g)
                    if not first:
                        pe.wait_ge(s_xte, i + PAIRS * l)
                    turn_rows(b).then_inc(s_xt, 1)

                def pair(i, b, g, first=False, last=False):
                    pe.wait_ge(s_wgu[l][b], 64 * g)
                    pe.wait_ge(s_xte, i + 1 + PAIRS * l)
                    if not first:
                        pe.wait_ge(s_hh, i - 1 + PAIRS * l)
                    up(b).then_inc(s_gud, 1)
                    if not (last and b == 1):
                        turned(i + 1, 1 - b, g + b)
                    pe.wait_ge(s_hh, i + 1 + PAIRS * l)
                    if not (first and b == 0):
                        pe.wait_ge(s_hte, i + PAIRS * l)
                    turn_hidden().then_inc(s_ht2, 1)
                    pe.wait_ge(s_wd[l][b], 32 * g)
                    pe.wait_ge(s_hte, i + 1 + PAIRS * l)
                    if not (first and b == 0):
                        pe.wait_ge(s_yea, i + PAIRS * l)
                        pe.wait_ge(s_yed, i + PAIRS * l)
                    down(b).then_inc(s_dd, 1)

                turned(0, 0, 1, True)
                pair(0, 0, 1, True)
                pair(1, 1, 1, True)
                with pe.Fori(1, PAIRS // 2 - 1) as r:
                    pair(2 * r, 0, r + 1)
                    pair(2 * r + 1, 1, r + 1)
                pair(PAIRS - 2, 0, PAIRS // 2)
                pair(PAIRS - 1, 1, PAIRS // 2, last=True)
                pe.wait_ge(s_ovf, l + 1)
                npairs = pe.value_load(ovf[0:1, NOV + 1:NOV + 2], min_val=0, max_val=NOV // 2)
                with pe.If(npairs > 0):
                    with pe.Fori(0, npairs) as m:
                        pe.wait_ge(o_xg[l], 16 * m + 16)
                        turn_rows(0).then_inc(o_t[l], 1)
                        pe.wait_ge(o_te[l], m + 1)
                        pe.wait_ge(o_w[l], 96 * m + 96)
                        up(0).then_inc(o_gu[l], 1)
                        pe.wait_ge(o_h[l], m + 1)
                        turn_hidden().then_inc(o_ht[l], 1)
                        pe.wait_ge(o_hte[l], m + 1)
                        down(0).then_inc(o_d[l], 1)
                with pe.Else():
                    pass

            def mixer_ready(n, j):
                if n < NT:
                    pe.wait_ge(s_oe, NKV * (j + 1))
                if n == 0:
                    pe.wait_ge(s_ype, 8)
                    pe.wait_ge(s_oe, NU // 2)
            dense_out(0, mixer_ready)
            route(0)
            experts(0)
            for j in range(NT):
                norm_turn(2, j)
            pe.wait_ge(s_gml, 48)
            pe.wait_ge(s_ht, 3 * NT)
            for g in range(8):
                ins = turn(ps[g // 4][:, (g % 4) * P:(g % 4 + 1) * P], wsr[:, g, :], P)
            ins.then_inc(s_wst, 1)

            def gm_in(n):
                q, j = 7 + n // NT, n % NT
                r = ROWS[j]
                if j == 0:
                    dense_ready(q)
                if n >= 4:
                    pe.wait_ge(s_gev, n - 3)
                for c in range(C):
                    ins = pe.matmul(ps[4 + n % 4][0:r, :], hT[:, c, T0[j]:T0[j] + r], dw[:, q % 2, c, :],
                                    start=(c == 0), stop=(c == C - 1))
                ins.then_inc(s_gps, 1)
                if j == NT - 1:
                    pe.wait_ge(s_gps, n + 1)
                    pe.nop().then_inc(s_dwf, 1)

            def mix(j):
                r = ROWS[j]
                pe.wait_ge(s_ln, j + 1)
                if j >= 2:
                    pe.wait_ge(s_mxe, j - 1)
                else:
                    pe.wait_ge(s_wsm, 1)
                for g in range(8):
                    ins = pe.matmul(ps[2 * (j % 2) + g // 4][0:r, (g % 4) * P:(g % 4 + 1) * P], wsm[0:r, g, 0:r],
                                    v[0:r, j, g * P:(g + 1) * P], start=True, stop=True)
                ins.then_inc(s_mx, 1)

            def gated_turn(j):
                r = ROWS[j]
                pe.wait_ge(s_gu, NT + j + 1)
                pe.wait_ge(s_mxe, NT)
                if j >= 2:
                    pe.wait_ge(s_gte, j - 1)
                for c in range(C):
                    ins = turn(ps[2 * (j % 2) + c // 4][:, (c % 4) * P:(c % 4) * P + r], v[0:r, j, c:D:C], r)
                ins.then_inc(s_gt, 1)
            for n in range(2 * NT):
                gm_in(n)
            for j in range(NT):
                gm_in(2 * NT + j)
                mix(j)
            gm_in(3 * NT)
            for j in range(NT):
                if j + 1 < NT:
                    gm_in(3 * NT + j + 1)
                gated_turn(j)
            dense_out(1, lambda n, j: pe.wait_ge(s_gte, j + 1) if n < NT else None)
            route(1)
            experts(1)


_INS = ["x_prompt", "x_sample", "cache_k", "cache_v", "cache_idx_k", "state_pool", "norm_mix", "norm_ffn", "norm_final",
        "par_w_in", "par_pool_w", "par_pool_scale", "par_w_out", "gm_w_in", "gm_ln_g", "gm_ln_b", "gm_ws", "gm_bs",
        "gm_w_out", "moe_router_group", "moe_router_expert", "moe_w_gate", "moe_w_up", "moe_w_down"]
_OUTS = [(1, TP, D), (1, TS, D), (1, 1, TP, NKV, HD), (1, 1, TP, NKV, HD), (1, 1, TP, HD), (1, 1, HIST, PW_),
         (1, 1, TS, NKV, HD), (1, 1, TS, NKV, HD), (1, 1, TS, HD), (1, 1, HIST, PW_), (1, 1, TS, D)]


def kernel(**inputs):
    import concourse.bacc as _bacc
    from concourse.bass_utils import run_bass_kernel_spmd as _run

    nc = _bacc.Bacc("TRN2", target_bir_lowering=False, num_devices=1)
    con, icon = constants()
    arrays, args = {}, {}
    for name in _INS + ["con", "icon"]:
        arr = np.ascontiguousarray({"con": con, "icon": icon}[name] if name in ("con", "icon") else inputs[name])
        arrays[f"in_{name}"] = arr
        args[name] = nc.dram_tensor(f"in_{name}", arr.shape, mybir.dt.from_np(arr.dtype), kind="ExternalInput").ap()
    outs = [nc.dram_tensor(f"out_{i}", shape, F32, kind="ExternalOutput").ap() for i, shape in enumerate(_OUTS)]
    build(nc, args, outs)
    r = _run(nc, [arrays], core_ids=[0])
    return tuple(r.results[0][f"out_{i}"] for i in range(len(_OUTS)))
```

```python
from contextlib import ExitStack

import numpy as np
import concourse.bass as bass
from concourse import mybir

F32 = mybir.dt.float32
BF16 = mybir.dt.bfloat16
I32 = mybir.dt.int32
U32 = mybir.dt.uint32
ALU = mybir.AluOpType
ACT = mybir.ActivationFunctionType
AX = mybir.AxisListType

P = 128
D = 1024
C = D // P
TP, TS = 512, 64
T = TP + TS
PAST = 128
ROWS = [P] * (TP // P) + [TS]
T0 = [P * j for j in range(len(ROWS))]
NT = len(ROWS)
PW_ = 512
NG = 4
HIST = 15
NH, NKV, HD = 8, 4, 64
NIH = 8
QKV = 1608
QC = QKV // 4
OQ, OK_, OV, OQI, OKI, OWI = 0, 512, 768, 1024, 1536, 1600
NE, EG, NGRP = 32, 8, 4
FE = 256
BLK = 64
PAIRS = NE * BLK // P
MAIN = NE * BLK
NOV = 18
NPB = PAIRS + NOV // 2
OOB = 1 << 15
TK_P, TK_S = 128, 48
NEG_ADM = -3.0e38
NEG_SEL = -3.4e38
NEG = -1.0e30
LINE = HIST + TP + HIST + TS
XP0, XS0 = HIST, HIST + TP + HIST
HALF = T // 2
SCALE = HD ** -0.5

CON = {}
_at = 0
for _name, _w in [("ident", P), ("cos", NT * 8), ("sin", NT * 8), ("tri", P), ("upper", P), ("ones", P),
                  ("iota", P), ("egrp", NE), ("base", NE), ("rcnt", NG * 16),
                  ("parts", 8 * NT)]:
    CON[_name] = (_at, _at + _w)
    _at += _w
NCON = _at


def constants():
    con = np.zeros((P, NCON), np.float32)

    def put(name, a):
        lo, hi = CON[name]
        con[:, lo:hi] = a

    put("ident", np.eye(P))
    half = 8
    inv = (np.float32(1.0) / (np.float32(500000.0) ** (np.arange(half, dtype=np.float32) / np.float32(half)))).astype(np.float32)
    pos = np.stack([np.arange(P) + P * j for j in range(4)] + [PAST + np.arange(P)], 1).astype(np.float32)
    ang = (pos[:, :, None] * inv[None, None, :]).astype(np.float32)
    put("cos", np.cos(ang).reshape(P, -1))
    put("sin", np.sin(ang).reshape(P, -1))
    r = np.arange(P)
    put("tri", (r[:, None] <= r[None, :]))
    put("upper", (r[:, None] < r[None, :]))
    put("ones", 1.0)
    e = np.arange(NE)
    put("iota", r)
    put("egrp", e // EG)
    put("base", e * BLK)
    put("rcnt", np.concatenate([1.0 / np.minimum(np.arange(16) + 1, 2 << g) for g in range(NG)]))
    parts = np.zeros((P, 2, NT, 2, 2), np.float32)
    for j in range(NT):
        for k in range(2):
            parts[:, 0, j, k, 0], parts[:, 1, j, k, 0] = T0[j] - OOB, r
            parts[:, 0, j, k, 1], parts[:, 1, j, k, 1] = 2 * T0[j] - OOB, 2 * r + k
    put("parts", parts.reshape(P, -1))
    return con


def build(nc, a, out):
    es = ExitStack()
    with es:
        sb = lambda name, shape, dt=F32: es.enter_context(nc.sbuf_tensor(name, shape, dt))
        sem = lambda name: es.enter_context(nc.semaphore(name))
        ps = [es.enter_context(nc.psum_tensor(f"bank{i}", [P, 512], F32)) for i in range(8)]
        dram = lambda name, shape, dt=F32: nc.dram_tensor(name, shape, dt, kind="Internal").ap()

        h_rows = [dram(f"h_rows{l}", [T, D]) for l in range(2)]
        y_rows = [dram(f"y_rows{l}", [2 * T, D]) for l in range(2)]

        x = sb("x", [P, NT, D])
        hT = sb("hT", [P, C, T])
        ring = sb("ring", [P, 24576])
        mid = sb("mid", [P, 7168])
        dw = sb("dw", [P, 2, C, 512])
        gain = sb("gain", [P, D])
        con = sb("con", [P, NCON])
        wr = sb("wr", [P, C, 4 + NE])
        cbf = sb("cbf", [P, 2, P], BF16)
        pscale = sb("pscale", [P, NG])
        gbias = sb("gbias", [P, 8])
        st = sb("st", [P, 64])
        eps = sb("eps", [P, 2])
        cell = sb("cell", [1, 6])
        tab = sb("tab", [P, NPB, 2], I32)
        m8 = sb("m8", [P, 8])
        gates = sb("gates", [P, NT, 2])
        gix = sb("gix", [P, 2, 2], I32)
        six = sb("six", [P, 2, 2], I32)
        ovf = sb("ovf", [P, NOV + 2], I32)

        def c_(name, n=None):
            lo, hi = CON[name]
            v = con[:, lo:hi]
            return v.rearrange("p (a b) -> p a b", a=n) if n else v

        ident, cos, sin = c_("ident"), c_("cos", NT), c_("sin", NT)

        at = [0]

        def cut(mem, n):
            v = mem[:, at[0]:at[0] + n]
            at[0] += n
            return v
        qiT = cut(ring, 4 * T).rearrange("p (a t) -> p a t", a=4)
        kiT = cut(ring, TP)
        kiTs = cut(ring, PAST + TS)
        rl = cut(ring, 1024).rearrange("p (a n) -> p a n", a=2)
        pool_out = rl.rearrange("p a n -> p (a n)").rearrange("p (a n) -> p a n", a=2)
        sm = cut(ring, 1024).rearrange("p (a n) -> p a n", a=2)
        pr = cut(ring, 1024).rearrange("p (a n) -> p a n", a=2)
        pT = cut(ring, 1024).rearrange("p (a n) -> p a n", a=2)
        kdc = pT.rearrange("p a n -> p (a n)")[:, 0:640].rearrange("p (a n) -> p a n", a=5)
        kd = cut(ring, 1024).rearrange("p (b a n) -> p b a n", b=2, a=4)
        at[0] = 8192
        R = cut(ring, NT * QKV).rearrange("p (j n) -> p j n", j=NT)
        qT = cut(ring, 4 * T).rearrange("p (a t) -> p a t", a=4)
        kT = cut(ring, NKV * TP).rearrange("p (a t) -> p a t", a=NKV)
        kTs = cut(ring, NKV * (PAST + TS)).rearrange("p (a t) -> p a t", a=NKV)
        index = cut(ring, NT * TP).rearrange("p (j n) -> p j n", j=NT)
        vc = cut(ring, 256)
        kic = cut(ring, 64)
        kdi = cut(ring, 256).rearrange("p (b n) -> p b n", b=2)
        assert at[0] <= 24576
        wgu = [ring[:, 12288 * b:12288 * b + 8192].rearrange("p (e c n) -> p e c n", e=2, c=C) for b in range(2)]
        wgu.append(dw)
        wdn = [ring[:, 12288 * b + 8192:12288 * b + 12288].rearrange("p (e c n) -> p e c n", e=2, c=2) for b in range(2)]
        ut = ring[:, 20480:21504].rearrange("p (b n) -> p b n", b=2)
        wsr = ring[:, 20480:21504].rearrange("p (g n) -> p g n", g=8)
        lng, lnb = ring[:, 21504:22528], ring[:, 22528:23552]
        wsm = ring[:, 23552:24576].rearrange("p (g n) -> p g n", g=8)

        hr = mid[:, 0:2048].rearrange("p (b n) -> p b n", b=2)
        junk = mid[:, 6144:7168]
        ckr = mid[:, 2048:2304]
        dT = mid[:, 0:4 * T].rearrange("p (g t) -> p g t", g=NG)
        line = mid[:, 2304:2304 + NG * LINE].rearrange("p (g t) -> p g t", g=NG)
        ta, tb = mid[:, 4728:4728 + LINE], mid[:, 4728 + LINE:4728 + 2 * LINE]
        rt = mid[:, 6144:6528].rearrange("p (a n) -> p a n", a=4)
        pw = mid[:, 6528:7040].rearrange("p (g n) -> p g n", g=NG)
        sp15 = sb("sp15", [HIST, 512])
        xg = hr
        xT = mid[:, 2048:4096].rearrange("p (b c n) -> p b c n", b=2, c=C)
        yb = mid[:, 4096:6144].rearrange("p (b n) -> p b n", b=2)
        sg, hh = mid[:, 6144:6400], mid[:, 6400:6656]
        hhT = mid[:, 6656:7168].rearrange("p (b c n) -> p b c n", b=2, c=2)
        cb = ring[:, 10240:20480].rearrange("p (j k n) -> p j k n", j=NT, k=2)
        v = mid[:, 2048:7168].rearrange("p (j n) -> p j n", j=NT)
        rq = hT[:, :, :].rearrange("p c t -> p (c t)")
        rat = [0]

        def rcut(n, k=None):
            w = rq[:, rat[0]:rat[0] + n]
            rat[0] += n
            return w.rearrange("p (j n) -> p j n", j=k) if k else w
        ls = rcut(NT * 36, NT)
        lgp = rcut(NT * 8, NT)
        mg = rcut(NT * 8, NT)
        ig = rcut(NT * 8, NT)
        igf = rcut(NT, NT)
        lem = rcut(NT * NE, NT)
        me = rcut(NT * 8, NT)
        ie = rcut(NT * 8, NT)
        ief = rcut(NT * 2, NT)
        oh = [rcut(NT * NE, NT) for _ in range(2)]
        mbf = rcut(NT * NE // 2).bitcast(BF16).rearrange("p (j n) -> p j n", j=NT)
        cnt = rcut(NE)
        cnti = rcut(NE).bitcast(I32)
        nov = rcut(NE)
        inc = rcut(NE)
        dlt = rcut(NE)
        slt = rcut(NT * NE, NT)
        slo = rcut(NT * NE, NT)
        slf = rcut(NT * 2, NT)
        gex = rcut(NT * 4, NT)
        gsm = rcut(NT * 2, NT)
        gdf = rcut(NT * 2, NT)
        ov1 = rcut(NOV * NE, NOV)
        ov2 = rcut(NOV + 2)
        ohl = rcut(NT * P).bitcast(BF16).rearrange("p (a n) -> p a n", a=2 * NT)
        ohh = rcut(2 * NT * NPB, 2 * NT)
        sval = rcut(4 * NT * NPB).bitcast(BF16).rearrange("p (h a q v) -> p h a q v", h=2, a=2 * NT, q=NPB)
        slh = rcut(2 * 2 * NT).rearrange("p (h a) -> p h a", h=2)
        slhi = rcut(2 * 2 * NT).bitcast(I32).rearrange("p (h a) -> p h a", h=2)
        assert rat[0] <= 4608

        s_con, s_small, s_xl = sem("con_loaded"), sem("small_loaded"), [sem(f"x_loaded{j}") for j in range(NT)]
        s_cache, s_gain, s_wr = sem("cache_loaded"), sem("gain_loaded"), sem("router_loaded")
        s_dw, s_dwf = [sem(f"dense_loaded{b}") for b in range(2)], sem("dense_used")
        s_pwl, s_gml = sem("pool_w_loaded"), sem("gmlp_small_loaded")
        s_ssq, s_h, s_tp, s_ht = sem("squares"), sem("rows_normed"), sem("rows_turned"), sem("hT_written")
        s_eps = sem("eps_set")
        s_rs, s_va, s_vr, s_vc = sem("rstd"), sem("v_stats"), sem("v_rstd"), sem("v_centred")
        s_hst = [sem(f"rows_stored{b}") for b in range(2)]
        s_res = sem("residual_added")
        s_pps, s_pev = sem("proj_done"), sem("proj_copied")
        s_dup, s_rope, s_tt, s_te = sem("keys_doubled"), sem("roped"), sem("heads_turned"), sem("heads_copied")
        s_is, s_ie, s_ia, s_mb = sem("index_scores"), sem("index_relu"), sem("index_added"), sem("mask_made")
        s_m0, s_pz = sem("mask0_made"), sem("line_zeroed")
        s_s, s_sm, s_nm, s_ex = sem("scores"), sem("scores_masked"), sem("neg_max"), sem("exp_done")
        s_pr, s_ptp, s_pte = sem("probs"), sem("probs_turned"), sem("probsT_copied")
        s_pv, s_oe = sem("pv_done"), sem("heads_out")
        s_pc, s_dt, s_yp, s_ype = sem("pool_chain"), sem("pool_diff"), sem("pool_y"), sem("pool_y_copied")
        s_pot, s_poe = sem("pool_state_turned"), sem("pool_state_copied")
        s_ops = sem("dense_out_done")
        s_lz, s_lg, s_m, s_cnt, s_slot = sem("logits_zeroed"), sem("logits"), sem("choices"), sem("counts"), sem("slots")
        s_dc, s_bf = sem("vector_chain"), sem("bf16_consts")
        s_ovf, s_nrm4 = sem("overflow_table"), sem("gate_exp_in")
        s_ge = sem("gate_exp")
        s_tab, s_tabc = sem("slots_inverted"), sem("slot_tab_written")
        s_kvo, s_poo, s_gvo, s_out = sem("kv_out"), sem("pool_state_out"), sem("gm_v_out"), sem("y_out")
        s_wst, s_wsm, s_gps, s_gev = sem("ws_turned"), sem("ws_masked"), sem("gm_in_done"), sem("gelu_done")
        s_ln, s_mx, s_mxe, s_gu, s_gt, s_gte = (sem("v_normed"), sem("mixed"), sem("mixed_copied"), sem("gated"),
                                               sem("gated_turned"), sem("gated_copied"))
        L2 = range(2)
        s_wgu = [[sem(f"gate_up_loaded{l}{b}") for b in range(3)] for l in L2]
        s_wd = [[sem(f"down_loaded{l}{b}") for b in range(2)] for l in L2]
        s_xg = [[sem(f"gathered{l}{b}") for b in range(2)] for l in L2]
        s_sc = [[sem(f"scattered{l}{b}") for b in range(2)] for l in L2]
        s_xt, s_xte, s_gud = sem("x_turned"), sem("xT_copied"), sem("gate_up_done")
        s_sg, s_hh, s_ht2 = sem("silu_done"), sem("hidden"), sem("hidden_turned")
        s_hte, s_dd, s_yea, s_yed = sem("hiddenT"), sem("down_done"), sem("y_by_act"), sem("y_by_dve")
        s_moe = [sem(f"moe_done{l}") for l in L2]
        s_cl = [sem(f"y_loaded{j}") for j in range(NT)]
        s_cry, o_cry = ([sem(f"{n}{l}") for l in L2] for n in ("carried", "ov_carried"))
        o_wgu, o_wd, o_xg, o_t, o_te, o_gu = ([sem(f"ov_{n}{l}") for l in L2] for n in
                                              ("gate_up_loaded", "down_loaded", "gathered", "turned", "xT", "gate_up"))
        o_sg, o_h, o_ht, o_hte, o_d, o_y, o_sc = ([sem(f"ov_{n}{l}") for l in L2] for n in
                                                  ("silu", "hidden", "hid_turned", "hiddenT", "down", "y", "scattered"))

        IDX_TILES = [1, 2, 3, 4]
        tasks = [("turn", 0)]
        tasks += [("proj", q, j) for q in (0, 1) for j in range(NT)]
        tasks += [("proj", 2, 0)] + [("turn", 1 + j) for j in range(NT)]
        idx = lambda b: [("index", (b - 1) * NIH + h) for h in range(NIH)]
        tasks += idx(1) + [("proj", 2, 1), ("proj", 2, 2)] + idx(2) + [("proj", 2, 3), ("proj", 2, 4), ("proj", 3, 0)]
        tasks += idx(3) + [("proj", 3, j) for j in range(1, NT)] + [("pool", m) for m in range(4)]
        tasks += [("turn", 6 + j) for j in range(NT)] + idx(4) + [("pool", m) for m in range(4, 8)]
        NPROJ = 28
        nkeys = lambda b: PAST + TS if b == 4 else P * (b + 1)
        NU = NT * NH

        def order(q):
            return (3 - q) * QC

        block = es.enter_context(nc.Block())

        @block.sync
        def _(sp):
            def dense(q):
                if q >= 2:
                    sp.wait_ge(s_dwf, q - 1)
                if q < 4:
                    lo = PW_ + order(q)
                    src = a["par_w_in"][0, :, lo:lo + QC].rearrange("(p c) n -> p c n", c=C)
                elif q == 4:
                    src = a["par_w_in"][0, :, 0:PW_].rearrange("(p c) n -> p c n", c=C)
                elif q < 7:
                    src = a["par_w_out"][0, :, (q - 5) * 512:(q - 4) * 512].rearrange("(c p) n -> p c n", c=C)
                elif q < 11:
                    lo = [1024, 1536, 0, 512][q - 7]
                    src = a["gm_w_in"][0, :, lo:lo + 512].rearrange("(p c) n -> p c n", c=C)
                else:
                    src = a["gm_w_out"][0, :, (q - 11) * 512:(q - 10) * 512].rearrange("(p c) n -> p c n", c=C)
                sp.dma_start(dw[:, q % 2, :, 0:src.shape[2]], src).then_inc(s_dw[q % 2], 16)

            def load_gain(n):
                src = [a["norm_mix"][0], a["norm_ffn"][0], a["norm_mix"][1], a["norm_ffn"][1], a["norm_final"]][n]
                if n:
                    sp.wait_ge(s_h, NT * n)
                sp.dma_start(gain[:, :], src.partition_broadcast(P)).then_inc(s_gain, 16)

            def load_router(l):
                if l:
                    sp.wait_ge(s_lg, 1)
                sp.dma_start(wr[:, :, 0:4], a["moe_router_group"][l].rearrange("(p c) n -> p c n", c=C)).then_inc(s_wr, 16)
                sp.dma_start(wr[:, :, 4:36], a["moe_router_expert"][l].rearrange("(p c) n -> p c n", c=C)).then_inc(s_wr, 16)

            def gate_ups(l, e0, dst, signal, ks=(0, 1)):
                for k in ks:
                    for lo, w in ((0, "moe_w_gate"), (FE, "moe_w_up")):
                        sp.dma_start(dst[:, k, :, lo:lo + FE], a[w][l, bass.ds(e0 + k, 1)]
                                     .rearrange("e (p c) n -> p (e c) n", c=C)).then_inc(signal, 16)

            def downs(l, e0, dst, signal):
                for k in range(2):
                    sp.dma_start(dst[:, k], a["moe_w_down"][l, bass.ds(e0 + k, 1)]
                                 .rearrange("e (p c) n -> p (e c) n", c=2)).then_inc(signal, 16)

            def store_rows(n, l):
                for j in range(NT):
                    sp.wait_ge(s_h, NT * n + j + 1)
                    sp.dma_start(h_rows[l][T0[j]:T0[j] + ROWS[j], :], hr[0:ROWS[j], j % 2, :]).then_inc(s_hst[j % 2], 16)

            def experts(l):
                def gu(i, b, used):
                    sp.wait_ge(s_gud, used + PAIRS * l)
                    gate_ups(l, 2 * i, wgu[b], s_wgu[l][b])

                def dn(i, b):
                    sp.wait_ge(s_dd, i - 1 + PAIRS * l)
                    downs(l, 2 * i, wdn[b], s_wd[l][b])

                gu(3, 0, 1)
                dn(2, 0)
                gu(4, 1, 2)
                dn(3, 1)
                with sp.Fori(2, PAIRS // 2 - 1) as r:
                    dn(2 * r, 0)
                    gu(2 * r + 1, 0, 2 * r)
                    dn(2 * r + 1, 1)
                    gu(2 * r + 2, 1, 2 * r + 1)
                dn(PAIRS - 2, 0)
                gu(PAIRS - 1, 0, PAIRS - 2)
                dn(PAIRS - 1, 1)
                if l == 0:
                    for q in (7, 8):
                        dense(q)
                sp.wait_ge(s_ovf, l + 1)
                npairs = sp.value_load(ovf[0:1, NOV + 1:NOV + 2], min_val=0, max_val=NOV // 2)
                with sp.If(npairs > 0):
                    with sp.Fori(0, npairs) as m:
                        sp.wait_ge(o_d[l], m + 1)
                        es_ = [sp.value_load(ovf[0:1, bass.ds(2 * m + k, 1)], min_val=0, max_val=NE - 1) for k in range(2)]
                        for k, e in enumerate(es_):
                            for lo, w in ((0, "moe_w_gate"), (FE, "moe_w_up")):
                                sp.dma_start(wgu[1][:, k, :, lo:lo + FE], a[w][l, bass.ds(e, 1)]
                                             .rearrange("e (p c) n -> p (e c) n", c=C)).then_inc(o_wgu[l], 16)
                        for k, e in enumerate(es_):
                            sp.dma_start(wdn[0][:, k], a["moe_w_down"][l, bass.ds(e, 1)]
                                         .rearrange("e (p c) n -> p (e c) n", c=2)).then_inc(o_wd[l], 16)
                with sp.Else():
                    pass

            def third_pair(l):
                for k in (1, 0):
                    sp.wait_ge(s_dwf, 6 * (l + 1) + 1 - k)
                    gate_ups(l, 4, wgu[2], s_wgu[l][2], (k,))

            def combine(l):
                sp.wait_ge(s_moe[l], 1)
                for j in range(NT):
                    sp.dma_start(cb[0:ROWS[j], j], y_rows[l][2 * T0[j]:2 * (T0[j] + ROWS[j]), :]
                                 .rearrange("(p k) n -> p k n", k=2)).then_inc(s_cl[j], 16)

            sp.dma_start(x[:, 0, :], a["x_prompt"][0, 0:P, :]).then_inc(s_xl[0], 16)
            sp.dma_start(con[:, :], a["con"]).then_inc(s_con, 16)
            load_gain(0)
            for j in range(1, 4):
                sp.dma_start(x[:, j, :], a["x_prompt"][0, P * j:P * j + P, :]).then_inc(s_xl[j], 16)
            sp.dma_start(x[0:TS, 4, :], a["x_sample"][0]).then_inc(s_xl[4], 16)
            sp.dma_start(kic, a["cache_idx_k"][0, 0]).then_inc(s_cache, 16)
            sp.dma_start(ckr, a["cache_k"][0, 0].rearrange("s h d -> s (h d)")).then_inc(s_cache, 16)
            sp.dma_start(vc, a["cache_v"][0, 0].rearrange("s h d -> s (h d)")).then_inc(s_cache, 16)
            sp.dma_start(sp15[:, :], a["state_pool"][0, 0]).then_inc(s_cache, 16)
            dense(0)
            dense(1)
            sp.dma_start(pscale[:, :], a["par_pool_scale"][0].rearrange("(g p) -> p g", p=P), allow_slow_non_contiguous=True).then_inc(s_small, 16)
            sp.dma_start(gbias[:, :], a["gm_bs"][0].rearrange("g t -> t g"), allow_slow_non_contiguous=True).then_inc(s_small, 16)
            load_router(0)
            sp.wait_ge(s_ssq, NT)
            sp.dma_start(pw[:, :, :], a["par_pool_w"][0].rearrange("g c d -> c g d")).then_inc(s_pwl, 16)
            load_gain(1)
            for q in range(2, 7):
                dense(q)
            sp.wait_ge(s_rope, 2 * NT)
            for o, lo, w in ((2, OK_, 256), (3, OV, 256), (4, OKI, 64)):
                dst = out[o][0, 0] if o == 4 else out[o][0, 0].rearrange("t h d -> t (h d)")
                sp.dma_start(dst.rearrange("(j p) n -> p j n", p=P), R[:, 0:4, lo:lo + w]).then_inc(s_kvo, 16)
                dst = out[o + 4][0, 0] if o == 4 else out[o + 4][0, 0].rearrange("t h d -> t (h d)")
                sp.dma_start(dst, R[0:TS, 4, lo:lo + w]).then_inc(s_kvo, 16)
            sp.wait_ge(s_poe, 1)
            for k in range(2):
                sp.dma_start(out[5 + 4 * k][0, 0], pool_out[0:HIST, k, :]).then_inc(s_poo, 16)
            sp.wait_ge(s_kvo, 16 * 6)
            sp.wait_ge(s_poo, 16 * 2)
            sp.wait_ge(s_pv, NU)
            for i in range(2):
                gate_ups(0, 2 * i, wgu[i], s_wgu[0][i])
                downs(0, 2 * i, wdn[i], s_wd[0][i])
            third_pair(0)
            store_rows(1, 0)
            load_gain(2)
            experts(0)
            combine(0)
            for b in range(2):
                sp.dma_start(*((lng, a["gm_ln_g"][0].partition_broadcast(P)) if b else
                               (lnb, a["gm_ln_b"][0].partition_broadcast(P)))).then_inc(s_gml, 16)
            sp.dma_start(wsr, a["gm_ws"][0].rearrange("g t s -> t g s")).then_inc(s_gml, 16)
            load_router(1)
            gate_ups(1, 0, wgu[0], s_wgu[1][0])
            sp.wait_ge(s_res, 15)
            downs(1, 0, wdn[0], s_wd[1][0])
            gate_ups(1, 2, wgu[1], s_wgu[1][1])
            load_gain(3)
            dense(9)
            dense(10)
            sp.wait_ge(s_ln, NT)
            sp.dma_start(out[10][0, 0], v[0:TS, 4, :]).then_inc(s_gvo, 16)
            dense(11)
            dense(12)
            sp.wait_ge(s_gt, NT)
            sp.wait_ge(s_gu, 2 * NT)
            downs(1, 2, wdn[1], s_wd[1][1])
            third_pair(1)
            store_rows(3, 1)
            load_gain(4)
            experts(1)
            combine(1)
            for j in range(NT):
                sp.wait_ge(s_h, 4 * NT + j + 1)
                dst = out[0][0, T0[j]:T0[j] + P, :] if j < 4 else out[1][0]
                sp.dma_start(dst, hr[0:ROWS[j], j % 2, :]).then_inc(s_hst[j % 2], 16)
            sp.wait_ge(s_hst[0], 16 * 9)
            sp.wait_ge(s_hst[1], 16 * 6)
            sp.wait_ge(s_gvo, 16)

        @block.gpsimd
        def _(pool):
            done = [0]

            def link(ins):
                done[0] += 1
                ins.then_inc(s_pc, 1)
                pool.wait_ge(s_pc, done[0])

            pool.memset(eps[:, 0:1], 1e-6).then_inc(s_eps, 1)
            pool.memset(eps[:, 1:2], 1e-5).then_inc(s_eps, 1)
            link(pool.memset(cell[:, :], 0.0))
            pool.memset(line[:, :, 0:HIST], 0.0).then_inc(s_pz, 1)
            link(pool.memset(index[:, 0, 0:P], 0.0))
            pool.memset(index[0:64, 0, 64:P], NEG).then_inc(s_m0, 1)
            pool.wait_ge(s_pev, NPROJ)
            pool.wait_ge(s_pz, 1)
            pool.wait_ge(s_te, 1)
            for g in range(NG):
                src, w = line[:, g, :], 1
                for i in range(g + 1):
                    dst = (ta, tb)[i % 2]
                    w *= 2
                    link(pool.tensor_tensor(dst[:, w - 1:LINE], src[:, w - 1:LINE], src[:, w - 1 - w // 2:LINE - w // 2], ALU.add))
                    src = dst
                dst = (ta, tb)[(g + 1) % 2]
                pool.tensor_tensor(dst[:, XP0:XP0 + 16], src[:, XP0:XP0 + 16], c_("rcnt", NG)[:, g, :], ALU.mult)
                link(pool.tensor_scalar(dst[:, XP0 + 16:LINE], src[:, XP0 + 16:LINE], 1.0 / w, None, ALU.mult))
                pool.tensor_tensor(dT[:, g, 0:TP], dst[:, XP0:XP0 + TP], line[:, g, XP0:XP0 + TP], ALU.subtract)
                link(pool.tensor_tensor(dT[:, g, TP:T], dst[:, XS0:LINE], line[:, g, XS0:LINE], ALU.subtract))
                pool.nop().then_inc(s_dt, 1)

            def carry(signal, to, before):
                pool.wait_ge(signal, before)
                pool.tensor_tensor(cell[:, to:to + 1], cell[:, 4:5], cell[:, 5:6], ALU.add).then_inc(signal, 1)

            def take_index(dst, l, i, n):
                pool.tensor_copy(dst, tab[:, bass.ds(i, 1), :].rearrange("p a v -> p (a v)")).then_inc(s_cry[l], 1)
                carry(s_cry[l], 2 * l, 2 * n + 1)

            def gather(l, i, b, n, turned=None):
                if turned is not None:
                    pool.wait_ge(s_xt, turned + PAIRS * l)
                take_index(gix[:, b, :], l, i, n)
                pool.indirect_dma_start(xg[:, b, :], None, h_rows[l], bass.IndirectOffsetOnAxis(ap=gix[:, b, 0:1], axis=0),
                                        bounds_check=T - 1, oob_is_err=False).then_inc(s_xg[l][b], 16)

            def scatter(l, i, b, n):
                pool.wait_ge(s_yea, i + 1 + PAIRS * l)
                pool.wait_ge(s_yed, i + 1 + PAIRS * l)
                take_index(six[:, b, :], l, i, n)
                pool.indirect_dma_start(y_rows[l], bass.IndirectOffsetOnAxis(ap=six[:, b, 1:2], axis=0), yb[:, b, :], None,
                                        bounds_check=2 * T - 1, oob_is_err=False).then_inc(s_sc[l][b], 16)

            for l in range(2):
                pool.wait_ge(s_tabc, l + 1)
                for b in range(2):
                    pool.wait_ge(s_hst[b], 16 * ((3 - b) * (l + 1)))
                pool.wait_ge(s_tp, NT * (2 * l + 2))
                gather(l, 0, 0, 0)
                gather(l, 1, 1, 1)

                def step(i, b):
                    gather(l, i + 2, b, 2 * i + 2, i + 1)
                    scatter(l, i, b, 2 * i + 3)

                with pool.Fori(0, PAIRS // 2 - 1) as r:
                    step(2 * r, 0)
                    step(2 * r + 1, 1)
                scatter(l, PAIRS - 2, 0, 2 * PAIRS - 2)
                scatter(l, PAIRS - 1, 1, 2 * PAIRS - 1)
                pool.wait_ge(s_ovf, l + 1)
                npairs = pool.value_load(ovf[0:1, NOV + 1:NOV + 2], min_val=0, max_val=NOV // 2)
                with pool.If(npairs > 0):
                    with pool.Fori(0, npairs) as m:
                        pool.tensor_copy(gix[:, 0, :], tab[:, bass.ds(m + PAIRS, 1), :].rearrange("p a v -> p (a v)")).then_inc(o_cry[l], 1)
                        carry(o_cry[l], 2 * l + 1, 6 * m + 1)
                        pool.indirect_dma_start(xg[:, 0, :], None, h_rows[l], bass.IndirectOffsetOnAxis(ap=gix[:, 0, 0:1], axis=0),
                                                bounds_check=T - 1, oob_is_err=False).then_inc(o_xg[l], 16)
                        pool.wait_ge(o_y[l], 2 * m + 2)
                        pool.wait_ge(s_sc[l][0], 16 * PAIRS // 2)
                        carry(o_cry[l], 2 * l + 1, 6 * m + 2)
                        pool.tensor_copy(six[:, 0, :], tab[:, bass.ds(m + PAIRS, 1), :].rearrange("p a v -> p (a v)")).then_inc(o_cry[l], 1)
                        carry(o_cry[l], 2 * l + 1, 6 * m + 4)
                        pool.indirect_dma_start(y_rows[l], bass.IndirectOffsetOnAxis(ap=six[:, 0, 1:2], axis=0), yb[:, 0, :], None,
                                                bounds_check=2 * T - 1, oob_is_err=False).then_inc(o_sc[l], 16)
                        pool.wait_ge(o_sc[l], 16 * m + 16)
                        carry(o_cry[l], 2 * l + 1, 6 * m + 5)
                with pool.Else():
                    pass
                for b in range(2):
                    pool.wait_ge(s_sc[l][b], 16 * PAIRS // 2)
                pool.nop().then_inc(s_moe[l], 1)

        @block.scalar
        def _(act):
            def copy(dst, src):
                return act.activation(dst, src, ACT.Copy)

            def norm(n):
                def square(j):
                    if n == 0:
                        act.wait_ge(s_xl[j], 16)
                    else:
                        act.wait_ge(s_res, [0, 10, 15, 25, 30][n] - NT + j + 1)
                    act.activation(junk[0:ROWS[j], :], x[0:ROWS[j], j, :], ACT.Square, scale=D ** -0.5,
                                   accum_out=st[0:ROWS[j], j:j + 1]).then_inc(s_ssq, 1)
                    act.wait_ge(s_ssq, NT * n + j + 1)
                    act.activation(st[0:ROWS[j], 5 + j:6 + j], st[0:ROWS[j], j:j + 1], ACT.Sqrt, bias=eps[0:ROWS[j], 0:1]).then_inc(s_rs, 1)

                def hT_copy(j):
                    act.wait_ge(s_tp, NT * n + j + 1)
                    for k in range(2):
                        ins = copy(hT[:, 4 * k:4 * k + 4, T0[j]:T0[j] + ROWS[j]],
                                   ps[2 * (j % 2) + k][:, :].rearrange("p (c t) -> p c t", c=4)[:, :, 0:ROWS[j]])
                    ins.then_inc(s_ht, 1)
                square(0)
                for j in range(NT):
                    if j + 1 < NT:
                        square(j + 1)
                    if n < 4:
                        hT_copy(j)

            act.wait_ge(s_eps, 2)
            norm(0)
            for task in tasks:
                if task[0] == "proj":
                    _, q, j = task
                    n = NT * q + j
                    act.wait_ge(s_pps, n + 1)
                    copy(R[0:ROWS[j], j, order(q):order(q) + QC], ps[4 + n % 4][0:ROWS[j], 0:QC]).then_inc(s_pev, 1)
                elif task[0] == "pool":
                    m = task[1]
                    g, n = m // 2, 20 + m
                    act.wait_ge(s_pps, n + 1)
                    acc = ps[4 + n % 4]
                    if m % 2 == 0:
                        copy(line[:, g, XP0:XP0 + HALF], acc[:, 0:HALF]).then_inc(s_pev, 1)
                    else:
                        copy(line[:, g, XP0 + HALF:XP0 + TP], acc[:, 0:TP - HALF])
                        copy(line[:, g, XS0:LINE], acc[:, TP - HALF:HALF]).then_inc(s_pev, 1)
                elif task[0] == "turn":
                    i = task[1]
                    act.wait_ge(s_tt, i + 1)
                    b0 = ps[0][:, :].rearrange("p (a n) -> p a n", a=4)
                    b1 = ps[1][:, :].rearrange("p (a n) -> p a n", a=4)
                    if i == 0:
                        copy(kiTs[:, 0:PAST], b0[:, 0, :])
                        copy(line[:, :, XS0 - HIST:XS0], ps[0][:, 128:192].rearrange("p (g n) -> p g n", g=4)[:, :, 0:HIST])
                        copy(kTs[:, :, 0:PAST], b1).then_inc(s_te, 1)
                    elif i < 6:
                        j = i - 1
                        copy(qiT[:, :, T0[j]:T0[j] + ROWS[j]], b0[:, :, 0:ROWS[j]])
                        dst = kiT[:, T0[j]:T0[j] + P] if j < 4 else kiTs[:, PAST:PAST + TS]
                        copy(dst, b1[:, 0, 0:ROWS[j]]).then_inc(s_te, 1)
                    else:
                        j = i - 6
                        copy(qT[:, :, T0[j]:T0[j] + ROWS[j]], b0[:, :, 0:ROWS[j]])
                        dst = kT[:, :, T0[j]:T0[j] + P] if j < 4 else kTs[:, :, PAST:PAST + TS]
                        copy(dst, b1[:, :, 0:ROWS[j]]).then_inc(s_te, 1)
                else:
                    u = task[1]
                    b = IDX_TILES[u // NIH]
                    act.wait_ge(s_is, u + 1)
                    if u >= 2:
                        act.wait_ge(s_ia, u - 1)
                    act.activation(rl[0:ROWS[b], u % 2, 0:nkeys(b)], ps[2 + u % 2][0:ROWS[b], 0:nkeys(b)],
                                   ACT.Relu).then_inc(s_ie, 1)

            def exp(u):
                b = u // NH
                n, r = nkeys(b), ROWS[b]
                act.wait_ge(s_nm, u + 1)
                if u >= 2:
                    act.wait_ge(s_ptp, u - 1)
                act.activation(pr[0:r, u % 2, 0:n], sm[0:r, u % 2, 0:n], ACT.Exp, bias=st[0:r, 10 + u % 2:11 + u % 2],
                               scale=SCALE, accum_out=st[0:r, 12 + u % 2:13 + u % 2]).then_inc(s_ex, 1)

            def probsT(u):
                b = u // NH
                act.wait_ge(s_ptp, u + 1)
                if u >= 2:
                    act.wait_ge(s_pv, u - 1)
                src, dst = (z.rearrange("p (c n) -> p c n", c=4) for z in (ps[u % 2][:, :], pT[:, u % 2, :]))
                if b < 4:
                    copy(dst[:, 0:b + 1, :], src[:, 0:b + 1, :]).then_inc(s_pte, 1)
                else:
                    copy(dst[:, 0, 0:TS], src[:, 0, 0:TS])
                    copy(dst[0:TS, 1, 0:TS], src[0:TS, 1, 0:TS]).then_inc(s_pte, 1)

            def heads(k):
                b, g = k // NKV, k % NKV
                act.wait_ge(s_pv, 2 * k + 2)
                copy(hT[:, 4 + g, T0[b]:T0[b] + ROWS[b]], ps[4 + k % 2][:, 0:ROWS[b]]).then_inc(s_oe, 1)

            exp(0)
            for u in range(NU):
                if u + 1 < NU:
                    exp(u + 1)
                probsT(u)
                if u % 2 == 0 and u:
                    heads(u // 2 - 1)
            heads(NU // 2 - 1)
            act.wait_ge(s_pot, 1)
            for k in range(2):
                ins = copy(pool_out[0:HIST, k, :], ps[6 + k][0:HIST, :])
            ins.then_inc(s_poe, 1)
            act.wait_ge(s_small, 32)
            for m in range(8):
                act.wait_ge(s_yp, m + 1)
                g = m // 2
                act.activation(hT[:, g, (m % 2) * HALF:(m % 2 + 1) * HALF], ps[6 + m % 2][:, 0:HALF], ACT.Copy,
                               scale=pscale[:, g:g + 1]).then_inc(s_ype, 1)

            def experts(l):
                act.wait_ge(s_nrm4, l + 1)
                act.activation(gex[:, :, :], ls[:, :, 0:4], ACT.Exp)
                act.activation(gsm[:, :, 1:2], gdf[:, :, 0:1], ACT.Exp).then_inc(s_ge, 1)

                def turned(i, b, first=False):
                    act.wait_ge(s_xt, i + 1 + PAIRS * l)
                    if not first:
                        act.wait_ge(s_gud, i - 1 + PAIRS * l)
                    for k in range(2):
                        ins = copy(xT[:, b, 4 * k:4 * k + 4, :], ps[k][:, :].rearrange("p (c t) -> p c t", c=4))
                    ins.then_inc(s_xte, 1)

                def rest(i, b, g, first=False, last=False):
                    act.wait_ge(s_gud, i + 1 + PAIRS * l)
                    if not (first and b == 0):
                        act.wait_ge(s_hh, i + PAIRS * l)
                    act.activation(sg, ps[2 + b][:, 0:FE], ACT.Silu).then_inc(s_sg, 1)
                    if not (last and b == 1):
                        turned(i + 1, 1 - b, first and b == 0)
                    act.wait_ge(s_dd, i + 1 + PAIRS * l)
                    if not first:
                        act.wait_ge(s_sc[l][b], 16 * g)
                    copy(yb[:, b, 512:1024], ps[7][:, :]).then_inc(s_yea, 1)

                turned(0, 0, True)
                rest(0, 0, 0, True)
                rest(1, 1, 0, True)
                with act.Fori(1, PAIRS // 2 - 1) as r:
                    rest(2 * r, 0, r)
                    rest(2 * r + 1, 1, r)
                rest(PAIRS - 2, 0, PAIRS // 2 - 1)
                rest(PAIRS - 1, 1, PAIRS // 2 - 1, last=True)
                act.wait_ge(s_ovf, l + 1)
                npairs = act.value_load(ovf[0:1, NOV + 1:NOV + 2], min_val=0, max_val=NOV // 2)
                with act.If(npairs > 0):
                    with act.Fori(0, npairs) as m:
                        act.wait_ge(o_t[l], m + 1)
                        for k in range(2):
                            ins = copy(xT[:, 0, 4 * k:4 * k + 4, :], ps[k][:, :].rearrange("p (c t) -> p c t", c=4))
                        ins.then_inc(o_te[l], 1)
                        act.wait_ge(o_gu[l], m + 1)
                        act.activation(sg, ps[2][:, 0:FE], ACT.Silu).then_inc(o_sg[l], 1)
                        act.wait_ge(o_d[l], m + 2)
                        copy(yb[:, 0, 512:1024], ps[7][:, :]).then_inc(o_y[l], 1)
                with act.Else():
                    pass

            norm(1)
            experts(0)
            norm(2)
            for n in range(2 * NT):
                j = n % NT
                act.wait_ge(s_gps, n + 1)
                act.activation(v[0:ROWS[j], j, (n // NT) * 512:(n // NT + 1) * 512], ps[4 + n % 4][0:ROWS[j], :],
                               ACT.Gelu_apprx_tanh).then_inc(s_gev, 1)

            def v_root(j):
                act.wait_ge(s_va, j + 1)
                act.activation(st[0:ROWS[j], 46 + j:47 + j], st[0:ROWS[j], 37 + 2 * j:38 + 2 * j], ACT.Sqrt,
                               bias=eps[0:ROWS[j], 1:2]).then_inc(s_vr, 1)

            def u_gelu(n):
                j = n % NT
                act.wait_ge(s_gps, n + 1)
                if n - 2 * NT >= 2:
                    act.wait_ge(s_gu, n - 2 * NT - 1)
                else:
                    act.wait_ge(s_wsm, 1)
                act.activation(ut[0:ROWS[j], n % 2, :], ps[4 + n % 4][0:ROWS[j], :], ACT.Gelu_apprx_tanh).then_inc(s_gev, 1)

            def gated(j):
                act.wait_ge(s_gt, j + 1)
                for k in range(2):
                    ins = copy(hT[:, 4 * k:4 * k + 4, T0[j]:T0[j] + ROWS[j]],
                               ps[2 * (j % 2) + k][:, :].rearrange("p (c t) -> p c t", c=4)[:, :, 0:ROWS[j]])
                ins.then_inc(s_gte, 1)
            for j in range(NT):
                v_root(j)
            for n in range(2 * NT, 3 * NT + 1):
                u_gelu(n)
            for j in range(NT):
                if j + 1 < NT:
                    u_gelu(3 * NT + j + 1)
                gated(j)
            norm(3)
            experts(1)
            norm(4)

        @block.vector
        def _(dve):
            done = [0]

            def link(ins):
                done[0] += 1
                ins.then_inc(s_dc, 1)
                dve.wait_ge(s_dc, done[0])

            def inverse_root(r, square, root, e, dst):
                link(dve.reciprocal(dst, root))
                link(dve.scalar_tensor_tensor(st[0:r, 60:61], square, e, dst, ALU.add, ALU.mult))
                link(dve.tensor_tensor(st[0:r, 60:61], st[0:r, 60:61], dst, ALU.mult))
                link(dve.tensor_scalar(st[0:r, 60:61], st[0:r, 60:61], -0.5, 1.5, ALU.mult, ALU.add))
                link(dve.tensor_tensor(dst, dst, st[0:r, 60:61], ALU.mult))

            def norm(n, first=None):
                if first:
                    first(0)
                dve.wait_ge(s_gain, 16 * (n + 1))
                for j in range(NT):
                    r = ROWS[j]
                    if first and j + 1 < NT:
                        first(j + 1)
                    dve.wait_ge(s_rs, NT * n + j + 1)
                    inverse_root(r, st[0:r, j:j + 1], st[0:r, 5 + j:6 + j], 1e-6, st[0:r, 14 + j:15 + j])
                    if j >= 2:
                        if n < 4:
                            dve.wait_ge(s_tp, NT * n + j - 1)
                        if n in (1, 3, 4):
                            before = {1: 0, 3: 1, 4: 2}[n] * (3 - j % 2) + j // 2
                            dve.wait_ge(s_hst[j % 2], 16 * before)
                    dve.scalar_tensor_tensor(hr[0:r, j % 2, :], x[0:r, j, :], st[0:r, 14 + j:15 + j], gain[0:r, :],
                                             ALU.mult, ALU.mult).then_inc(s_h, 1)

            def rope(j, lo, nh, dup, dst_n):
                r = ROWS[j]
                hv = R[0:r, j, lo:lo + nh * HD].rearrange("p (h d) -> p h d", h=nh)
                x1, x2 = hv[:, :, 0:8], hv[:, :, 8:16]
                co = cos[0:r, j, :].unsqueeze(1).to_broadcast([r, nh, 8])
                si = sin[0:r, j, :].unsqueeze(1).to_broadcast([r, nh, 8])
                t = [rt[0:r, k, 0:nh * 8].rearrange("p (h d) -> p h d", h=nh) for k in range(4)]
                dve.tensor_tensor(t[0], x1, co, ALU.mult)
                dve.tensor_tensor(t[1], x2, si, ALU.mult)
                dve.tensor_tensor(t[2], x2, co, ALU.mult)
                link(dve.tensor_tensor(t[3], x1, si, ALU.mult))
                dve.tensor_tensor(x1, t[0], t[1], ALU.subtract)
                link(dve.tensor_tensor(x2, t[2], t[3], ALU.add))
                if j >= 2:
                    dve.wait_ge(s_tt, dst_n - 1)
                dve.tensor_copy(dup[0], dup[1]).then_inc(s_rope, 1)

            dve.wait_ge(s_con, 16)
            dve.tensor_copy(cbf[:, 0, :], c_("upper"))
            dve.tensor_copy(cbf[:, 1, :], c_("ones")).then_inc(s_bf, 1)
            dve.wait_ge(s_cache, 64)
            dve.tensor_copy(kdc[:, 0, :].rearrange("p (b n) -> p b n", b=2), kic.unsqueeze(1).to_broadcast([P, 2, HD]))
            for g in range(NKV):
                ins = dve.tensor_copy(kdc[:, 1 + g, :].rearrange("p (b n) -> p b n", b=2),
                                      ckr[:, g * HD:(g + 1) * HD].unsqueeze(1).to_broadcast([P, 2, HD]))
            ins.then_inc(s_dup, 1)
            norm(0)
            for j in range(NT):
                dve.wait_ge(s_pev, NT + j + 1)
                rope(j, OQI, NIH + 1, (kdi[0:ROWS[j], j % 2, :].rearrange("p (b n) -> p b n", b=2),
                                       R[0:ROWS[j], j, OKI:OKI + HD].unsqueeze(1).to_broadcast([ROWS[j], 2, HD])), j + 1)

            def index_add(b):
                r, n = ROWS[b], nkeys(b)
                acc = index[0:r, b, 0:n]
                for h in range(NIH):
                    u = IDX_TILES.index(b) * NIH + h
                    dve.wait_ge(s_ie, u + 1)
                    wi = R[0:r, b, OWI + h:OWI + h + 1]
                    if h == 0:
                        dve.tensor_scalar(acc, rl[0:r, u % 2, 0:n], wi, None, ALU.mult).then_inc(s_ia, 1)
                    else:
                        dve.scalar_tensor_tensor(acc, rl[0:r, u % 2, 0:n], wi, acc, ALU.mult, ALU.add).then_inc(s_ia, 1)
                    dve.wait_ge(s_ia, u + 1)

            def top_k(b):
                r, n = ROWS[b], nkeys(b)
                acc = index[0:r, b, 0:n]
                if b < 4:
                    link(dve.memset(index[0:64, b, n - 64:n], NEG_ADM))
                for _ in range((TK_P if b < 4 else TK_S) // 8):
                    link(dve.max(m8[0:r, :], acc))
                    link(dve.match_replace(acc, m8[0:r, :], acc, NEG_SEL))
                dve.tensor_scalar(acc, acc, 0.5 * (NEG_SEL + NEG_ADM), NEG, ALU.is_gt, ALU.mult).then_inc(s_mb, 1)

            for b in (1, 2, 3):
                index_add(b)
                top_k(b)
            for j in range(NT):
                dve.wait_ge(s_pev, 3 * NT + j + 1)
                r = ROWS[j]
                rope(j, OQ, NH + NKV, (kd[0:r, j % 2].rearrange("p a (b n) -> p a b n", b=2),
                                       R[0:r, j, OK_:OK_ + 256].rearrange("p (a n) -> p a n", a=NKV).unsqueeze(2)
                                       .to_broadcast([r, NKV, 2, HD])), j + 6)
            index_add(4)
            top_k(4)

            def masked(u):
                b = u // NH
                r, n = ROWS[b], nkeys(b)
                dve.wait_ge(s_s, u + 1)
                if b == 0:
                    dve.wait_ge(s_m0, 1)
                else:
                    dve.wait_ge(s_mb, b)
                if u >= 2:
                    dve.wait_ge(s_ex, u - 1)
                dve.tensor_tensor_reduce(sm[0:r, u % 2, 0:n], ps[2 + u % 2][0:r, 0:n], index[0:r, b, 0:n], 1.0, -3.0e38,
                                         ALU.add, ALU.max, st[0:r, 20 + u % 2:21 + u % 2]).then_inc(s_sm, 1)
                dve.wait_ge(s_sm, u + 1)
                dve.tensor_scalar(st[0:r, 10 + u % 2:11 + u % 2], st[0:r, 20 + u % 2:21 + u % 2], -SCALE, None,
                                  ALU.mult).then_inc(s_nm, 1)

            def normed(u):
                b = u // NH
                r, n = ROWS[b], nkeys(b)
                dve.wait_ge(s_ex, u + 1)
                link(dve.reciprocal(st[0:r, 22 + u % 2:23 + u % 2], st[0:r, 12 + u % 2:13 + u % 2]))
                dve.tensor_scalar(pr[0:r, u % 2, 0:n], pr[0:r, u % 2, 0:n], st[0:r, 22 + u % 2:23 + u % 2], None,
                                  ALU.mult).then_inc(s_pr, 1)

            masked(0)
            for u in range(NU):
                if u + 1 < NU:
                    masked(u + 1)
                normed(u)

            def dense_out(k):
                for n in range(2 * NT):
                    hf, j = n // NT, n % NT
                    r = ROWS[j]
                    dve.wait_ge(s_ops, 10 * k + n + 1)
                    xs = x[0:r, j, hf * 512:hf * 512 + 512]
                    dve.tensor_tensor(xs, xs, ps[4 + n % 4][0:r, :], ALU.add).then_inc(s_res, 1)

            def route(l):
                bc = lambda name: c_(name)[:, 0:NE].unsqueeze(1).to_broadcast([P, NT, NE])
                dve.wait_ge(s_lg, l + 1)
                link(dve.memset(lgp, NEG))
                link(dve.tensor_copy(ls, ps[4][:, 0:180].rearrange("p (j n) -> p j n", j=NT)))
                link(dve.tensor_copy(lgp[:, :, 0:4], ls[:, :, 0:4]))
                for j in range(NT):
                    link(dve.max(mg[:, j, :], lgp[:, j, :]))
                    link(dve.max_index(ig[:, j, :].bitcast(U32), mg[:, j, :], lgp[:, j, :]))
                link(dve.tensor_copy(igf, ig[:, :, 0:1].bitcast(U32)))
                link(dve.tensor_tensor(lem, bc("egrp"), igf.to_broadcast([P, NT, NE]), ALU.not_equal))
                link(dve.scalar_tensor_tensor(lem, lem, NEG, ls[:, :, 4:36], ALU.mult, ALU.add))
                for j in range(NT):
                    link(dve.max(me[:, j, :], lem[:, j, :]))
                    link(dve.max_index(ie[:, j, :].bitcast(U32), me[:, j, :], lem[:, j, :]))
                link(dve.tensor_tensor(ls[:, :, 0:4], ls[:, :, 0:4], mg[:, :, 0:1].to_broadcast([P, NT, 4]), ALU.subtract))
                dve.tensor_tensor(gdf[:, :, 0:1], me[:, :, 1:2], me[:, :, 0:1], ALU.subtract).then_inc(s_nrm4, 1)
                link(dve.tensor_copy(ief, ie[:, :, 0:2].bitcast(U32)))
                for k in range(2):
                    link(dve.tensor_tensor(oh[k], bc("iota"), ief[:, :, k:k + 1].to_broadcast([P, NT, NE]), ALU.is_equal))
                dve.tensor_tensor(mbf, oh[0], oh[1], ALU.add).then_inc(s_m, 1)
                dve.wait_ge(s_cnt, l + 1)
                link(dve.tensor_scalar(cnti, ps[5][:, 160:192], float(BLK - 1), None, ALU.add))
                link(dve.tensor_scalar(cnti, cnti, 6, None, ALU.logical_shift_right))
                link(dve.tensor_scalar(nov, cnti, -1.0, 0.0, ALU.add, ALU.max))
                link(dve.tensor_tensor_scan(inc, c_("ones")[:, 0:NE], nov, 0.0, ALU.mult, ALU.add))
                link(dve.tensor_tensor(dlt, inc, nov, ALU.subtract))
                link(dve.tensor_scalar(dlt, dlt, float(BLK), float(MAIN - BLK), ALU.mult, ALU.add))
                link(dve.tensor_tensor(dlt, dlt, c_("base"), ALU.subtract))
                pp = ps[5][:, 0:160].rearrange("p (j n) -> p j n", j=NT)
                link(dve.scalar_tensor_tensor(slt, pp, float(BLK), dlt.unsqueeze(1).to_broadcast([P, NT, NE]), ALU.is_ge, ALU.mult))
                link(dve.tensor_tensor(slt, slt, pp, ALU.add))
                link(dve.tensor_tensor(slt, slt, bc("base"), ALU.add))
                for k in range(2):
                    link(dve.tensor_tensor(slo, slt, oh[k], ALU.mult))
                    link(dve.tensor_reduce(slf[:, :, k:k + 1], slo, AX.X, ALU.add))
                slot_i = slf.rearrange("p j k -> p (j k)")
                link(dve.tensor_copy(slhi[:, 0], slot_i))
                dve.tensor_scalar(slhi[:, 1], slhi[:, 0], P - 1, None, ALU.bitwise_and)
                link(dve.tensor_scalar(slhi[:, 0], slhi[:, 0], 7, None, ALU.logical_shift_right))
                link(dve.tensor_copy(slh, slhi))
                dve.tensor_tensor(ohl, c_("iota").unsqueeze(1).to_broadcast([P, 2 * NT, P]),
                                  slh[:, 1].unsqueeze(2).to_broadcast([P, 2 * NT, P]), ALU.is_equal)
                link(dve.tensor_tensor(ohh, c_("iota")[:, 0:NPB].unsqueeze(1).to_broadcast([P, 2 * NT, NPB]),
                                       slh[:, 0].unsqueeze(2).to_broadcast([P, 2 * NT, NPB]), ALU.is_equal))
                parts = c_("parts", 2).rearrange("p h (a v) -> p h a v", v=2)
                for h in range(2):
                    for k in range(2):
                        ins = dve.tensor_tensor(sval[:, h, :, :, k], ohh, parts[:, h, :, k:k + 1].to_broadcast([P, 2 * NT, NPB]), ALU.mult)
                ins.then_inc(s_slot, 1)
                dve.wait_ge(s_tab, l + 1)
                dve.tensor_scalar(tab[:, :, :], ps[5][:, 192:192 + 2 * NPB].rearrange("p (q v) -> p q v", v=2), float(OOB), None,
                                  ALU.add).then_inc(s_tabc, 1)
                link(dve.tensor_tensor(ov1, c_("iota")[:, 0:NOV].unsqueeze(2).to_broadcast([P, NOV, NE]), inc.unsqueeze(1).to_broadcast([P, NOV, NE]), ALU.is_ge))
                link(dve.tensor_reduce(ov2[:, 0:NOV].unsqueeze(2), ov1, AX.X, ALU.add))
                link(dve.tensor_scalar(ov2[:, 0:NOV], ov2[:, 0:NOV], float(NE - 1), None, ALU.min))
                link(dve.tensor_copy(ov2[:, NOV:NOV + 1], inc[:, NE - 1:NE]))
                link(dve.tensor_scalar(ov2[:, NOV + 1:NOV + 2], inc[:, NE - 1:NE], 1.0, None, ALU.add))
                link(dve.tensor_copy(ovf[:, :], ov2))
                dve.tensor_scalar(ovf[:, NOV + 1:NOV + 2], ovf[:, NOV + 1:NOV + 2], 1, None, ALU.logical_shift_right).then_inc(s_ovf, 1)
                dve.wait_ge(s_ge, l + 1)
                link(dve.tensor_reduce(gdf[:, :, 0:1], gex, AX.X, ALU.add))
                link(dve.tensor_scalar(gdf[:, :, 1:2], gsm[:, :, 1:2], 1.0, None, ALU.add))
                link(dve.tensor_tensor(gdf[:, :, 0:1], gdf[:, :, 0:1], gdf[:, :, 1:2], ALU.mult))
                link(dve.reciprocal(gates[:, :, 0:1], gdf[:, :, 0:1]))
                link(dve.tensor_tensor(gates[:, :, 1:2], gates[:, :, 0:1], gsm[:, :, 1:2], ALU.mult))

            def experts(l):
                def pair(i, b, g, first=False):
                    dve.wait_ge(s_sg, i + 1 + PAIRS * l)
                    if not (first and b == 0):
                        dve.wait_ge(s_ht2, i + PAIRS * l)
                    dve.tensor_tensor(hh, sg, ps[2 + b][:, FE:2 * FE], ALU.mult).then_inc(s_hh, 1)
                    dve.wait_ge(s_ht2, i + 1 + PAIRS * l)
                    if not first:
                        dve.wait_ge(s_dd, i - 1 + PAIRS * l)
                    dve.tensor_copy(hhT[:, b], ps[4][:, 0:256].rearrange("p (c n) -> p c n", c=2)).then_inc(s_hte, 1)
                    dve.wait_ge(s_dd, i + 1 + PAIRS * l)
                    if not first:
                        dve.wait_ge(s_sc[l][b], 16 * g)
                    dve.tensor_copy(yb[:, b, 0:512], ps[6][:, :]).then_inc(s_yed, 1)
                pair(0, 0, 0, True)
                pair(1, 1, 0, True)
                with dve.Fori(1, PAIRS // 2) as r:
                    pair(2 * r, 0, r)
                    pair(2 * r + 1, 1, r)
                dve.wait_ge(s_ovf, l + 1)
                npairs = dve.value_load(ovf[0:1, NOV + 1:NOV + 2], min_val=0, max_val=NOV // 2)
                with dve.If(npairs > 0):
                    with dve.Fori(0, npairs) as m:
                        dve.wait_ge(o_sg[l], m + 1)
                        dve.tensor_tensor(hh, sg, ps[2][:, FE:2 * FE], ALU.mult).then_inc(o_h[l], 1)
                        dve.wait_ge(o_ht[l], m + 1)
                        dve.tensor_copy(hhT[:, 0], ps[4][:, 0:256].rearrange("p (c n) -> p c n", c=2)).then_inc(o_hte[l], 1)
                        dve.wait_ge(o_d[l], m + 2)
                        dve.tensor_copy(yb[:, 0, 0:512], ps[6][:, :]).then_inc(o_y[l], 1)
                with dve.Else():
                    pass

            def combine(l, j):
                r = ROWS[j]
                dve.wait_ge(s_cl[j], 16 * (l + 1))
                link(dve.scalar_tensor_tensor(x[0:r, j, :], cb[0:r, j, 0, :], gates[0:r, j, 0:1], x[0:r, j, :],
                                              ALU.mult, ALU.add))
                dve.scalar_tensor_tensor(x[0:r, j, :], cb[0:r, j, 1, :], gates[0:r, j, 1:2], x[0:r, j, :],
                                         ALU.mult, ALU.add).then_inc(s_res, 1)

            def zero_logits(l):
                dve.wait_ge(s_res, 15 * l + 10)
                dve.memset(ps[4][64:P, 144:180], 0.0).then_inc(s_lz, 1)

            dense_out(0)
            zero_logits(0)
            norm(1)
            route(0)
            experts(0)
            norm(2, lambda j: combine(0, j))
            dve.wait_ge(s_wst, 1)
            for k in range(2):
                ins = dve.tensor_tensor(wsm[:, 4 * k:4 * k + 4, :], ps[k][:, :].rearrange("p (g n) -> p g n", g=4),
                                        c_("tri").unsqueeze(1).to_broadcast([P, 4, P]), ALU.mult)
            ins.then_inc(s_wsm, 1)
            dve.wait_ge(s_gml, 48)
            for j in range(NT):
                r = ROWS[j]
                dve.wait_ge(s_gev, NT + j + 1)
                for k in range(2):
                    ins = dve.bn_stats(st[0:r, 24 + 6 * k:30 + 6 * k], v[0:r, j, k * 512:k * 512 + 512])
                link(ins)
                dve.bn_aggr(st[0:r, 36 + 2 * j:38 + 2 * j], st[0:r, 24:36]).then_inc(s_va, 1)
                dve.wait_ge(s_va, j + 1)
                dve.scalar_tensor_tensor(v[0:r, j, :], v[0:r, j, :], st[0:r, 36 + 2 * j:37 + 2 * j], lng[0:r, :], ALU.subtract, ALU.mult).then_inc(s_vc, 1)
                dve.wait_ge(s_vc, j + 1)
                dve.wait_ge(s_vr, j + 1)
                inverse_root(r, st[0:r, 37 + 2 * j:38 + 2 * j], st[0:r, 46 + j:47 + j], 1e-5, st[0:r, 51 + j:52 + j])
                dve.scalar_tensor_tensor(v[0:r, j, :], v[0:r, j, :], st[0:r, 51 + j:52 + j], lnb[0:r, :], ALU.mult, ALU.add).then_inc(s_ln, 1)

            def mix_out(j):
                r = ROWS[j]
                dve.wait_ge(s_mx, j + 1)
                if j == 0:
                    dve.wait_ge(s_small, 32)
                if j == 4:
                    dve.wait_ge(s_gvo, 16)
                for k in range(2):
                    ins = dve.tensor_tensor(v[0:r, j, k * 512:k * 512 + 512].rearrange("p (g n) -> p g n", g=4),
                                            ps[2 * (j % 2) + k][0:r, :].rearrange("p (g n) -> p g n", g=4),
                                            gbias[0:r, 4 * k:4 * k + 4].unsqueeze(2).to_broadcast([r, 4, P]), ALU.add)
                ins.then_inc(s_mxe, 1)
                dve.wait_ge(s_mxe, j + 1)

            def gate(n):
                hf, j = n // NT - 2, n % NT
                r = ROWS[j]
                dve.wait_ge(s_gev, n + 1)
                vs = v[0:r, j, hf * 512:hf * 512 + 512]
                dve.tensor_tensor(vs, vs, ut[0:r, n % 2, :], ALU.mult).then_inc(s_gu, 1)
            for j in range(NT):
                mix_out(j)
                gate(2 * NT + j)
            for j in range(NT):
                gate(3 * NT + j)
            dense_out(1)
            zero_logits(1)
            norm(3)
            route(1)
            experts(1)
            norm(4, lambda j: combine(1, j))

        @block.tensor
        def _(pe):
            def turn(dst, src, k):
                return pe.transpose(dst, src, ident[0:k, 0:k])

            def norm_turn(n, j):
                r = ROWS[j]
                pe.wait_ge(s_h, NT * n + j + 1)
                if j >= 2:
                    pe.wait_ge(s_ht, NT * n + j - 1)
                for c in range(C):
                    ins = turn(ps[2 * (j % 2) + c // 4][:, (c % 4) * P:(c % 4) * P + r], hr[0:r, j % 2, c:D:C], r)
                ins.then_inc(s_tp, 1)

            pe.wait_ge(s_con, 16)
            for j in range(NT):
                norm_turn(0, j)

            def dense_ready(q):
                pe.wait_ge(s_dw[q % 2], 16 * (q // 2 + 1))

            for task in tasks:
                if task[0] == "proj":
                    _, q, j = task
                    n, r = NT * q + j, ROWS[j]
                    if j == 0:
                        dense_ready(q)
                    pe.wait_ge(s_ht, j + 1)
                    if n >= 4:
                        pe.wait_ge(s_pev, n - 3)
                    for c in range(C):
                        ins = pe.matmul(ps[4 + n % 4][0:r, 0:QC], hT[:, c, T0[j]:T0[j] + r], dw[:, q % 2, c, 0:QC],
                                        start=(c == 0), stop=(c == C - 1))
                    ins.then_inc(s_pps, 1)
                    if j == NT - 1:
                        pe.wait_ge(s_pps, n + 1)
                        pe.nop().then_inc(s_dwf, 1)
                elif task[0] == "pool":
                    m = task[1]
                    n, g = 20 + m, m // 2
                    if m == 0:
                        dense_ready(4)
                    pe.wait_ge(s_pev, n - 3)
                    for c in range(C):
                        ins = pe.matmul(ps[4 + n % 4][:, 0:HALF], dw[:, 0, c, g * P:(g + 1) * P],
                                        hT[:, c, (m % 2) * HALF:(m % 2 + 1) * HALF], start=(c == 0), stop=(c == C - 1))
                    ins.then_inc(s_pps, 1)
                    if m == 7:
                        pe.wait_ge(s_pps, n + 1)
                        pe.nop().then_inc(s_dwf, 1)
                elif task[0] == "turn":
                    i = task[1]
                    if i:
                        pe.wait_ge(s_te, i)
                    if i == 0:
                        pe.wait_ge(s_ht, NT)
                        pe.wait_ge(s_dup, 1)
                        turn(ps[0][:, 0:P], kdc[:, 0, :], P)
                        for g in range(NG):
                            turn(ps[0][:, P + 16 * g:P + 16 * g + HIST], sp15[:, g * P:(g + 1) * P], HIST)
                            ins = turn(ps[1][:, g * P:(g + 1) * P], kdc[:, 1 + g, :], P)
                    elif i < 6:
                        j = i - 1
                        r = ROWS[j]
                        pe.wait_ge(s_rope, j + 1)
                        for k in range(4):
                            turn(ps[0][:, k * P:k * P + r], R[0:r, j, OQI + k * P:OQI + (k + 1) * P], r)
                        ins = turn(ps[1][:, 0:r], kdi[0:r, j % 2, :], r)
                    else:
                        j = i - 6
                        r = ROWS[j]
                        pe.wait_ge(s_rope, NT + j + 1)
                        for k in range(4):
                            turn(ps[0][:, k * P:k * P + r], R[0:r, j, OQ + k * P:OQ + (k + 1) * P], r)
                            ins = turn(ps[1][:, k * P:k * P + r], kd[0:r, j % 2, k, :], r)
                    ins.then_inc(s_tt, 1)
                else:
                    u = task[1]
                    b, h = IDX_TILES[u // NIH], u % NIH
                    if u == 0:
                        pe.wait_ge(s_te, 6)
                    if u >= 2:
                        pe.wait_ge(s_ie, u - 1)
                    lo = 64 * (h % 2)
                    keys = kiTs if b == 4 else kiT
                    pe.matmul(ps[2 + u % 2][0:ROWS[b], 0:nkeys(b)], qiT[lo:lo + 64, h // 2, T0[b]:T0[b] + ROWS[b]],
                              keys[lo:lo + 64, 0:nkeys(b)], start=True, stop=True).then_inc(s_is, 1)

            def scores(u):
                b, h = u // NH, u % NH
                if u >= 2:
                    pe.wait_ge(s_sm, u - 1)
                else:
                    pe.wait_ge(s_ie, 4 * NIH)
                    pe.wait_ge(s_te, 11)
                lo, g = 64 * (h % 2), h // 2
                keys = kTs if b == 4 else kT
                pe.matmul(ps[2 + u % 2][0:ROWS[b], 0:nkeys(b)], qT[lo:lo + 64, g, T0[b]:T0[b] + ROWS[b]],
                          keys[lo:lo + 64, g, 0:nkeys(b)], start=True, stop=True).then_inc(s_s, 1)

            def chunks(b):
                if b == 4:
                    return [(P, vc[:, :]), (TS, R[0:TS, 4, OV:OV + 256])]
                return [(P, R[:, c, OV:OV + 256]) for c in range(b + 1)]

            def probs_turn(u):
                b = u // NH
                r = ROWS[b]
                pe.wait_ge(s_pr, u + 1)
                if u >= 2:
                    pe.wait_ge(s_pte, u - 1)
                for c, (k, _) in enumerate(chunks(b)):
                    ins = turn(ps[u % 2][0:k, c * P:c * P + r], pr[0:r, u % 2, c * P:c * P + k], r)
                ins.then_inc(s_ptp, 1)

            def values(u):
                b, h = u // NH, u % NH
                r, k2, lo = ROWS[b], u // 2, 64 * (h % 2)
                pe.wait_ge(s_pte, u + 1)
                if k2 >= 2:
                    pe.wait_ge(s_oe, k2 - 1)
                else:
                    pe.wait_ge(s_pev, NPROJ)
                ch = chunks(b)
                g = h // 2
                for c, (k, vals) in enumerate(ch):
                    ins = pe.matmul(ps[4 + k2 % 2][lo:lo + 64, 0:r], vals[:, g * HD:(g + 1) * HD],
                                    pT[0:k, u % 2, c * P:c * P + r], start=(c == 0), stop=(c == len(ch) - 1))
                ins.then_inc(s_pv, 1)

            scores(0)
            scores(1)
            for u in range(NU):
                probs_turn(u)
                if u + 2 < NU:
                    scores(u + 2)
                values(u)
            for g in range(NG):
                turn(ps[6][0:HIST, g * P:(g + 1) * P], line[:, g, XP0 + TP - HIST:XP0 + TP], P)
                ins = turn(ps[7][0:HIST, g * P:(g + 1) * P], line[:, g, LINE - HIST:LINE], P)
            ins.then_inc(s_pot, 1)
            pe.wait_ge(s_pwl, 16)
            for m in range(8):
                pe.wait_ge(s_dt, m // 2 + 1)
                if m < 2:
                    pe.wait_ge(s_poe, 1)
                else:
                    pe.wait_ge(s_ype, m - 1)
                pe.matmul(ps[6 + m % 2][:, 0:HALF], pw[:, m // 2, :], dT[:, m // 2, (m % 2) * HALF:(m % 2 + 1) * HALF],
                          start=True, stop=True).then_inc(s_yp, 1)

            def dense_out(k, ready):
                for n in range(2 * NT):
                    hf, j = n // NT, n % NT
                    q, r = 5 + 6 * k + hf, ROWS[j]
                    if j == 0:
                        dense_ready(q)
                    ready(n, j)
                    if n >= 4:
                        pe.wait_ge(s_res, 15 * k + n - 3)
                    for c in range(C):
                        ins = pe.matmul(ps[4 + n % 4][0:r, :], hT[:, c, T0[j]:T0[j] + r], dw[:, q % 2, c, :],
                                        start=(c == 0), stop=(c == C - 1))
                    ins.then_inc(s_ops, 1)
                    if j == NT - 1:
                        pe.wait_ge(s_ops, 10 * k + n + 1)
                        pe.nop().then_inc(s_dwf, 1)

            def route(l):
                n = 2 * l + 1
                pe.wait_ge(s_wr, 32 * (l + 1))
                for j in range(NT + 1):
                    if j < NT:
                        norm_turn(n, j)
                    if j:
                        i, r = j - 1, ROWS[j - 1]
                        pe.wait_ge(s_ht, NT * n + i + 1)
                        if i == 0:
                            pe.wait_ge(s_lz, l + 1)
                        for c in range(C):
                            ins = pe.matmul(ps[4][0:r, 36 * i:36 * i + 36], hT[:, c, T0[i]:T0[i] + r], wr[:, c, :],
                                            start=(c == 0), stop=(c == C - 1))
                ins.then_inc(s_lg, 1)
                pe.wait_ge(s_m, l + 1)
                pe.wait_ge(s_bf, 1)
                for j in range(NT):
                    for i in range(j + 1):
                        k, r = ROWS[i], ROWS[j]
                        w = cbf[0:k, 0, 0:r] if i == j else cbf[0:k, 1, 0:r]
                        pe.matmul(ps[5][0:r, NE * j:NE * j + NE], w, mbf[0:k, i, :], start=(i == 0), stop=(i == j))
                for i in range(NT):
                    ins = pe.matmul(ps[5][:, 160:192], cbf[0:ROWS[i], 1, :], mbf[0:ROWS[i], i, :],
                                    start=(i == 0), stop=(i == NT - 1))
                ins.then_inc(s_cnt, 1)
                pe.wait_ge(s_slot, l + 1)
                for i in range(2 * NT):
                    for h in range(2):
                        r = ROWS[i // 2]
                        ins = pe.matmul(ps[5][:, 192:192 + 2 * NPB], ohl[0:r, i, :], sval[0:r, h, i].rearrange("p q v -> p (q v)"),
                                        start=(i == 0 and h == 0), stop=(i == 2 * NT - 1 and h == 1))
                ins.then_inc(s_tab, 1)

            def experts(l):
                def turn_rows(b):
                    for c in range(C):
                        ins = turn(ps[c // 4][:, (c % 4) * P:(c % 4 + 1) * P], xg[:, b, c:D:C], P)
                    return ins

                def up(b, w):
                    for c in range(C):
                        for k in range(2):
                            ins = pe.matmul(ps[2 + b][64 * k:64 * k + 64, :], xT[:, b, c, 64 * k:64 * k + 64],
                                            w[:, k, c, :], start=(c == 0), stop=(c == C - 1))
                    return ins

                def turn_hidden():
                    for c in range(2):
                        ins = turn(ps[4][:, c * P:(c + 1) * P], hh[:, c:FE:2], P)
                    return ins

                def down(b):
                    for c in range(2):
                        for hf in range(2):
                            for k in range(2):
                                ins = pe.matmul(ps[6 + hf][64 * k:64 * k + 64, :], hhT[:, b, c, 64 * k:64 * k + 64],
                                                wdn[b][:, k, c, hf * 512:hf * 512 + 512], start=(c == 0), stop=(c == 1))
                    return ins

                def turned(i, b, g, first=False):
                    pe.wait_ge(s_xg[l][b], 16 * g)
                    if not first:
                        pe.wait_ge(s_xte, i + PAIRS * l)
                    turn_rows(b).then_inc(s_xt, 1)

                def pair(i, b, g, w, gw, first=False, last=False):
                    pe.wait_ge(s_wgu[l][w], 64 * gw)
                    pe.wait_ge(s_xte, i + 1 + PAIRS * l)
                    if not first:
                        pe.wait_ge(s_hh, i - 1 + PAIRS * l)
                    up(b, wgu[w]).then_inc(s_gud, 1)
                    if not (last and b == 1):
                        turned(i + 1, 1 - b, g + b)
                    pe.wait_ge(s_hh, i + 1 + PAIRS * l)
                    if not (first and b == 0):
                        pe.wait_ge(s_hte, i + PAIRS * l)
                    turn_hidden().then_inc(s_ht2, 1)
                    pe.wait_ge(s_wd[l][b], 32 * g)
                    pe.wait_ge(s_hte, i + 1 + PAIRS * l)
                    if not (first and b == 0):
                        pe.wait_ge(s_yea, i + PAIRS * l)
                        pe.wait_ge(s_yed, i + PAIRS * l)
                    down(b).then_inc(s_dd, 1)

                turned(0, 0, 1, True)
                pair(0, 0, 1, 0, 1, first=True)
                pair(1, 1, 1, 1, 1, first=True)
                pair(2, 0, 2, 2, 1)
                pair(3, 1, 2, 0, 2)
                with pe.Fori(2, PAIRS // 2 - 1) as r:
                    pair(2 * r, 0, r + 1, 1, r)
                    pair(2 * r + 1, 1, r + 1, 0, r + 1)
                pair(PAIRS - 2, 0, PAIRS // 2, 1, PAIRS // 2 - 1)
                pe.wait_ge(s_dd, PAIRS - 1 + PAIRS * l)
                pe.nop().then_inc(o_d[l], 1)
                pair(PAIRS - 1, 1, PAIRS // 2, 0, PAIRS // 2, last=True)
                pe.wait_ge(s_ovf, l + 1)
                npairs = pe.value_load(ovf[0:1, NOV + 1:NOV + 2], min_val=0, max_val=NOV // 2)
                with pe.If(npairs > 0):
                    with pe.Fori(0, npairs) as m:
                        pe.wait_ge(o_xg[l], 16 * m + 16)
                        turn_rows(0).then_inc(o_t[l], 1)
                        pe.wait_ge(o_te[l], m + 1)
                        pe.wait_ge(o_wgu[l], 64 * m + 64)
                        up(0, wgu[1]).then_inc(o_gu[l], 1)
                        pe.wait_ge(o_h[l], m + 1)
                        turn_hidden().then_inc(o_ht[l], 1)
                        pe.wait_ge(o_hte[l], m + 1)
                        pe.wait_ge(o_wd[l], 32 * m + 32)
                        down(0).then_inc(o_d[l], 1)
                with pe.Else():
                    pass

            def mixer_ready(n, j):
                if n < NT:
                    pe.wait_ge(s_oe, NKV * (j + 1))
                if n == 0:
                    pe.wait_ge(s_ype, 8)
                    pe.wait_ge(s_oe, NU // 2)
            dense_out(0, mixer_ready)
            route(0)
            experts(0)
            for j in range(NT):
                norm_turn(2, j)
            pe.wait_ge(s_gml, 48)
            pe.wait_ge(s_ht, 3 * NT)
            for g in range(8):
                ins = turn(ps[g // 4][:, (g % 4) * P:(g % 4 + 1) * P], wsr[:, g, :], P)
            ins.then_inc(s_wst, 1)

            def gm_in(n):
                q, j = 7 + n // NT, n % NT
                r = ROWS[j]
                if j == 0:
                    dense_ready(q)
                if n >= 4:
                    pe.wait_ge(s_gev, n - 3)
                for c in range(C):
                    ins = pe.matmul(ps[4 + n % 4][0:r, :], hT[:, c, T0[j]:T0[j] + r], dw[:, q % 2, c, :],
                                    start=(c == 0), stop=(c == C - 1))
                ins.then_inc(s_gps, 1)
                if j == NT - 1:
                    pe.wait_ge(s_gps, n + 1)
                    pe.nop().then_inc(s_dwf, 1)

            def mix(j):
                r = ROWS[j]
                pe.wait_ge(s_ln, j + 1)
                if j >= 2:
                    pe.wait_ge(s_mxe, j - 1)
                else:
                    pe.wait_ge(s_wsm, 1)
                for g in range(8):
                    ins = pe.matmul(ps[2 * (j % 2) + g // 4][0:r, (g % 4) * P:(g % 4 + 1) * P], wsm[0:r, g, 0:r],
                                    v[0:r, j, g * P:(g + 1) * P], start=True, stop=True)
                ins.then_inc(s_mx, 1)

            def gated_turn(j):
                r = ROWS[j]
                pe.wait_ge(s_gu, NT + j + 1)
                pe.wait_ge(s_mxe, NT)
                if j >= 2:
                    pe.wait_ge(s_gte, j - 1)
                for c in range(C):
                    ins = turn(ps[2 * (j % 2) + c // 4][:, (c % 4) * P:(c % 4) * P + r], v[0:r, j, c:D:C], r)
                ins.then_inc(s_gt, 1)
            for n in range(2 * NT):
                gm_in(n)
            for j in range(NT):
                gm_in(2 * NT + j)
                mix(j)
            gm_in(3 * NT)
            for j in range(NT):
                if j + 1 < NT:
                    gm_in(3 * NT + j + 1)
                gated_turn(j)
            dense_out(1, lambda n, j: pe.wait_ge(s_gte, j + 1) if n < NT else None)
            route(1)
            experts(1)


_INS = ["x_prompt", "x_sample", "cache_k", "cache_v", "cache_idx_k", "state_pool", "norm_mix", "norm_ffn", "norm_final",
        "par_w_in", "par_pool_w", "par_pool_scale", "par_w_out", "gm_w_in", "gm_ln_g", "gm_ln_b", "gm_ws", "gm_bs",
        "gm_w_out", "moe_router_group", "moe_router_expert", "moe_w_gate", "moe_w_up", "moe_w_down"]
_OUTS = [(1, TP, D), (1, TS, D), (1, 1, TP, NKV, HD), (1, 1, TP, NKV, HD), (1, 1, TP, HD), (1, 1, HIST, PW_),
         (1, 1, TS, NKV, HD), (1, 1, TS, NKV, HD), (1, 1, TS, HD), (1, 1, HIST, PW_), (1, 1, TS, D)]


def kernel(**inputs):
    import concourse.bacc as _bacc
    from concourse.bass_utils import run_bass_kernel_spmd as _run

    nc = _bacc.Bacc("TRN2", target_bir_lowering=False, num_devices=1)
    con = constants()
    arrays, args = {}, {}
    for name in _INS + ["con"]:
        arr = np.ascontiguousarray(con if name == "con" else inputs[name])
        arrays[f"in_{name}"] = arr
        args[name] = nc.dram_tensor(f"in_{name}", arr.shape, mybir.dt.from_np(arr.dtype), kind="ExternalInput").ap()
    outs = [nc.dram_tensor(f"out_{i}", shape, F32, kind="ExternalOutput").ap() for i, shape in enumerate(_OUTS)]
    build(nc, args, outs)
    r = _run(nc, [arrays], core_ids=[0])
    return tuple(r.results[0][f"out_{i}"] for i in range(len(_OUTS)))
```

```python
from contextlib import ExitStack

import numpy as np
import concourse.bass as bass
from concourse import mybir

F32 = mybir.dt.float32
F32R = mybir.dt.float32r
BF16 = mybir.dt.bfloat16
I32 = mybir.dt.int32
U32 = mybir.dt.uint32
ALU = mybir.AluOpType
ACT = mybir.ActivationFunctionType
AX = mybir.AxisListType

P = 128
D = 1024
C = D // P
TP, TS = 512, 64
T = TP + TS
PAST = 128
ROWS = [P] * (TP // P) + [TS]
T0 = [P * j for j in range(len(ROWS))]
NT = len(ROWS)
PW_ = 512
NG = 4
HIST = 15
NH, NKV, HD = 8, 4, 64
NIH = 8
QKV = 1608
QC = QKV // 4
OQ, OK_, OV, OQI, OKI, OWI = 0, 512, 768, 1024, 1536, 1600
NE, EG, NGRP = 32, 8, 4
FE = 256
BLK = 64
PAIRS = NE * BLK // P
MAIN = NE * BLK
NOV = 18
NPB = PAIRS + NOV // 2 + 1
OOB = 1 << 15
TK_P, TK_S = 128, 48
NEG_ADM = -3.0e38
NEG_SEL = -3.4e38
NEG = -1.0e30
LINE = HIST + TP + HIST + TS
XP0, XS0 = HIST, HIST + TP + HIST
HALF = T // 2
SCALE = HD ** -0.5

CON = {}
_at = 0
for _name, _w in [("ident", P), ("cos", NT * 8), ("sin", NT * 8), ("tri", P), ("upper", P), ("ones", P),
                  ("iota", P), ("egrp", NE), ("base", NE), ("rcnt", NG * 16),
                  ("parts", 8 * NT)]:
    CON[_name] = (_at, _at + _w)
    _at += _w
NCON = _at


def constants():
    con = np.zeros((P, NCON), np.float32)

    def put(name, a):
        lo, hi = CON[name]
        con[:, lo:hi] = a

    put("ident", np.eye(P))
    half = 8
    inv = (np.float32(1.0) / (np.float32(500000.0) ** (np.arange(half, dtype=np.float32) / np.float32(half)))).astype(np.float32)
    pos = np.stack([np.arange(P) + P * j for j in range(4)] + [PAST + np.arange(P)], 1).astype(np.float32)
    ang = (pos[:, :, None] * inv[None, None, :]).astype(np.float32)
    put("cos", np.cos(ang).reshape(P, -1))
    put("sin", np.sin(ang).reshape(P, -1))
    r = np.arange(P)
    put("tri", (r[:, None] <= r[None, :]))
    put("upper", (r[:, None] < r[None, :]))
    put("ones", 1.0)
    e = np.arange(NE)
    put("iota", r)
    put("egrp", e // EG)
    put("base", e * BLK)
    put("rcnt", np.concatenate([1.0 / np.minimum(np.arange(16) + 1, 2 << g) for g in range(NG)]))
    parts = np.zeros((P, 2, NT, 2, 2), np.float32)
    for j in range(NT):
        for k in range(2):
            parts[:, 0, j, k, 0], parts[:, 1, j, k, 0] = T0[j] - OOB, r
            parts[:, 0, j, k, 1], parts[:, 1, j, k, 1] = 2 * T0[j] - OOB, 2 * r + k
    put("parts", parts.reshape(P, -1))
    return con


def build(nc, a, out):
    es = ExitStack()
    with es:
        sb = lambda name, shape, dt=F32: es.enter_context(nc.sbuf_tensor(name, shape, dt))
        sem = lambda name: es.enter_context(nc.semaphore(name))
        ps = [es.enter_context(nc.psum_tensor(f"bank{i}", [P, 512], F32)) for i in range(8)]
        dram = lambda name, shape, dt=F32: nc.dram_tensor(name, shape, dt, kind="Internal").ap()

        h_rows = [dram(f"h_rows{l}", [T, D]) for l in range(2)]
        y_rows = [dram(f"y_rows{l}", [2 * T, D]) for l in range(2)]

        x = sb("x", [P, NT, D])
        place = lambda: -(-nc.sbuf_base // 32) * 32
        hT_at = place()
        hT = sb("hT", [P, C, T])
        ring_at = place()
        ring = sb("ring", [P, 24576])
        mid = sb("mid", [P, 7168])
        dw_at = place()
        dw = sb("dw", [P, 2, C, 512])
        gain = sb("gain", [P, D])
        con = sb("con", [P, NCON])
        wr = sb("wr", [P, C, 4 + NE])
        cbf = sb("cbf", [P, 2, P], BF16)
        pscale = sb("pscale", [P, NG])
        gbias = sb("gbias", [P, 8])
        st = sb("st", [P, 64])
        eps = sb("eps", [P, 2])
        cell = sb("cell", [1, 6])
        tab = sb("tab", [P, NPB, 2], I32)
        m8 = sb("m8", [P, 8])
        gates = sb("gates", [P, NT, 2])
        gix = sb("gix", [P, 2, 2], I32)
        six = sb("six", [P, 2, 2], I32)
        ovf = sb("ovf", [P, NOV + 2], I32)

        def c_(name, n=None):
            lo, hi = CON[name]
            v = con[:, lo:hi]
            return v.rearrange("p (a b) -> p a b", a=n) if n else v

        ident, cos, sin = c_("ident"), c_("cos", NT), c_("sin", NT)

        at = [0]

        def cut(mem, n):
            v = mem[:, at[0]:at[0] + n]
            at[0] += n
            return v
        qiT = cut(ring, 4 * T).rearrange("p (a t) -> p a t", a=4)
        kiT = cut(ring, TP)
        kiTs = cut(ring, PAST + TS)
        rl = cut(ring, 1024).rearrange("p (a n) -> p a n", a=2)
        pool_out = rl.rearrange("p a n -> p (a n)").rearrange("p (a n) -> p a n", a=2)
        sm = cut(ring, 1024).rearrange("p (a n) -> p a n", a=2)
        pr = cut(ring, 1024).rearrange("p (a n) -> p a n", a=2)
        pT = cut(ring, 1024).rearrange("p (a n) -> p a n", a=2)
        kdc = pT.rearrange("p a n -> p (a n)")[:, 0:640].rearrange("p (a n) -> p a n", a=5)
        kd = cut(ring, 1024).rearrange("p (b a n) -> p b a n", b=2, a=4)
        at[0] = 8192
        R = cut(ring, NT * QKV).rearrange("p (j n) -> p j n", j=NT)
        qT = cut(ring, 4 * T).rearrange("p (a t) -> p a t", a=4)
        kT = cut(ring, NKV * TP).rearrange("p (a t) -> p a t", a=NKV)
        kTs = cut(ring, NKV * (PAST + TS)).rearrange("p (a t) -> p a t", a=NKV)
        index = cut(ring, NT * TP).rearrange("p (j n) -> p j n", j=NT)
        vc = cut(ring, 256)
        kic = cut(ring, 64)
        kdi = cut(ring, 256).rearrange("p (b n) -> p b n", b=2)
        assert at[0] <= 24576
        wgu = [ring[:, 12288 * b:12288 * b + 8192].rearrange("p (e c n) -> p e c n", e=2, c=C) for b in range(2)]
        wgu.append(dw)
        wdn = [ring[:, 12288 * b + 8192:12288 * b + 12288].rearrange("p (e c n) -> p e c n", e=2, c=2) for b in range(2)]
        wdn.append(hT[:, :, :].rearrange("p c t -> p (c t)")[:, 0:4096].rearrange("p (e c n) -> p e c n", e=2, c=2))
        ut = ring[:, 20480:21504].rearrange("p (b n) -> p b n", b=2)
        wsr = ring[:, 20480:21504].rearrange("p (g n) -> p g n", g=8)
        lng, lnb = ring[:, 21504:22528], ring[:, 22528:23552]
        wsm = ring[:, 23552:24576].rearrange("p (g n) -> p g n", g=8)

        hr = mid[:, 0:2048].rearrange("p (b n) -> p b n", b=2)
        row = lambda n, j: mid[:, j * D:(j + 1) * D] if n in (1, 3, 4) else hr[:, j % 2, :]
        junk = mid[:, 6144:7168]
        ckr = mid[:, 2048:2304]
        dT = mid[:, 0:4 * T].rearrange("p (g t) -> p g t", g=NG)
        line = mid[:, 2304:2304 + NG * LINE].rearrange("p (g t) -> p g t", g=NG)
        ta, tb = mid[:, 4728:4728 + LINE], mid[:, 4728 + LINE:4728 + 2 * LINE]
        rt = mid[:, 6144:6528].rearrange("p (a n) -> p a n", a=4)
        pw = mid[:, 6528:7040].rearrange("p (g n) -> p g n", g=NG)
        sp15 = sb("sp15", [HIST, 512])
        xg = hr
        xT = mid[:, 2048:4096].rearrange("p (b c n) -> p b c n", b=2, c=C)
        yb = mid[:, 4096:6144].rearrange("p (b n) -> p b n", b=2)
        sg, hh = mid[:, 6144:6400], mid[:, 6400:6656]
        hhT = mid[:, 6656:7168].rearrange("p (b c n) -> p b c n", b=2, c=2)
        cb = ring[:, 10240:20480].rearrange("p (j k n) -> p j k n", j=NT, k=2)
        v = mid[:, 2048:7168].rearrange("p (j n) -> p j n", j=NT)
        hTf = ring[:, 0:C * T].rearrange("p (c t) -> p c t", c=C)
        rounded = lambda name, shape, at: nc.alloc_sbuf_tensor_at(name, shape, F32R, offset=at)
        hTl = rounded("hT_low", [P, C, T], ring_at)
        hTh = rounded("hT_high", [P, C, T], hT_at)
        dwl = rounded("dw_low", [P, 2, C, 512], dw_at)
        high = [rounded(f"dw_high{i}", [P, C, 512], ring_at + 4 * lo) for i, lo in enumerate((4608, 12288, 16384))]
        high += [high[1], high[2], high[1]]
        rq = hT[:, :, :].rearrange("p c t -> p (c t)")
        rat = [0]

        def rcut(n, k=None):
            w = rq[:, rat[0]:rat[0] + n]
            rat[0] += n
            return w.rearrange("p (j n) -> p j n", j=k) if k else w
        ls = rcut(NT * 36, NT)
        igp = rcut(NT * NGRP, NT)
        mg = rcut(NT, NT)
        igf = rcut(NT, NT)
        lem = rcut(NT * NE, NT)
        me = rcut(NT * 8, NT)
        ie = rcut(NT * 8, NT)
        ief = rcut(NT * 2, NT)
        oh = [rcut(NT * NE, NT) for _ in range(2)]
        mbf = rcut(NT * NE // 2).bitcast(BF16).rearrange("p (j n) -> p j n", j=NT)
        cnt = rcut(NE)
        cnti = rcut(NE).bitcast(I32)
        nov = rcut(NE)
        inc = rcut(NE)
        dlt = rcut(NE)
        slt = rcut(NT * NE, NT)
        slo = [rcut(NT * NE, NT) for _ in range(2)]
        slf = rcut(NT * 2, NT)
        gex = rcut(NT * 4, NT)
        gsm = rcut(NT * 2, NT)
        gdf = rcut(NT * 2, NT)
        ov1 = rcut(NOV * NE, NOV)
        ov2 = rcut(NOV + 2)
        ohl = rcut(NT * P).bitcast(BF16).rearrange("p (a n) -> p a n", a=2 * NT)
        ohh = rcut(2 * NT * NPB, 2 * NT)
        sval = rcut(4 * NT * NPB).bitcast(BF16).rearrange("p (h a q v) -> p h a q v", h=2, a=2 * NT, q=NPB)
        slh = rcut(2 * 2 * NT).rearrange("p (h a) -> p h a", h=2)
        slhi = rcut(2 * 2 * NT).bitcast(I32).rearrange("p (h a) -> p h a", h=2)
        assert rat[0] <= 4608

        s_con, s_small, s_xl = sem("con_loaded"), sem("small_loaded"), [sem(f"x_loaded{j}") for j in range(NT)]
        s_cache, s_gain, s_wr = sem("cache_loaded"), sem("gain_loaded"), sem("router_loaded")
        s_dw, s_dwf = [sem(f"dense_loaded{b}") for b in range(2)], sem("dense_used")
        s_pwl, s_gml = sem("pool_w_loaded"), sem("gmlp_small_loaded")
        s_ssq, s_h, s_tp, s_ht = sem("squares"), sem("rows_normed"), sem("rows_turned"), sem("hT_written")
        s_eps = sem("eps_set")
        s_hi, s_lo, s_hl = sem("weights_high"), sem("weights_low"), sem("hT_low_written")
        s_rs, s_va, s_vr, s_vc = sem("rstd"), sem("v_stats"), sem("v_rstd"), sem("v_centred")
        s_hst = [sem(f"rows_stored{b}") for b in range(2)]
        s_res = sem("residual_added")
        s_pps, s_pev = sem("proj_done"), sem("proj_copied")
        s_dup, s_rope, s_tt, s_te = sem("keys_doubled"), sem("roped"), sem("heads_turned"), sem("heads_copied")
        s_is, s_ie, s_ia, s_mb = sem("index_scores"), sem("index_relu"), sem("index_added"), sem("mask_made")
        s_m0, s_pz = sem("mask0_made"), sem("line_zeroed")
        s_s, s_sm, s_nm, s_ex = sem("scores"), sem("scores_masked"), sem("neg_max"), sem("exp_done")
        s_pr, s_ptp, s_pte = sem("probs"), sem("probs_turned"), sem("probsT_copied")
        s_pv, s_oe = sem("pv_done"), sem("heads_out")
        s_pc, s_dt, s_yp, s_ype = sem("pool_chain"), sem("pool_diff"), sem("pool_y"), sem("pool_y_copied")
        s_pot, s_poe = sem("pool_state_turned"), sem("pool_state_copied")
        s_ops = sem("dense_out_done")
        s_lz, s_lg, s_m, s_cnt, s_slot = sem("logits_zeroed"), sem("logits"), sem("choices"), sem("counts"), sem("slots")
        s_dc, s_bf = sem("vector_chain"), sem("bf16_consts")
        s_ovf, s_nrm4 = sem("overflow_table"), sem("gate_exp_in")
        s_ge, s_gat = sem("gate_exp"), sem("gates")
        s_tab, s_tabc = sem("slots_inverted"), sem("slot_tab_written")
        s_kvo, s_poo, s_gvo, s_out = sem("kv_out"), sem("pool_state_out"), sem("gm_v_out"), sem("y_out")
        s_wst, s_wsm, s_gps, s_gev = sem("ws_turned"), sem("ws_masked"), sem("gm_in_done"), sem("gelu_done")
        s_ln, s_mx, s_mxe, s_gu, s_gt, s_gte = (sem("v_normed"), sem("mixed"), sem("mixed_copied"), sem("gated"),
                                               sem("gated_turned"), sem("gated_copied"))
        L2 = range(2)
        s_wgu = [[sem(f"gate_up_loaded{l}{b}") for b in range(3)] for l in L2]
        s_wd = [[sem(f"down_loaded{l}{b}") for b in range(3)] for l in L2]
        s_xg = [[sem(f"gathered{l}{b}") for b in range(2)] for l in L2]
        s_sc = [[sem(f"scattered{l}{b}") for b in range(2)] for l in L2]
        s_xt, s_xte, s_gud = sem("x_turned"), sem("xT_copied"), sem("gate_up_done")
        s_sg, s_hh, s_ht2 = sem("silu_done"), sem("hidden"), sem("hidden_turned")
        s_hte, s_dd, s_yea, s_yed = sem("hiddenT"), sem("down_done"), sem("y_by_act"), sem("y_by_dve")
        s_moe = [sem(f"moe_done{l}") for l in L2]
        s_cl = [sem(f"y_loaded{j}") for j in range(NT)]
        s_cry, o_cry, o_fr = ([sem(f"{n}{l}") for l in L2] for n in ("carried", "ov_carried", "ov_rows_out"))
        o_wgu, o_wd, o_xg, o_t, o_te, o_gu = ([sem(f"ov_{n}{l}") for l in L2] for n in
                                              ("gate_up_loaded", "down_loaded", "gathered", "turned", "xT", "gate_up"))
        o_sg, o_h, o_ht, o_hte, o_d, o_y, o_sc = ([sem(f"ov_{n}{l}") for l in L2] for n in
                                                  ("silu", "hidden", "hid_turned", "hiddenT", "down", "y", "scattered"))

        IDX_TILES = [1, 2, 3, 4]
        tasks = [("proj", 0, 0), ("proj", 0, 1), ("turn", 0)] + [("proj", 0, j) for j in range(2, NT)]
        tasks += [("proj", 1, j) for j in range(NT)]
        tasks += [("proj", 2, 0)] + [("turn", 1 + j) for j in range(NT)]
        idx = lambda b: [("index", (b - 1) * NIH + h) for h in range(NIH)]
        tasks += idx(1) + [("proj", 2, 1), ("proj", 2, 2)] + idx(2) + [("proj", 2, 3), ("proj", 2, 4), ("proj", 3, 0)]
        tasks += idx(3) + [("proj", 3, j) for j in range(1, NT)] + [("pool", m) for m in range(4)]
        tasks += [("turn", 6 + j) for j in range(NT)] + idx(4) + [("pool", m) for m in range(4, 8)]
        NPROJ = 28
        out_bank = lambda n: ps[(6, 7, 5)[n % 3]]
        nkeys = lambda b: PAST + TS if b == 4 else P * (b + 1)
        NU = NT * NH
        POOL_U = 22

        def order(q):
            return (3 - q) * QC

        block = es.enter_context(nc.Block())

        @block.sync
        def _(sp):
            def dense(q):
                if q >= 2:
                    sp.wait_ge(s_dwf, q - 1)
                if q < 4:
                    lo = PW_ + order(q)
                    src = a["par_w_in"][0, :, lo:lo + QC].rearrange("(p c) n -> p c n", c=C)
                elif q == 4:
                    src = a["par_w_in"][0, :, 0:PW_].rearrange("(p c) n -> p c n", c=C)
                elif q < 7:
                    src = a["par_w_out"][0, :, (q - 5) * 512:(q - 4) * 512].rearrange("(c p) n -> p c n", c=C)
                elif q < 11:
                    lo = [1024, 1536, 0, 512][q - 7]
                    src = a["gm_w_in"][0, :, lo:lo + 512].rearrange("(p c) n -> p c n", c=C)
                else:
                    src = a["gm_w_out"][0, :, (q - 11) * 512:(q - 10) * 512].rearrange("(p c) n -> p c n", c=C)
                sp.dma_start(dw[:, q % 2, :, 0:src.shape[2]], src).then_inc(s_dw[q % 2], 16)

            def load_gain(n):
                src = [a["norm_mix"][0], a["norm_ffn"][0], a["norm_mix"][1], a["norm_ffn"][1], a["norm_final"]][n]
                if n:
                    sp.wait_ge(s_h, NT * n)
                sp.dma_start(gain[:, :], src.partition_broadcast(P)).then_inc(s_gain, 16)

            def load_router(l):
                if l:
                    sp.wait_ge(s_lg, 1)
                sp.dma_start(wr[:, :, 0:4], a["moe_router_group"][l].rearrange("(p c) n -> p c n", c=C)).then_inc(s_wr, 16)
                sp.dma_start(wr[:, :, 4:36], a["moe_router_expert"][l].rearrange("(p c) n -> p c n", c=C)).then_inc(s_wr, 16)

            def gate_ups(l, e0, dst, signal, ks=(0, 1)):
                for k in ks:
                    for lo, w in ((0, "moe_w_gate"), (FE, "moe_w_up")):
                        sp.dma_start(dst[:, k, :, lo:lo + FE], a[w][l, bass.ds(e0 + k, 1)]
                                     .rearrange("e (p c) n -> p (e c) n", c=C)).then_inc(signal, 16)

            def downs(l, e0, dst, signal):
                for k in range(2):
                    sp.dma_start(dst[:, k], a["moe_w_down"][l, bass.ds(e0 + k, 1)]
                                 .rearrange("e (p c) n -> p (e c) n", c=2)).then_inc(signal, 16)

            def store_rows(n, l):
                for j in range(NT):
                    sp.wait_ge(s_h, NT * n + j + 1)
                    sp.dma_start(h_rows[l][T0[j]:T0[j] + ROWS[j], :], row(n, j)[0:ROWS[j], :]).then_inc(s_hst[j % 2], 16)

            def experts(l):
                def gu(i, b, used):
                    sp.wait_ge(s_gud, used + PAIRS * l)
                    gate_ups(l, 2 * i, wgu[b], s_wgu[l][b])

                def dn(i, b, used):
                    sp.wait_ge(s_dd, used + PAIRS * l)
                    downs(l, 2 * i, wdn[b], s_wd[l][b])

                sp.wait_ge(s_gat, l + 1)
                downs(l, 4, wdn[2], s_wd[l][2])
                gu(3, 0, 1)
                dn(3, 0, 1)
                gu(4, 1, 2)
                dn(4, 1, 2)
                with sp.Fori(2, PAIRS // 2 - 1) as r:
                    gu(2 * r + 1, 0, 2 * r)
                    dn(2 * r + 1, 0, 2 * r)
                    gu(2 * r + 2, 1, 2 * r + 1)
                    dn(2 * r + 2, 1, 2 * r + 1)
                gu(PAIRS - 1, 0, PAIRS - 2)
                dn(PAIRS - 1, 0, PAIRS - 2)
                if l == 0:
                    for q in (7, 8):
                        dense(q)
                sp.wait_ge(s_ovf, l + 1)
                npairs = sp.value_load(ovf[0:1, NOV + 1:NOV + 2], min_val=0, max_val=NOV // 2)
                with sp.If(npairs > 0):
                    with sp.Fori(0, npairs) as m:
                        sp.wait_ge(o_d[l], m + 1)
                        es_ = [sp.value_load(ovf[0:1, bass.ds(2 * m + k, 1)], min_val=0, max_val=NE - 1) for k in range(2)]
                        for k, e in enumerate(es_):
                            for lo, w in ((0, "moe_w_gate"), (FE, "moe_w_up")):
                                sp.dma_start(wgu[1][:, k, :, lo:lo + FE], a[w][l, bass.ds(e, 1)]
                                             .rearrange("e (p c) n -> p (e c) n", c=C)).then_inc(o_wgu[l], 16)
                        for k, e in enumerate(es_):
                            sp.dma_start(wdn[1][:, k], a["moe_w_down"][l, bass.ds(e, 1)]
                                         .rearrange("e (p c) n -> p (e c) n", c=2)).then_inc(o_wd[l], 16)
                with sp.Else():
                    pass

            def third_pair(l, k):
                sp.wait_ge(s_dwf, 6 * (l + 1) + 1 - k)
                gate_ups(l, 4, wgu[2], s_wgu[l][2], (k,))

            def combine(l):
                sp.wait_ge(s_moe[l], 1)
                for j in range(NT):
                    sp.dma_start(cb[0:ROWS[j], j], y_rows[l][2 * T0[j]:2 * (T0[j] + ROWS[j]), :]
                                 .rearrange("(p k) n -> p k n", k=2)).then_inc(s_cl[j], 16)

            sp.dma_start(x[:, 0, :], a["x_prompt"][0, 0:P, :]).then_inc(s_xl[0], 16)
            load_gain(0)
            sp.dma_start(con[:, :], a["con"]).then_inc(s_con, 16)
            sp.dma_start(x[:, 1, :], a["x_prompt"][0, P:2 * P, :]).then_inc(s_xl[1], 16)
            dense(0)
            for j in range(2, 4):
                sp.dma_start(x[:, j, :], a["x_prompt"][0, P * j:P * j + P, :]).then_inc(s_xl[j], 16)
            sp.dma_start(x[0:TS, 4, :], a["x_sample"][0]).then_inc(s_xl[4], 16)
            sp.dma_start(kic, a["cache_idx_k"][0, 0]).then_inc(s_cache, 16)
            sp.dma_start(ckr, a["cache_k"][0, 0].rearrange("s h d -> s (h d)")).then_inc(s_cache, 16)
            sp.dma_start(vc, a["cache_v"][0, 0].rearrange("s h d -> s (h d)")).then_inc(s_cache, 16)
            sp.dma_start(sp15[:, :], a["state_pool"][0, 0]).then_inc(s_cache, 16)
            dense(1)
            sp.dma_start(pscale[:, :], a["par_pool_scale"][0].rearrange("(g p) -> p g", p=P), allow_slow_non_contiguous=True).then_inc(s_small, 16)
            sp.dma_start(gbias[:, :], a["gm_bs"][0].rearrange("g t -> t g"), allow_slow_non_contiguous=True).then_inc(s_small, 16)
            load_router(0)
            sp.wait_ge(s_ssq, NT)
            sp.dma_start(pw[:, :, :], a["par_pool_w"][0].rearrange("g c d -> c g d")).then_inc(s_pwl, 16)
            load_gain(1)
            for q in range(2, 7):
                dense(q)
            sp.wait_ge(s_rope, 2 * NT)
            for o, lo, w in ((2, OK_, 256), (3, OV, 256), (4, OKI, 64)):
                dst = out[o][0, 0] if o == 4 else out[o][0, 0].rearrange("t h d -> t (h d)")
                sp.dma_start(dst.rearrange("(j p) n -> p j n", p=P), R[:, 0:4, lo:lo + w]).then_inc(s_kvo, 16)
                dst = out[o + 4][0, 0] if o == 4 else out[o + 4][0, 0].rearrange("t h d -> t (h d)")
                sp.dma_start(dst, R[0:TS, 4, lo:lo + w]).then_inc(s_kvo, 16)
            sp.wait_ge(s_poe, 1)
            for k in range(2):
                sp.dma_start(out[5 + 4 * k][0, 0], pool_out[0:HIST, k, :]).then_inc(s_poo, 16)
            sp.wait_ge(s_kvo, 16 * 6)
            sp.wait_ge(s_poo, 16 * 2)
            sp.wait_ge(s_pv, NU)
            for i in range(2):
                gate_ups(0, 2 * i, wgu[i], s_wgu[0][i])
                downs(0, 2 * i, wdn[i], s_wd[0][i])
            third_pair(0, 1)
            third_pair(0, 0)
            store_rows(1, 0)
            load_gain(2)
            experts(0)
            combine(0)
            for b in range(2):
                sp.dma_start(*((lng, a["gm_ln_g"][0].partition_broadcast(P)) if b else
                               (lnb, a["gm_ln_b"][0].partition_broadcast(P)))).then_inc(s_gml, 16)
            sp.dma_start(wsr, a["gm_ws"][0].rearrange("g t s -> t g s")).then_inc(s_gml, 16)
            load_router(1)
            load_gain(3)
            dense(9)
            sp.wait_ge(s_res, 15)
            downs(1, 0, wdn[0], s_wd[1][0])
            dense(10)
            sp.wait_ge(s_ln, NT)
            sp.dma_start(out[10][0, 0], v[0:TS, 4, :]).then_inc(s_gvo, 16)
            dense(11)
            dense(12)
            sp.wait_ge(s_gt, NT)
            sp.wait_ge(s_gu, 2 * NT)
            downs(1, 2, wdn[1], s_wd[1][1])
            third_pair(1, 1)
            sp.wait_ge(s_dwf, 13)
            gate_ups(1, 0, wgu[0], s_wgu[1][0])
            store_rows(3, 1)
            third_pair(1, 0)
            gate_ups(1, 2, wgu[1], s_wgu[1][1], (0,))
            for b in range(2):
                sp.wait_ge(s_xg[1][b], 16)
            gate_ups(1, 2, wgu[1], s_wgu[1][1], (1,))
            load_gain(4)
            experts(1)
            combine(1)
            for j in range(NT):
                sp.wait_ge(s_h, 4 * NT + j + 1)
                dst = out[0][0, T0[j]:T0[j] + P, :] if j < 4 else out[1][0]
                sp.dma_start(dst, row(4, j)[0:ROWS[j], :]).then_inc(s_hst[j % 2], 16)
            sp.wait_ge(s_hst[0], 16 * 9)
            sp.wait_ge(s_hst[1], 16 * 6)
            sp.wait_ge(s_gvo, 16)

        @block.gpsimd
        def _(pool):
            done = [0]

            def link(ins):
                done[0] += 1
                ins.then_inc(s_pc, 1)
                pool.wait_ge(s_pc, done[0])

            pool.memset(eps[:, 0:1], 1e-6).then_inc(s_eps, 1)
            pool.memset(eps[:, 1:2], 1e-5).then_inc(s_eps, 1)
            link(pool.memset(cell[:, :], 0.0))
            pool.memset(line[:, :, 0:HIST], 0.0).then_inc(s_pz, 1)
            link(pool.memset(index[:, 0, 0:P], 0.0))
            pool.memset(index[0:64, 0, 64:P], NEG).then_inc(s_m0, 1)
            pool.wait_ge(s_pev, NPROJ)
            pool.wait_ge(s_pz, 1)
            pool.wait_ge(s_te, 1)
            for g in range(NG):
                src, w = line[:, g, :], 1
                for i in range(g + 1):
                    dst = (ta, tb)[i % 2]
                    w *= 2
                    link(pool.tensor_tensor(dst[:, w - 1:LINE], src[:, w - 1:LINE], src[:, w - 1 - w // 2:LINE - w // 2], ALU.add))
                    src = dst
                dst = (ta, tb)[(g + 1) % 2]
                pool.tensor_tensor(dst[:, XP0:XP0 + 16], src[:, XP0:XP0 + 16], c_("rcnt", NG)[:, g, :], ALU.mult)
                link(pool.tensor_scalar(dst[:, XP0 + 16:LINE], src[:, XP0 + 16:LINE], 1.0 / w, None, ALU.mult))
                pool.tensor_tensor(dT[:, g, 0:TP], dst[:, XP0:XP0 + TP], line[:, g, XP0:XP0 + TP], ALU.subtract)
                link(pool.tensor_tensor(dT[:, g, TP:T], dst[:, XS0:LINE], line[:, g, XS0:LINE], ALU.subtract))
                pool.nop().then_inc(s_dt, 1)

            def carry(signal, to, before):
                pool.wait_ge(signal, before)
                pool.tensor_tensor(cell[:, to:to + 1], cell[:, 4:5], cell[:, 5:6], ALU.add).then_inc(signal, 1)

            def take_index(dst, l, i, n):
                pool.tensor_copy(dst, tab[:, bass.ds(i, 1), :].rearrange("p a v -> p (a v)")).then_inc(s_cry[l], 1)
                carry(s_cry[l], 2 * l, 2 * n + 1)

            def gather(l, i, b, n, turned=None, signal=None):
                if turned is not None:
                    pool.wait_ge(s_xt, turned + PAIRS * l)
                take_index(gix[:, b, :], l, i, n)
                pool.indirect_dma_start(xg[:, b, :], None, h_rows[l], bass.IndirectOffsetOnAxis(ap=gix[:, b, 0:1], axis=0),
                                        bounds_check=T - 1, oob_is_err=False).then_inc(signal or s_xg[l][b], 16)

            def scatter(l, i, b, n):
                pool.wait_ge(s_yea, i + 1 + PAIRS * l)
                pool.wait_ge(s_yed, i + 1 + PAIRS * l)
                take_index(six[:, b, :], l, i, n)
                pool.indirect_dma_start(y_rows[l], bass.IndirectOffsetOnAxis(ap=six[:, b, 1:2], axis=0), yb[:, b, :], None,
                                        bounds_check=2 * T - 1, oob_is_err=False).then_inc(s_sc[l][b], 16)

            def weights_low(q):
                for k in range(2):
                    pool.wait_ge(s_hi, 2 * (q - 7) + k + 1)
                    part = dw[:, q % 2, 4 * k:4 * k + 4, :]
                    pool.tensor_tensor(dwl[:, q % 2, 4 * k:4 * k + 4, :], part, high[q - 7][:, 4 * k:4 * k + 4, :].bitcast(F32),
                                       ALU.subtract).then_inc(s_lo, 1)

            def hT_low(j, written, before):
                pool.wait_ge(written, before + j + 1)
                cols = slice(T0[j], T0[j] + ROWS[j])
                pool.tensor_tensor(hTl[:, :, cols], hTf[:, :, cols], hTh[:, :, cols].bitcast(F32), ALU.subtract).then_inc(s_hl, 1)

            for l in range(2):
                pool.wait_ge(s_tabc, l + 1)
                for b in range(2):
                    pool.wait_ge(s_hst[b], 16 * ((3 - b) * (l + 1)))
                pool.wait_ge(s_tp, NT * (2 * l + 2))
                gather(l, 0, 0, 0)
                gather(l, 1, 1, 1)

                def step(i, b):
                    gather(l, i + 2, b, 2 * i + 2, i + 1)
                    scatter(l, i, b, 2 * i + 3)

                with pool.Fori(0, PAIRS // 2 - 1) as r:
                    step(2 * r, 0)
                    step(2 * r + 1, 1)
                gather(l, PAIRS, 0, 2 * PAIRS - 2, PAIRS - 1, o_xg[l])
                scatter(l, PAIRS - 2, 0, 2 * PAIRS - 1)
                scatter(l, PAIRS - 1, 1, 2 * PAIRS)
                pool.wait_ge(s_ovf, l + 1)
                npairs = pool.value_load(ovf[0:1, NOV + 1:NOV + 2], min_val=0, max_val=NOV // 2)
                with pool.If(npairs > 0):
                    pool.tensor_tensor(cell[:, 2 * l + 1:2 * l + 2], cell[:, 4:5], cell[:, 5:6], ALU.add).then_inc(o_cry[l], 1)
                    pool.wait_ge(s_sc[l][0], 16 * PAIRS // 2)
                    pool.nop().then_inc(o_fr[l], 1)
                    with pool.Fori(0, npairs) as m:
                        pool.wait_ge(o_t[l], m + 1)
                        carry(o_cry[l], 2 * l + 1, 7 * m + 1)
                        pool.tensor_copy(gix[:, 0, :], tab[:, bass.ds(m + PAIRS + 1, 1), :].rearrange("p a v -> p (a v)")).then_inc(o_cry[l], 1)
                        carry(o_cry[l], 2 * l + 1, 7 * m + 3)
                        pool.indirect_dma_start(xg[:, 0, :], None, h_rows[l], bass.IndirectOffsetOnAxis(ap=gix[:, 0, 0:1], axis=0),
                                                bounds_check=T - 1, oob_is_err=False).then_inc(o_xg[l], 16)
                        pool.wait_ge(o_y[l], 2 * m + 2)
                        carry(o_cry[l], 2 * l + 1, 7 * m + 4)
                        pool.tensor_copy(six[:, 0, :], tab[:, bass.ds(m + PAIRS, 1), :].rearrange("p a v -> p (a v)")).then_inc(o_cry[l], 1)
                        carry(o_cry[l], 2 * l + 1, 7 * m + 6)
                        pool.indirect_dma_start(y_rows[l], bass.IndirectOffsetOnAxis(ap=six[:, 0, 1:2], axis=0), yb[:, 0, :], None,
                                                bounds_check=2 * T - 1, oob_is_err=False).then_inc(o_sc[l], 16)
                        pool.wait_ge(o_sc[l], 16 * m + 16)
                        pool.wait_ge(o_xg[l], 16 * m + 32)
                        carry(o_cry[l], 2 * l + 1, 7 * m + 7)
                        pool.nop().then_inc(o_fr[l], 1)
                with pool.Else():
                    pass
                for b in range(2):
                    pool.wait_ge(s_sc[l][b], 16 * PAIRS // 2)
                pool.wait_ge(o_xg[l], 16)
                pool.nop().then_inc(s_moe[l], 1)
                if l == 0:
                    weights_low(7)
                    for j in range(NT):
                        hT_low(j, s_ht, 2 * NT)
                    for q in range(8, 12):
                        weights_low(q)
                    for j in range(NT):
                        hT_low(j, s_gte, 0)
                    weights_low(12)

        @block.scalar
        def _(act):
            def copy(dst, src):
                return act.activation(dst, src, ACT.Copy)

            def split(q):
                act.wait_ge(s_dw[q % 2], 16 * (q // 2 + 1))
                if q in (8, 9):
                    act.wait_ge(s_res, 15)
                elif q > 9:
                    act.wait_ge(s_dwf, q - 1)
                for k in range(2):
                    copy(high[q - 7][:, 4 * k:4 * k + 4, :], dw[:, q % 2, 4 * k:4 * k + 4, :]).then_inc(s_hi, 1)

            def turned(j, parts):
                for dst in (hTh, hTf) if parts else (hT,):
                    for k in range(2):
                        ins = copy(dst[:, 4 * k:4 * k + 4, T0[j]:T0[j] + ROWS[j]],
                                   ps[2 * (j % 2) + k][:, :].rearrange("p (c t) -> p c t", c=4)[:, :, 0:ROWS[j]])
                return ins

            def norm(n):
                def square(j):
                    if n == 0:
                        act.wait_ge(s_xl[j], 16)
                    else:
                        act.wait_ge(s_res, [0, 10, 15, 25, 30][n] - NT + j + 1)
                    act.activation(junk[0:ROWS[j], :], x[0:ROWS[j], j, :], ACT.Square, scale=D ** -0.5,
                                   accum_out=st[0:ROWS[j], j:j + 1]).then_inc(s_ssq, 1)
                    act.wait_ge(s_ssq, NT * n + j + 1)
                    act.activation(st[0:ROWS[j], 5 + j:6 + j], st[0:ROWS[j], j:j + 1], ACT.Sqrt, bias=eps[0:ROWS[j], 0:1]).then_inc(s_rs, 1)

                def hT_copy(j):
                    act.wait_ge(s_tp, NT * n + j + 1)
                    turned(j, n == 2).then_inc(s_ht, 1)
                ahead = n % 2 == 0
                if ahead:
                    square(0)
                for j in range(NT):
                    if not ahead:
                        square(j)
                    elif j + 1 < NT:
                        square(j + 1)
                    if n < 4:
                        hT_copy(j)

            act.wait_ge(s_eps, 2)
            norm(0)
            for task in tasks:
                if task[0] == "proj":
                    _, q, j = task
                    n = NT * q + j
                    act.wait_ge(s_pps, n + 1)
                    if ROWS[j] == P:
                        copy(R[:, j, order(q):order(q) + QC], ps[4 + n % 4][:, 0:QC]).then_inc(s_pev, 1)
                    else:
                        h = QC // 2
                        copy(R[0:TS, j, order(q):order(q) + h], ps[4 + n % 4][0:TS, 0:h])
                        copy(R[0:TS, j, order(q) + h:order(q) + QC], ps[4 + n % 4][TS:P, 0:h]).then_inc(s_pev, 1)
                elif task[0] == "pool":
                    m = task[1]
                    g, n = m // 2, 20 + m
                    act.wait_ge(s_pps, n + 1)
                    acc = ps[4 + n % 4]
                    if m % 2 == 0:
                        copy(line[:, g, XP0:XP0 + HALF], acc[:, 0:HALF]).then_inc(s_pev, 1)
                    else:
                        copy(line[:, g, XP0 + HALF:XP0 + TP], acc[:, 0:TP - HALF])
                        copy(line[:, g, XS0:LINE], acc[:, TP - HALF:HALF]).then_inc(s_pev, 1)
                elif task[0] == "turn":
                    i = task[1]
                    act.wait_ge(s_tt, i + 1)
                    b0 = ps[0][:, :].rearrange("p (a n) -> p a n", a=4)
                    b1 = ps[1][:, :].rearrange("p (a n) -> p a n", a=4)
                    if i == 0:
                        copy(kiTs[:, 0:PAST], b0[:, 0, :])
                        copy(line[:, :, XS0 - HIST:XS0], ps[0][:, 128:192].rearrange("p (g n) -> p g n", g=4)[:, :, 0:HIST])
                        copy(kTs[:, :, 0:PAST], b1).then_inc(s_te, 1)
                    elif i < 6:
                        j = i - 1
                        copy(qiT[:, :, T0[j]:T0[j] + ROWS[j]], b0[:, :, 0:ROWS[j]])
                        dst = kiT[:, T0[j]:T0[j] + P] if j < 4 else kiTs[:, PAST:PAST + TS]
                        copy(dst, b1[:, 0, 0:ROWS[j]]).then_inc(s_te, 1)
                    else:
                        j = i - 6
                        copy(qT[:, :, T0[j]:T0[j] + ROWS[j]], b0[:, :, 0:ROWS[j]])
                        dst = kT[:, :, T0[j]:T0[j] + P] if j < 4 else kTs[:, :, PAST:PAST + TS]
                        copy(dst, b1[:, :, 0:ROWS[j]]).then_inc(s_te, 1)
                else:
                    u = task[1]
                    b = IDX_TILES[u // NIH]
                    act.wait_ge(s_is, u + 1)
                    if u >= 2:
                        act.wait_ge(s_ia, u - 1)
                    act.activation(rl[0:ROWS[b], u % 2, 0:nkeys(b)], ps[2 + u % 2][0:ROWS[b], 0:nkeys(b)],
                                   ACT.Relu).then_inc(s_ie, 1)

            def exp(u):
                b = u // NH
                n, r = nkeys(b), ROWS[b]
                act.wait_ge(s_nm, u + 1)
                if u >= 2:
                    act.wait_ge(s_ptp, u - 1)
                act.activation(pr[0:r, u % 2, 0:n], sm[0:r, u % 2, 0:n], ACT.Exp, bias=st[0:r, 10 + u % 2:11 + u % 2],
                               scale=SCALE, accum_out=st[0:r, 12 + u % 2:13 + u % 2]).then_inc(s_ex, 1)

            def probsT(u):
                b = u // NH
                act.wait_ge(s_ptp, u + 1)
                if u >= 2:
                    act.wait_ge(s_pv, u - 1)
                src, dst = (z.rearrange("p (c n) -> p c n", c=4) for z in (ps[u % 2][:, :], pT[:, u % 2, :]))
                if b < 4:
                    copy(dst[:, 0:b + 1, :], src[:, 0:b + 1, :]).then_inc(s_pte, 1)
                else:
                    copy(dst[:, 0, 0:TS], src[:, 0, 0:TS])
                    copy(dst[0:TS, 1, 0:TS], src[0:TS, 1, 0:TS]).then_inc(s_pte, 1)

            def heads(k):
                b, g = k // NKV, k % NKV
                act.wait_ge(s_pv, 2 * k + 2)
                copy(hT[:, 4 + g, T0[b]:T0[b] + ROWS[b]], ps[4 + k % 2][:, 0:ROWS[b]]).then_inc(s_oe, 1)

            def pool_state():
                act.wait_ge(s_pot, 1)
                for k in range(2):
                    ins = copy(pool_out[0:HIST, k, :], ps[6 + k][0:HIST, :])
                ins.then_inc(s_poe, 1)
                act.wait_ge(s_small, 32)

            def pool_map(m):
                act.wait_ge(s_yp, m + 1)
                g = m // 2
                act.activation(hT[:, g, (m % 2) * HALF:(m % 2 + 1) * HALF], ps[6 + m % 2][:, 0:HALF], ACT.Copy,
                               scale=pscale[:, g:g + 1]).then_inc(s_ype, 1)

            exp(0)
            for u in range(NU):
                if u + 1 < NU:
                    exp(u + 1)
                probsT(u)
                if u % 2 == 0 and u:
                    heads(u // 2 - 1)
                if u == POOL_U + 1:
                    pool_state()
                elif POOL_U + 1 < u <= POOL_U + 9:
                    pool_map(u - POOL_U - 2)
            heads(NU // 2 - 1)
            def experts(l):
                act.wait_ge(s_nrm4, l + 1)
                act.activation(gex[:, :, :], ls[:, :, 0:4], ACT.Exp)
                act.activation(gsm[:, :, 1:2], gdf[:, :, 0:1], ACT.Exp).then_inc(s_ge, 1)

                def turned(i, b, first=False):
                    act.wait_ge(s_xt, i + 1 + PAIRS * l)
                    if not first:
                        act.wait_ge(s_gud, i - 1 + PAIRS * l)
                    for k in range(2):
                        ins = copy(xT[:, b, 4 * k:4 * k + 4, :], ps[k][:, :].rearrange("p (c t) -> p c t", c=4))
                    ins.then_inc(s_xte, 1)

                def rest(i, b, g, first=False, last=False):
                    act.wait_ge(s_gud, i + 1 + PAIRS * l)
                    if not (first and b == 0):
                        act.wait_ge(s_hh, i + PAIRS * l)
                    act.activation(sg, ps[2 + b][:, 0:FE], ACT.Silu).then_inc(s_sg, 1)
                    if not (last and b == 1):
                        turned(i + 1, 1 - b, first and b == 0)
                    act.wait_ge(s_dd, i + 1 + PAIRS * l)
                    if not first:
                        act.wait_ge(s_sc[l][b], 16 * g)
                    copy(yb[:, b, 512:1024], ps[7][:, :]).then_inc(s_yea, 1)

                turned(0, 0, True)
                rest(0, 0, 0, True)
                rest(1, 1, 0, True)
                with act.Fori(1, PAIRS // 2 - 1) as r:
                    rest(2 * r, 0, r)
                    rest(2 * r + 1, 1, r)
                rest(PAIRS - 2, 0, PAIRS // 2 - 1)
                rest(PAIRS - 1, 1, PAIRS // 2 - 1, last=True)
                act.wait_ge(s_ovf, l + 1)
                npairs = act.value_load(ovf[0:1, NOV + 1:NOV + 2], min_val=0, max_val=NOV // 2)
                with act.If(npairs > 0):
                    with act.Fori(0, npairs) as m:
                        act.wait_ge(o_t[l], m + 1)
                        for k in range(2):
                            ins = copy(xT[:, 0, 4 * k:4 * k + 4, :], ps[k][:, :].rearrange("p (c t) -> p c t", c=4))
                        ins.then_inc(o_te[l], 1)
                        act.wait_ge(o_gu[l], m + 1)
                        act.activation(sg, ps[2][:, 0:FE], ACT.Silu).then_inc(o_sg[l], 1)
                        act.wait_ge(o_d[l], m + 2)
                        act.wait_ge(o_fr[l], m + 1)
                        copy(yb[:, 0, 512:1024], ps[7][:, :]).then_inc(o_y[l], 1)
                with act.Else():
                    pass

            norm(1)
            experts(0)
            split(7)
            norm(2)
            for n in range(2 * NT):
                j = n % NT
                if j == 1:
                    split(8 + n // NT)
                act.wait_ge(s_gps, n + 1)
                act.activation(v[0:ROWS[j], j, (n // NT) * 512:(n // NT + 1) * 512], ps[4 + n % 4][0:ROWS[j], :],
                               ACT.Gelu_apprx_tanh).then_inc(s_gev, 1)

            def v_root(j):
                act.wait_ge(s_va, j + 1)
                act.activation(st[0:ROWS[j], 46 + j:47 + j], st[0:ROWS[j], 37 + 2 * j:38 + 2 * j], ACT.Sqrt,
                               bias=eps[0:ROWS[j], 1:2]).then_inc(s_vr, 1)

            def u_gelu(n):
                j = n % NT
                act.wait_ge(s_gps, n + 1)
                if n - 2 * NT >= 2:
                    act.wait_ge(s_gu, n - 2 * NT - 1)
                else:
                    act.wait_ge(s_wsm, 1)
                act.activation(ut[0:ROWS[j], n % 2, :], ps[4 + n % 4][0:ROWS[j], :], ACT.Gelu_apprx_tanh).then_inc(s_gev, 1)

            def gated(j):
                act.wait_ge(s_gt, j + 1)
                turned(j, True).then_inc(s_gte, 1)
            for j in range(NT):
                v_root(j)
            for n in range(2 * NT, 3 * NT + 1):
                if n == 2 * NT + 1:
                    split(10)
                u_gelu(n)
            split(11)
            for j in range(NT):
                if j + 1 < NT:
                    u_gelu(3 * NT + j + 1)
                gated(j)
            split(12)
            norm(3)
            experts(1)
            norm(4)

        @block.vector
        def _(dve):
            done = [0]

            def link(ins):
                done[0] += 1
                ins.then_inc(s_dc, 1)
                dve.wait_ge(s_dc, done[0])

            def inverse_root(r, square, root, e, dst):
                link(dve.reciprocal(dst, root))
                link(dve.scalar_tensor_tensor(st[0:r, 60:61], square, e, dst, ALU.add, ALU.mult))
                link(dve.tensor_scalar(st[0:r, 60:61], st[0:r, 60:61], dst, 3.0, ALU.mult, ALU.subtract))
                link(dve.scalar_tensor_tensor(dst, st[0:r, 60:61], -0.5, dst, ALU.mult, ALU.mult))

            def norm_tile(n, j):
                r = ROWS[j]
                dve.wait_ge(s_rs, NT * n + j + 1)
                inverse_root(r, st[0:r, j:j + 1], st[0:r, 5 + j:6 + j], 1e-6, st[0:r, 14 + j:15 + j])
                if j >= 2 and n in (0, 2):
                    dve.wait_ge(s_tp, NT * n + j - 1)
                dve.scalar_tensor_tensor(row(n, j)[0:r, :], x[0:r, j, :], st[0:r, 14 + j:15 + j], gain[0:r, :],
                                         ALU.mult, ALU.mult).then_inc(s_h, 1)

            def norm(n, first):
                first(0)
                dve.wait_ge(s_gain, 16 * (n + 1))
                for j in range(NT):
                    if j + 1 < NT:
                        first(j + 1)
                    norm_tile(n, j)

            def rope(j, lo, nh, dup, dst_n):
                r = ROWS[j]
                hv = R[0:r, j, lo:lo + nh * HD].rearrange("p (h d) -> p h d", h=nh)
                x1, x2 = hv[:, :, 0:8], hv[:, :, 8:16]
                co = cos[0:r, j, :].unsqueeze(1).to_broadcast([r, nh, 8])
                si = sin[0:r, j, :].unsqueeze(1).to_broadcast([r, nh, 8])
                t = [rt[0:r, k, 0:nh * 8].rearrange("p (h d) -> p h d", h=nh) for k in range(4)]
                dve.tensor_tensor(t[0], x1, co, ALU.mult)
                dve.tensor_tensor(t[1], x2, si, ALU.mult)
                dve.tensor_tensor(t[2], x2, co, ALU.mult)
                link(dve.tensor_tensor(t[3], x1, si, ALU.mult))
                dve.tensor_tensor(x1, t[0], t[1], ALU.subtract)
                link(dve.tensor_tensor(x2, t[2], t[3], ALU.add))
                if j >= 2:
                    dve.wait_ge(s_tt, dst_n - 1)
                dve.tensor_copy(dup[0], dup[1]).then_inc(s_rope, 1)

            dve.wait_ge(s_con, 16)
            dve.tensor_copy(cbf[:, 0, :], c_("upper"))
            dve.tensor_copy(cbf[:, 1, :], c_("ones")).then_inc(s_bf, 1)

            def double_cached(j):
                if j == 3:
                    dve.wait_ge(s_cache, 64)
                    dve.tensor_copy(kdc[:, 0, :].rearrange("p (b n) -> p b n", b=2), kic.unsqueeze(1).to_broadcast([P, 2, HD]))
                    for g in range(NKV):
                        ins = dve.tensor_copy(kdc[:, 1 + g, :].rearrange("p (b n) -> p b n", b=2),
                                              ckr[:, g * HD:(g + 1) * HD].unsqueeze(1).to_broadcast([P, 2, HD]))
                    ins.then_inc(s_dup, 1)
            norm(0, double_cached)
            for j in range(NT):
                dve.wait_ge(s_pev, NT + j + 1)
                rope(j, OQI, NIH + 1, (kdi[0:ROWS[j], j % 2, :].rearrange("p (b n) -> p b n", b=2),
                                       R[0:ROWS[j], j, OKI:OKI + HD].unsqueeze(1).to_broadcast([ROWS[j], 2, HD])), j + 1)

            def index_add(b):
                r, n = ROWS[b], nkeys(b)
                acc = index[0:r, b, 0:n]
                for h in range(NIH):
                    u = IDX_TILES.index(b) * NIH + h
                    dve.wait_ge(s_ie, u + 1)
                    wi = R[0:r, b, OWI + h:OWI + h + 1]
                    if h == 0:
                        dve.tensor_scalar(acc, rl[0:r, u % 2, 0:n], wi, None, ALU.mult).then_inc(s_ia, 1)
                    else:
                        dve.scalar_tensor_tensor(acc, rl[0:r, u % 2, 0:n], wi, acc, ALU.mult, ALU.add).then_inc(s_ia, 1)
                    dve.wait_ge(s_ia, u + 1)

            def top_k(b):
                r, n = ROWS[b], nkeys(b)
                acc = index[0:r, b, 0:n]
                if b < 4:
                    link(dve.memset(index[0:64, b, n - 64:n], NEG_ADM))
                for _ in range((TK_P if b < 4 else TK_S) // 8):
                    link(dve.max(m8[0:r, :], acc))
                    link(dve.match_replace(acc, m8[0:r, :], acc, NEG_SEL))
                dve.tensor_scalar(acc, acc, 0.5 * (NEG_SEL + NEG_ADM), NEG, ALU.is_gt, ALU.mult).then_inc(s_mb, 1)

            for b in (1, 2, 3):
                index_add(b)
                top_k(b)
            for j in range(NT):
                dve.wait_ge(s_pev, 3 * NT + j + 1)
                r = ROWS[j]
                rope(j, OQ, NH + NKV, (kd[0:r, j % 2].rearrange("p a (b n) -> p a b n", b=2),
                                       R[0:r, j, OK_:OK_ + 256].rearrange("p (a n) -> p a n", a=NKV).unsqueeze(2)
                                       .to_broadcast([r, NKV, 2, HD])), j + 6)
            index_add(4)
            top_k(4)

            def masked(u):
                b = u // NH
                r, n = ROWS[b], nkeys(b)
                dve.wait_ge(s_s, u + 1)
                if b == 0:
                    dve.wait_ge(s_m0, 1)
                else:
                    dve.wait_ge(s_mb, b)
                if u >= 2:
                    dve.wait_ge(s_ex, u - 1)
                dve.tensor_tensor_reduce(sm[0:r, u % 2, 0:n], ps[2 + u % 2][0:r, 0:n], index[0:r, b, 0:n], 1.0, -3.0e38,
                                         ALU.add, ALU.max, st[0:r, 20 + u % 2:21 + u % 2]).then_inc(s_sm, 1)
                dve.wait_ge(s_sm, u + 1)
                dve.tensor_scalar(st[0:r, 10 + u % 2:11 + u % 2], st[0:r, 20 + u % 2:21 + u % 2], -SCALE, None,
                                  ALU.mult).then_inc(s_nm, 1)

            def normed(u):
                b = u // NH
                r, n = ROWS[b], nkeys(b)
                dve.wait_ge(s_ex, u + 1)
                link(dve.reciprocal(st[0:r, 22 + u % 2:23 + u % 2], st[0:r, 12 + u % 2:13 + u % 2]))
                dve.tensor_scalar(pr[0:r, u % 2, 0:n], pr[0:r, u % 2, 0:n], st[0:r, 22 + u % 2:23 + u % 2], None,
                                  ALU.mult).then_inc(s_pr, 1)

            masked(0)
            for u in range(NU):
                if u + 1 < NU:
                    masked(u + 1)
                normed(u)

            def dense_out(k):
                dve.wait_ge(*((s_gev, 4 * NT) if k else (s_oe, NU // 2)))
                dve.memset(ps[4][64:P, 144:180], 0.0).then_inc(s_lz, 1)
                dve.wait_ge(s_gain, 16 * (2 * k + 2))
                for n in range(2 * NT):
                    hf, j = n // NT, n % NT
                    r = ROWS[j]
                    dve.wait_ge(s_ops, 10 * k + n + 1)
                    xs = x[0:r, j, hf * 512:hf * 512 + 512]
                    if k or r == P:
                        dve.tensor_tensor(xs, xs, out_bank(n)[0:r, :], ALU.add).then_inc(s_res, 1)
                    else:
                        dve.tensor_tensor(xs[:, 0:256], xs[:, 0:256], out_bank(n)[0:r, 0:256], ALU.add)
                        dve.tensor_tensor(xs[:, 256:512], xs[:, 256:512], out_bank(n)[r:P, 0:256], ALU.add).then_inc(s_res, 1)
                    if hf:
                        norm_tile(2 * k + 1, j)

            def route(l):
                bc = lambda name: c_(name)[:, 0:NE].unsqueeze(1).to_broadcast([P, NT, NE])
                dve.wait_ge(s_lg, l + 1)
                link(dve.tensor_copy(ls, ps[4][:, 0:180].rearrange("p (j n) -> p j n", j=NT)))
                lg4 = ls[:, :, 0:NGRP]
                link(dve.tensor_reduce(mg, lg4, AX.X, ALU.max))
                link(dve.tensor_tensor(lg4, lg4, mg.to_broadcast([P, NT, NGRP]), ALU.subtract))
                link(dve.tensor_scalar(igp, lg4, 0.0, float(NGRP), ALU.is_lt, ALU.mult))
                link(dve.tensor_tensor(igp, igp, c_("iota")[:, 0:NGRP].unsqueeze(1).to_broadcast([P, NT, NGRP]), ALU.add))
                link(dve.tensor_reduce(igf, igp, AX.X, ALU.min))
                link(dve.tensor_tensor(lem, bc("egrp"), igf.to_broadcast([P, NT, NE]), ALU.not_equal))
                link(dve.scalar_tensor_tensor(lem, lem, NEG, ls[:, :, 4:36], ALU.mult, ALU.add))
                for j in range(NT):
                    ins = dve.max(me[:, j, :], lem[:, j, :])
                link(ins)
                for j in range(NT):
                    ins = dve.max_index(ie[:, j, :].bitcast(U32), me[:, j, :], lem[:, j, :])
                link(ins)
                dve.tensor_tensor(gdf[:, :, 0:1], me[:, :, 1:2], me[:, :, 0:1], ALU.subtract).then_inc(s_nrm4, 1)
                link(dve.tensor_copy(ief, ie[:, :, 0:2].bitcast(U32)))
                for k in range(2):
                    ins = dve.tensor_tensor(oh[k], bc("iota"), ief[:, :, k:k + 1].to_broadcast([P, NT, NE]), ALU.is_equal)
                link(ins)
                dve.tensor_tensor(mbf, oh[0], oh[1], ALU.add).then_inc(s_m, 1)
                dve.wait_ge(s_cnt, l + 1)
                link(dve.tensor_scalar(cnti, ps[5][:, 160:192], float(BLK - 1), None, ALU.add))
                link(dve.tensor_scalar(cnti, cnti, 6, None, ALU.logical_shift_right))
                link(dve.tensor_scalar(nov, cnti, -1.0, 0.0, ALU.add, ALU.max))
                link(dve.tensor_tensor_scan(inc, c_("ones")[:, 0:NE], nov, 0.0, ALU.mult, ALU.add))
                link(dve.tensor_tensor(dlt, inc, nov, ALU.subtract))
                link(dve.tensor_scalar(dlt, dlt, float(BLK), float(MAIN - BLK), ALU.mult, ALU.add))
                link(dve.tensor_tensor(dlt, dlt, c_("base"), ALU.subtract))
                pp = ps[5][:, 0:160].rearrange("p (j n) -> p j n", j=NT)
                link(dve.scalar_tensor_tensor(slt, pp, float(BLK), dlt.unsqueeze(1).to_broadcast([P, NT, NE]), ALU.is_ge, ALU.mult))
                link(dve.tensor_tensor(slt, slt, pp, ALU.add))
                link(dve.tensor_tensor(slt, slt, bc("base"), ALU.add))
                for k in range(2):
                    ins = dve.tensor_tensor(slo[k], slt, oh[k], ALU.mult)
                link(ins)
                for k in range(2):
                    ins = dve.tensor_reduce(slf[:, :, k:k + 1], slo[k], AX.X, ALU.add)
                link(ins)
                slot_i = slf.rearrange("p j k -> p (j k)")
                link(dve.tensor_copy(slhi[:, 0], slot_i))
                dve.tensor_scalar(slhi[:, 1], slhi[:, 0], P - 1, None, ALU.bitwise_and)
                link(dve.tensor_scalar(slhi[:, 0], slhi[:, 0], 7, None, ALU.logical_shift_right))
                link(dve.tensor_copy(slh, slhi))
                dve.tensor_tensor(ohl, c_("iota").unsqueeze(1).to_broadcast([P, 2 * NT, P]),
                                  slh[:, 1].unsqueeze(2).to_broadcast([P, 2 * NT, P]), ALU.is_equal)
                link(dve.tensor_tensor(ohh, c_("iota")[:, 0:NPB].unsqueeze(1).to_broadcast([P, 2 * NT, NPB]),
                                       slh[:, 0].unsqueeze(2).to_broadcast([P, 2 * NT, NPB]), ALU.is_equal))
                parts = c_("parts", 2).rearrange("p h (a v) -> p h a v", v=2)
                for h in range(2):
                    for k in range(2):
                        ins = dve.tensor_tensor(sval[:, h, :, :, k], ohh, parts[:, h, :, k:k + 1].to_broadcast([P, 2 * NT, NPB]), ALU.mult)
                ins.then_inc(s_slot, 1)
                dve.wait_ge(s_tab, l + 1)
                dve.tensor_scalar(tab[:, :, :], ps[5][:, 192:192 + 2 * NPB].rearrange("p (q v) -> p q v", v=2), float(OOB), None,
                                  ALU.add).then_inc(s_tabc, 1)
                link(dve.tensor_tensor(ov1, c_("iota")[:, 0:NOV].unsqueeze(2).to_broadcast([P, NOV, NE]), inc.unsqueeze(1).to_broadcast([P, NOV, NE]), ALU.is_ge))
                link(dve.tensor_reduce(ov2[:, 0:NOV].unsqueeze(2), ov1, AX.X, ALU.add))
                link(dve.tensor_scalar(ov2[:, 0:NOV], ov2[:, 0:NOV], float(NE - 1), None, ALU.min))
                link(dve.tensor_copy(ov2[:, NOV:NOV + 1], inc[:, NE - 1:NE]))
                link(dve.tensor_scalar(ov2[:, NOV + 1:NOV + 2], inc[:, NE - 1:NE], 1.0, None, ALU.add))
                link(dve.tensor_copy(ovf[:, :], ov2))
                dve.tensor_scalar(ovf[:, NOV + 1:NOV + 2], ovf[:, NOV + 1:NOV + 2], 1, None, ALU.logical_shift_right).then_inc(s_ovf, 1)
                dve.wait_ge(s_ge, l + 1)
                link(dve.tensor_reduce(gdf[:, :, 0:1], gex, AX.X, ALU.add))
                link(dve.tensor_scalar(gdf[:, :, 1:2], gsm[:, :, 1:2], 1.0, None, ALU.add))
                link(dve.tensor_tensor(gdf[:, :, 0:1], gdf[:, :, 0:1], gdf[:, :, 1:2], ALU.mult))
                link(dve.reciprocal(gates[:, :, 0:1], gdf[:, :, 0:1]))
                dve.tensor_tensor(gates[:, :, 1:2], gates[:, :, 0:1], gsm[:, :, 1:2], ALU.mult).then_inc(s_gat, 1)
                dve.wait_ge(s_gat, l + 1)

            def experts(l):
                def pair(i, b, g, first=False):
                    dve.wait_ge(s_sg, i + 1 + PAIRS * l)
                    if not (first and b == 0):
                        dve.wait_ge(s_ht2, i + PAIRS * l)
                    dve.tensor_tensor(hh, sg, ps[2 + b][:, FE:2 * FE], ALU.mult).then_inc(s_hh, 1)
                    dve.wait_ge(s_ht2, i + 1 + PAIRS * l)
                    if not first:
                        dve.wait_ge(s_dd, i - 1 + PAIRS * l)
                    dve.tensor_copy(hhT[:, b], ps[4][:, 0:256].rearrange("p (c n) -> p c n", c=2)).then_inc(s_hte, 1)
                    dve.wait_ge(s_dd, i + 1 + PAIRS * l)
                    if not first:
                        dve.wait_ge(s_sc[l][b], 16 * g)
                    dve.tensor_copy(yb[:, b, 0:512], ps[6][:, :]).then_inc(s_yed, 1)
                pair(0, 0, 0, True)
                pair(1, 1, 0, True)
                with dve.Fori(1, PAIRS // 2) as r:
                    pair(2 * r, 0, r)
                    pair(2 * r + 1, 1, r)
                dve.wait_ge(s_ovf, l + 1)
                npairs = dve.value_load(ovf[0:1, NOV + 1:NOV + 2], min_val=0, max_val=NOV // 2)
                with dve.If(npairs > 0):
                    with dve.Fori(0, npairs) as m:
                        dve.wait_ge(o_sg[l], m + 1)
                        dve.tensor_tensor(hh, sg, ps[2][:, FE:2 * FE], ALU.mult).then_inc(o_h[l], 1)
                        dve.wait_ge(o_ht[l], m + 1)
                        dve.tensor_copy(hhT[:, 0], ps[4][:, 0:256].rearrange("p (c n) -> p c n", c=2)).then_inc(o_hte[l], 1)
                        dve.wait_ge(o_d[l], m + 2)
                        dve.wait_ge(o_fr[l], m + 1)
                        dve.tensor_copy(yb[:, 0, 0:512], ps[6][:, :]).then_inc(o_y[l], 1)
                with dve.Else():
                    pass

            def combine(l, j):
                r = ROWS[j]
                dve.wait_ge(s_cl[j], 16 * (l + 1))
                link(dve.scalar_tensor_tensor(x[0:r, j, :], cb[0:r, j, 0, :], gates[0:r, j, 0:1], x[0:r, j, :],
                                              ALU.mult, ALU.add))
                dve.scalar_tensor_tensor(x[0:r, j, :], cb[0:r, j, 1, :], gates[0:r, j, 1:2], x[0:r, j, :],
                                         ALU.mult, ALU.add).then_inc(s_res, 1)

            dense_out(0)
            route(0)
            experts(0)
            norm(2, lambda j: combine(0, j))
            dve.wait_ge(s_wst, 1)
            for k in range(2):
                ins = dve.tensor_tensor(wsm[:, 4 * k:4 * k + 4, :], ps[k][:, :].rearrange("p (g n) -> p g n", g=4),
                                        c_("tri").unsqueeze(1).to_broadcast([P, 4, P]), ALU.mult)
            ins.then_inc(s_wsm, 1)
            dve.wait_ge(s_gml, 48)
            for j in range(NT):
                r = ROWS[j]
                dve.wait_ge(s_gev, NT + j + 1)
                for k in range(2):
                    ins = dve.bn_stats(st[0:r, 24 + 6 * k:30 + 6 * k], v[0:r, j, k * 512:k * 512 + 512])
                link(ins)
                dve.bn_aggr(st[0:r, 36 + 2 * j:38 + 2 * j], st[0:r, 24:36]).then_inc(s_va, 1)
                dve.wait_ge(s_va, j + 1)
                dve.scalar_tensor_tensor(v[0:r, j, :], v[0:r, j, :], st[0:r, 36 + 2 * j:37 + 2 * j], lng[0:r, :], ALU.subtract, ALU.mult).then_inc(s_vc, 1)
                dve.wait_ge(s_vc, j + 1)
                dve.wait_ge(s_vr, j + 1)
                inverse_root(r, st[0:r, 37 + 2 * j:38 + 2 * j], st[0:r, 46 + j:47 + j], 1e-5, st[0:r, 51 + j:52 + j])
                dve.scalar_tensor_tensor(v[0:r, j, :], v[0:r, j, :], st[0:r, 51 + j:52 + j], lnb[0:r, :], ALU.mult, ALU.add).then_inc(s_ln, 1)

            def mix_out(j):
                r = ROWS[j]
                dve.wait_ge(s_mx, j + 1)
                if j == 0:
                    dve.wait_ge(s_small, 32)
                if j == 4:
                    dve.wait_ge(s_gvo, 16)
                for k in range(2):
                    ins = dve.tensor_tensor(v[0:r, j, k * 512:k * 512 + 512].rearrange("p (g n) -> p g n", g=4),
                                            ps[2 * (j % 2) + k][0:r, :].rearrange("p (g n) -> p g n", g=4),
                                            gbias[0:r, 4 * k:4 * k + 4].unsqueeze(2).to_broadcast([r, 4, P]), ALU.add)
                ins.then_inc(s_mxe, 1)
                dve.wait_ge(s_mxe, j + 1)

            def gate(n):
                hf, j = n // NT - 2, n % NT
                r = ROWS[j]
                dve.wait_ge(s_gev, n + 1)
                vs = v[0:r, j, hf * 512:hf * 512 + 512]
                dve.tensor_tensor(vs, vs, ut[0:r, n % 2, :], ALU.mult).then_inc(s_gu, 1)
            for j in range(NT):
                mix_out(j)
                gate(2 * NT + j)
            for j in range(NT):
                gate(3 * NT + j)
            dense_out(1)
            route(1)
            experts(1)
            norm(4, lambda j: combine(1, j))

        @block.tensor
        def _(pe):
            def turn(dst, src, k):
                return pe.transpose(dst, src, ident[0:k, 0:k])

            def norm_turn(n, j):
                r = ROWS[j]
                pe.wait_ge(s_h, NT * n + j + 1)
                if j >= 2:
                    pe.wait_ge(s_ht, NT * n + j - 1)
                for c in range(C):
                    ins = turn(ps[2 * (j % 2) + c // 4][:, (c % 4) * P:(c % 4) * P + r], row(n, j)[0:r, c:D:C], r)
                ins.then_inc(s_tp, 1)

            pe.wait_ge(s_con, 16)
            norm_turn(0, 0)
            norm_turn(0, 1)

            def split_product(acc, q, j):
                cols = slice(T0[j], T0[j] + ROWS[j])
                steps = [(c, left, right) for c in range(C)
                         for left, right in ((hTh, high[q - 7]), (hTh, dwl[:, q % 2]), (hTl, high[q - 7]))]
                for n, (c, left, right) in enumerate(steps):
                    ins = pe.matmul(acc, left[:, c, cols], right[:, c, :],
                                    start=(n == 0), stop=(n == len(steps) - 1))
                return ins

            def plain_product(bank, q, j, w):
                r = ROWS[j]
                for c in range(C):
                    lhs = hT[:, c, T0[j]:T0[j] + r]
                    if r == P:
                        ins = pe.matmul(bank[:, 0:w], lhs, dw[:, q % 2, c, 0:w], start=(c == 0), stop=(c == C - 1))
                        continue
                    for k in range(2):
                        ins = pe.matmul(bank[64 * k:64 * k + 64, 0:w // 2], lhs, dw[:, q % 2, c, k * w // 2:(k + 1) * w // 2],
                                        start=(c == 0), stop=(c == C - 1))
                return ins

            def dense_ready(q):
                if q >= 7:
                    pe.wait_ge(s_lo, 2 * (q - 6))
                pe.wait_ge(s_dw[q % 2], 16 * (q // 2 + 1))

            for task in tasks:
                if task[0] == "proj":
                    _, q, j = task
                    n, r = NT * q + j, ROWS[j]
                    if j == 0:
                        dense_ready(q)
                    pe.wait_ge(s_ht, j + 1)
                    if n >= 4:
                        pe.wait_ge(s_pev, n - 3)
                    plain_product(ps[4 + n % 4], q, j, QC).then_inc(s_pps, 1)
                    if q == 0 and j < 2:
                        for i in ((2,), (3, 4))[j]:
                            norm_turn(0, i)
                    if j == NT - 1:
                        pe.wait_ge(s_pps, n + 1)
                        pe.nop().then_inc(s_dwf, 1)
                elif task[0] == "pool":
                    m = task[1]
                    n, g = 20 + m, m // 2
                    if m == 0:
                        dense_ready(4)
                    pe.wait_ge(s_pev, n - 3)
                    for c in range(C):
                        ins = pe.matmul(ps[4 + n % 4][:, 0:HALF], dw[:, 0, c, g * P:(g + 1) * P],
                                        hT[:, c, (m % 2) * HALF:(m % 2 + 1) * HALF], start=(c == 0), stop=(c == C - 1))
                    ins.then_inc(s_pps, 1)
                    if m == 7:
                        pe.wait_ge(s_pps, n + 1)
                        pe.nop().then_inc(s_dwf, 1)
                elif task[0] == "turn":
                    i = task[1]
                    if i:
                        pe.wait_ge(s_te, i)
                    if i == 0:
                        pe.wait_ge(s_ht, NT)
                        pe.wait_ge(s_dup, 1)
                        turn(ps[0][:, 0:P], kdc[:, 0, :], P)
                        for g in range(NG):
                            turn(ps[0][:, P + 16 * g:P + 16 * g + HIST], sp15[:, g * P:(g + 1) * P], HIST)
                            ins = turn(ps[1][:, g * P:(g + 1) * P], kdc[:, 1 + g, :], P)
                    elif i < 6:
                        j = i - 1
                        r = ROWS[j]
                        pe.wait_ge(s_rope, j + 1)
                        for k in range(4):
                            turn(ps[0][:, k * P:k * P + r], R[0:r, j, OQI + k * P:OQI + (k + 1) * P], r)
                        ins = turn(ps[1][:, 0:r], kdi[0:r, j % 2, :], r)
                    else:
                        j = i - 6
                        r = ROWS[j]
                        pe.wait_ge(s_rope, NT + j + 1)
                        for k in range(4):
                            turn(ps[0][:, k * P:k * P + r], R[0:r, j, OQ + k * P:OQ + (k + 1) * P], r)
                            ins = turn(ps[1][:, k * P:k * P + r], kd[0:r, j % 2, k, :], r)
                    ins.then_inc(s_tt, 1)
                else:
                    u = task[1]
                    b, h = IDX_TILES[u // NIH], u % NIH
                    if u == 0:
                        pe.wait_ge(s_te, 6)
                    if u >= 2:
                        pe.wait_ge(s_ie, u - 1)
                    lo = 64 * (h % 2)
                    keys = kiTs if b == 4 else kiT
                    pe.matmul(ps[2 + u % 2][0:ROWS[b], 0:nkeys(b)], qiT[lo:lo + 64, h // 2, T0[b]:T0[b] + ROWS[b]],
                              keys[lo:lo + 64, 0:nkeys(b)], start=True, stop=True).then_inc(s_is, 1)

            def scores(u):
                b, h = u // NH, u % NH
                if u >= 2:
                    pe.wait_ge(s_sm, u - 1)
                else:
                    pe.wait_ge(s_ie, 4 * NIH)
                    pe.wait_ge(s_te, 11)
                lo, g = 64 * (h % 2), h // 2
                keys = kTs if b == 4 else kT
                pe.matmul(ps[2 + u % 2][0:ROWS[b], 0:nkeys(b)], qT[lo:lo + 64, g, T0[b]:T0[b] + ROWS[b]],
                          keys[lo:lo + 64, g, 0:nkeys(b)], start=True, stop=True).then_inc(s_s, 1)

            def chunks(b):
                if b == 4:
                    return [(P, vc[:, :]), (TS, R[0:TS, 4, OV:OV + 256])]
                return [(P, R[:, c, OV:OV + 256]) for c in range(b + 1)]

            def probs_turn(u):
                b = u // NH
                r = ROWS[b]
                pe.wait_ge(s_pr, u + 1)
                if u >= 2:
                    pe.wait_ge(s_pte, u - 1)
                for c, (k, _) in enumerate(chunks(b)):
                    ins = turn(ps[u % 2][0:k, c * P:c * P + r], pr[0:r, u % 2, c * P:c * P + k], r)
                ins.then_inc(s_ptp, 1)

            def values(k2):
                b, g = k2 // NKV, k2 % NKV
                r = ROWS[b]
                pe.wait_ge(s_pte, 2 * k2 + 2)
                if k2 >= 2:
                    pe.wait_ge(s_oe, k2 - 1)
                else:
                    pe.wait_ge(s_pev, NPROJ)
                ch = chunks(b)
                for c, (k, vals) in enumerate(ch):
                    for i in range(2):
                        ins = pe.matmul(ps[4 + k2 % 2][64 * i:64 * i + 64, 0:r], vals[:, g * HD:(g + 1) * HD],
                                        pT[0:k, i, c * P:c * P + r], start=(c == 0), stop=(c == len(ch) - 1))
                        if c == len(ch) - 1:
                            ins.then_inc(s_pv, 1)

            def pool_state():
                for g in range(NG):
                    turn(ps[6][0:HIST, g * P:(g + 1) * P], line[:, g, XP0 + TP - HIST:XP0 + TP], P)
                    ins = turn(ps[7][0:HIST, g * P:(g + 1) * P], line[:, g, LINE - HIST:LINE], P)
                ins.then_inc(s_pot, 1)
                pe.wait_ge(s_pwl, 16)

            def pool_map(m):
                pe.wait_ge(s_dt, m // 2 + 1)
                if m < 2:
                    pe.wait_ge(s_poe, 1)
                else:
                    pe.wait_ge(s_ype, m - 1)
                pe.matmul(ps[6 + m % 2][:, 0:HALF], pw[:, m // 2, :], dT[:, m // 2, (m % 2) * HALF:(m % 2 + 1) * HALF],
                          start=True, stop=True).then_inc(s_yp, 1)

            scores(0)
            scores(1)
            for u in range(NU):
                probs_turn(u)
                if u + 2 < NU:
                    scores(u + 2)
                if u % 2:
                    values(u // 2)
                if u == POOL_U:
                    pool_state()
                elif POOL_U < u <= POOL_U + 8:
                    pool_map(u - POOL_U - 1)

            def logits(l, i):
                r = ROWS[i]
                pe.wait_ge(s_ht, NT * (2 * l + 1) + i + 1)
                if i == 0:
                    pe.wait_ge(s_wr, 32 * (l + 1))
                    pe.wait_ge(s_lz, l + 1)
                for c in range(C):
                    ins = pe.matmul(ps[4][0:r, 36 * i:36 * i + 36], hT[:, c, T0[i]:T0[i] + r], wr[:, c, :],
                                    start=(c == 0), stop=(c == C - 1))
                if i == NT - 1:
                    ins.then_inc(s_lg, 1)

            def dense_out(k, ready):
                for n in range(2 * NT):
                    hf, j = n // NT, n % NT
                    q, r = 5 + 6 * k + hf, ROWS[j]
                    if j == 0:
                        dense_ready(q)
                    ready(n, j)
                    if n >= 3:
                        pe.wait_ge(s_res, 15 * k + n - 2)
                    acc = out_bank(n)
                    ins = split_product(acc[0:r, :], q, j) if k else plain_product(acc, q, j, 512)
                    ins.then_inc(s_ops, 1)
                    if j == NT - 1:
                        pe.wait_ge(s_ops, 10 * k + n + 1)
                        pe.nop().then_inc(s_dwf, 1)
                    if n > NT + 1:
                        logits(k, j - 2)
                    if n > NT:
                        norm_turn(2 * k + 1, j - 1)
                logits(k, NT - 2)
                norm_turn(2 * k + 1, NT - 1)
                logits(k, NT - 1)

            def route(l):
                pe.wait_ge(s_m, l + 1)
                pe.wait_ge(s_bf, 1)
                for j in range(NT):
                    for i in range(j + 1):
                        k, r = ROWS[i], ROWS[j]
                        w = cbf[0:k, 0, 0:r] if i == j else cbf[0:k, 1, 0:r]
                        pe.matmul(ps[5][0:r, NE * j:NE * j + NE], w, mbf[0:k, i, :], start=(i == 0), stop=(i == j))
                for i in range(NT):
                    ins = pe.matmul(ps[5][:, 160:192], cbf[0:ROWS[i], 1, :], mbf[0:ROWS[i], i, :],
                                    start=(i == 0), stop=(i == NT - 1))
                ins.then_inc(s_cnt, 1)
                pe.wait_ge(s_slot, l + 1)
                for i in range(2 * NT):
                    for h in range(2):
                        r = ROWS[i // 2]
                        ins = pe.matmul(ps[5][:, 192:192 + 2 * NPB], ohl[0:r, i, :], sval[0:r, h, i].rearrange("p q v -> p (q v)"),
                                        start=(i == 0 and h == 0), stop=(i == 2 * NT - 1 and h == 1))
                ins.then_inc(s_tab, 1)

            def experts(l):
                def turn_rows(b):
                    for c in range(C):
                        ins = turn(ps[c // 4][:, (c % 4) * P:(c % 4 + 1) * P], xg[:, b, c:D:C], P)
                    return ins

                def up(b, w):
                    for c in range(C):
                        for k in range(2):
                            ins = pe.matmul(ps[2 + b][64 * k:64 * k + 64, :], xT[:, b, c, 64 * k:64 * k + 64],
                                            w[:, k, c, :], start=(c == 0), stop=(c == C - 1))
                    return ins

                def turn_hidden():
                    for c in range(2):
                        ins = turn(ps[4][:, c * P:(c + 1) * P], hh[:, c:FE:2], P)
                    return ins

                def down(b, w):
                    for c in range(2):
                        for hf in range(2):
                            for k in range(2):
                                ins = pe.matmul(ps[6 + hf][64 * k:64 * k + 64, :], hhT[:, b, c, 64 * k:64 * k + 64],
                                                w[:, k, c, hf * 512:hf * 512 + 512], start=(c == 0), stop=(c == 1))
                    return ins

                def turned(i, b, g, first=False):
                    pe.wait_ge(s_xg[l][b], 16 * g)
                    if not first:
                        pe.wait_ge(s_xte, i + PAIRS * l)
                    turn_rows(b).then_inc(s_xt, 1)

                def pair(i, b, g, w, gw, first=False, last=False):
                    pe.wait_ge(s_wgu[l][w], 64 * gw)
                    pe.wait_ge(s_xte, i + 1 + PAIRS * l)
                    if not first:
                        pe.wait_ge(s_hh, i - 1 + PAIRS * l)
                    up(b, wgu[w]).then_inc(s_gud, 1)
                    if not (last and b == 1):
                        turned(i + 1, 1 - b, g + b)
                    pe.wait_ge(s_hh, i + 1 + PAIRS * l)
                    if not (first and b == 0):
                        pe.wait_ge(s_hte, i + PAIRS * l)
                    turn_hidden().then_inc(s_ht2, 1)
                    pe.wait_ge(s_wd[l][w], 32 * gw)
                    pe.wait_ge(s_hte, i + 1 + PAIRS * l)
                    if not (first and b == 0):
                        pe.wait_ge(s_yea, i + PAIRS * l)
                        pe.wait_ge(s_yed, i + PAIRS * l)
                    down(b, wdn[w]).then_inc(s_dd, 1)

                turned(0, 0, 1, True)
                pair(0, 0, 1, 0, 1, first=True)
                pair(1, 1, 1, 1, 1, first=True)
                pair(2, 0, 2, 2, 1)
                pair(3, 1, 2, 0, 2)
                with pe.Fori(2, PAIRS // 2 - 1) as r:
                    pair(2 * r, 0, r + 1, 1, r)
                    pair(2 * r + 1, 1, r + 1, 0, r + 1)
                pair(PAIRS - 2, 0, PAIRS // 2, 1, PAIRS // 2 - 1)
                pe.wait_ge(s_dd, PAIRS - 1 + PAIRS * l)
                pe.nop().then_inc(o_d[l], 1)
                pair(PAIRS - 1, 1, PAIRS // 2, 0, PAIRS // 2, last=True)
                pe.wait_ge(s_ovf, l + 1)
                npairs = pe.value_load(ovf[0:1, NOV + 1:NOV + 2], min_val=0, max_val=NOV // 2)
                with pe.If(npairs > 0):
                    with pe.Fori(0, npairs) as m:
                        pe.wait_ge(o_xg[l], 16 * m + 16)
                        turn_rows(0).then_inc(o_t[l], 1)
                        pe.wait_ge(o_te[l], m + 1)
                        pe.wait_ge(o_wgu[l], 64 * m + 64)
                        up(0, wgu[1]).then_inc(o_gu[l], 1)
                        pe.wait_ge(o_h[l], m + 1)
                        turn_hidden().then_inc(o_ht[l], 1)
                        pe.wait_ge(o_hte[l], m + 1)
                        pe.wait_ge(o_wd[l], 32 * m + 32)
                        down(0, wdn[1]).then_inc(o_d[l], 1)
                with pe.Else():
                    pass

            def mixer_ready(n, j):
                if n < NT:
                    pe.wait_ge(s_oe, NKV * (j + 1) if n < 2 else NU // 2)
                if n == 0:
                    pe.wait_ge(s_ype, 8)
            dense_out(0, mixer_ready)
            route(0)
            experts(0)
            norm_turn(2, 0)
            norm_turn(2, 1)

            def ws_turn():
                pe.wait_ge(s_gml, 48)
                pe.wait_ge(s_ht, 3 * NT)
                for g in range(8):
                    ins = turn(ps[g // 4][:, (g % 4) * P:(g % 4 + 1) * P], wsr[:, g, :], P)
                ins.then_inc(s_wst, 1)

            def gm_in(n):
                q, j = 7 + n // NT, n % NT
                r = ROWS[j]
                if j == 0:
                    dense_ready(q)
                if n >= 4:
                    pe.wait_ge(s_gev, n - 3)
                if n < NT:
                    pe.wait_ge(s_hl, j + 1)
                split_product(ps[4 + n % 4][0:r, :], q, j).then_inc(s_gps, 1)
                if j == NT - 1:
                    pe.wait_ge(s_gps, n + 1)
                    pe.nop().then_inc(s_dwf, 1)

            def mix(j):
                r = ROWS[j]
                pe.wait_ge(s_ln, j + 1)
                if j >= 2:
                    pe.wait_ge(s_mxe, j - 1)
                else:
                    pe.wait_ge(s_wsm, 1)
                for g in range(8):
                    ins = pe.matmul(ps[2 * (j % 2) + g // 4][0:r, (g % 4) * P:(g % 4 + 1) * P], wsm[0:r, g, 0:r],
                                    v[0:r, j, g * P:(g + 1) * P], start=True, stop=True)
                ins.then_inc(s_mx, 1)

            def gated_turn(j):
                r = ROWS[j]
                pe.wait_ge(s_gu, NT + j + 1)
                pe.wait_ge(s_mxe, NT)
                if j >= 2:
                    pe.wait_ge(s_gte, j - 1)
                for c in range(C):
                    ins = turn(ps[2 * (j % 2) + c // 4][:, (c % 4) * P:(c % 4) * P + r], v[0:r, j, c:D:C], r)
                ins.then_inc(s_gt, 1)
            for n in range(2 * NT):
                gm_in(n)
                if n + 2 < NT:
                    norm_turn(2, n + 2)
                elif n == NT - 1:
                    ws_turn()
            for j in range(NT):
                gm_in(2 * NT + j)
                mix(j)
            gm_in(3 * NT)
            for j in range(NT):
                if j + 1 < NT:
                    gm_in(3 * NT + j + 1)
                gated_turn(j)
            dense_out(1, lambda n, j: pe.wait_ge(s_hl, NT + j + 1) if n < NT else None)
            route(1)
            experts(1)


_INS = ["x_prompt", "x_sample", "cache_k", "cache_v", "cache_idx_k", "state_pool", "norm_mix", "norm_ffn", "norm_final",
        "par_w_in", "par_pool_w", "par_pool_scale", "par_w_out", "gm_w_in", "gm_ln_g", "gm_ln_b", "gm_ws", "gm_bs",
        "gm_w_out", "moe_router_group", "moe_router_expert", "moe_w_gate", "moe_w_up", "moe_w_down"]
_OUTS = [(1, TP, D), (1, TS, D), (1, 1, TP, NKV, HD), (1, 1, TP, NKV, HD), (1, 1, TP, HD), (1, 1, HIST, PW_),
         (1, 1, TS, NKV, HD), (1, 1, TS, NKV, HD), (1, 1, TS, HD), (1, 1, HIST, PW_), (1, 1, TS, D)]


def kernel(**inputs):
    import concourse.bacc as _bacc
    from concourse.bass_utils import run_bass_kernel_spmd as _run

    nc = _bacc.Bacc("TRN2", target_bir_lowering=False, num_devices=1)
    con = constants()
    arrays, args = {}, {}
    for name in _INS + ["con"]:
        arr = np.ascontiguousarray(con if name == "con" else inputs[name])
        arrays[f"in_{name}"] = arr
        args[name] = nc.dram_tensor(f"in_{name}", arr.shape, mybir.dt.from_np(arr.dtype), kind="ExternalInput").ap()
    outs = [nc.dram_tensor(f"out_{i}", shape, F32, kind="ExternalOutput").ap() for i, shape in enumerate(_OUTS)]
    build(nc, args, outs)
    r = _run(nc, [arrays], core_ids=[0])
    return tuple(r.results[0][f"out_{i}"] for i in range(len(_OUTS)))
```
